# Optimizing a Trainium2 kernel written in Bass

```python
import math
import jax, jax.numpy as jnp
from jax import lax
import numpy as np

D_MODEL = 1024
BATCH = 1
SEQ = 1024
DEPTH = 1
DEC_BATCH = 8
DEC_SEQ = 1
PAST_LEN = 2048
PAGE_SIZE = 128

A_HEADS = 8
A_KV_HEADS = 2
A_HEAD_DIM = 64
A_GROUP = A_HEADS // A_KV_HEADS
WINDOW = 128
N_BUCKETS = 32
MAX_DISTANCE = 128
A_Q_COLS = A_HEADS * A_HEAD_DIM
A_KV_COLS = A_KV_HEADS * A_HEAD_DIM
POOL_WINDOWS = (2, 4, 8, 16)
POOL_GROUPS = 4
POOL_GROUP_W = 128
POOL_W = POOL_GROUPS * POOL_GROUP_W
POOL_BUF = 15
C_HEADS = 4
C_HEAD_DIM = 128
C_W = C_HEADS * C_HEAD_DIM
C_CHUNK = 128
N_BRANCH = 3
IN_COLS = A_Q_COLS + 2 * A_KV_COLS + POOL_W + 4 * C_W + 2 * C_HEADS + N_BRANCH * D_MODEL
PEER_HEADS = 8
PEER_DK = 256
N_KEYS = 128
N_EXPERTS = N_KEYS * N_KEYS
PEER_TOPK = 16
PEER_BLOCK = 256
EPS = 1e-6

kernel_name = "hybrid_swa_pool_mlstm_peer_step"

def _split_points():
    sizes = (A_Q_COLS, A_KV_COLS, A_KV_COLS, POOL_W, C_W, C_W, C_W, C_HEADS, C_HEADS, C_W,
             D_MODEL, D_MODEL, D_MODEL)
    pts, acc = [], 0
    for s in sizes[:-1]:
        acc += s
        pts.append(acc)
    return pts

def _rmsnorm(x, g):
    xf = x.astype(jnp.float32)
    y = xf * lax.rsqrt(jnp.mean(xf * xf, axis=-1, keepdims=True) + EPS)
    return (y * g.astype(jnp.float32)).astype(x.dtype)

def _rel_bucket(dist):
    max_exact = N_BUCKETS // 2
    d = jnp.maximum(dist, 0)
    df = jnp.maximum(d, 1).astype(jnp.float32)
    large = max_exact + (jnp.log(df / max_exact) / math.log(MAX_DISTANCE / max_exact)
                         * (N_BUCKETS - max_exact)).astype(jnp.int32)
    large = jnp.minimum(large, N_BUCKETS - 1)
    return jnp.where(d < max_exact, d, large)

def _sink_attention(q, k, v, dist, valid, sink, rel_bias):
    Tq, Tk = dist.shape
    logits = jnp.einsum('...qkgd,...skd->...kgqs', q, k).astype(jnp.float32) * (A_HEAD_DIM ** -0.5)
    bias = jnp.moveaxis(rel_bias[_rel_bucket(dist)].astype(jnp.float32), -1, 0)
    bias = bias.reshape(A_KV_HEADS, A_GROUP, Tq, Tk)
    logits = jnp.where(valid, logits + bias, -jnp.inf)
    sink_l = sink.astype(jnp.float32).reshape(A_KV_HEADS, A_GROUP, 1, 1)
    mx = jnp.maximum(jnp.max(logits, axis=-1, keepdims=True), sink_l)
    p = jnp.exp(logits - mx)
    p = p / (jnp.sum(p, axis=-1, keepdims=True) + jnp.exp(sink_l - mx))
    return jnp.einsum('...kgqs,...skd->...qkgd', p.astype(v.dtype), v)

def _swa_prompt(q, k, v, sink, rel_bias):
    N, T = q.shape[:2]
    nb = T // WINDOW
    qb = q.reshape(N, nb, WINDOW, A_KV_HEADS, A_GROUP, A_HEAD_DIM)
    pad = ((0, 0), (WINDOW, 0), (0, 0), (0, 0))
    kp = jnp.pad(k, pad).reshape(N, nb + 1, WINDOW, A_KV_HEADS, A_HEAD_DIM)
    vp = jnp.pad(v, pad).reshape(N, nb + 1, WINDOW, A_KV_HEADS, A_HEAD_DIM)
    kb = jnp.concatenate([kp[:, :-1], kp[:, 1:]], axis=2)
    vb = jnp.concatenate([vp[:, :-1], vp[:, 1:]], axis=2)
    dist = jnp.arange(WINDOW)[:, None] + WINDOW - jnp.arange(2 * WINDOW)[None, :]
    kpos = jnp.arange(nb)[:, None] * WINDOW - WINDOW + jnp.arange(2 * WINDOW)[None, :]
    valid = (dist >= 0)[None] & (dist < WINDOW)[None] & (kpos >= 0)[:, None, :]
    out = _sink_attention(qb, kb, vb, dist, valid[:, None, None], sink, rel_bias)
    return out.reshape(N, T, A_Q_COLS), k[:, -WINDOW:], v[:, -WINDOW:]

def _swa_sample(q, k, v, k_buf, v_buf, sink, rel_bias):
    N, T = q.shape[:2]
    kk = jnp.concatenate([k_buf.astype(k.dtype), k], axis=1)
    vv = jnp.concatenate([v_buf.astype(v.dtype), v], axis=1)
    dist = (WINDOW + jnp.arange(T))[:, None] - jnp.arange(WINDOW + T)[None, :]
    valid = (dist >= 0) & (dist < WINDOW)
    out = _sink_attention(q, kk, vv, dist, valid, sink, rel_bias)
    return out.reshape(N, T, A_Q_COLS), kk[:, T:], vv[:, T:]

def _pool_mixer(xp, buf, pos0, w_pool, pool_scale):
    T = xp.shape[1]
    full = jnp.concatenate([buf.astype(xp.dtype), xp], axis=1)
    cs = jnp.cumsum(full.astype(jnp.float32), axis=1)
    cs = jnp.concatenate([jnp.zeros_like(cs[:, :1]), cs], axis=1)
    end = cs[:, POOL_BUF + 1:]
    pos = pos0 + jnp.arange(T)
    outs = []
    for g, w in enumerate(POOL_WINDOWS):
        sl = slice(g * POOL_GROUP_W, (g + 1) * POOL_GROUP_W)
        start = cs[:, POOL_BUF + 1 - w: POOL_BUF + 1 - w + T, sl]
        cnt = jnp.minimum(pos + 1, w).astype(jnp.float32)[None, :, None]
        outs.append((end[..., sl] - start) / cnt - full[:, POOL_BUF:, sl].astype(jnp.float32))
    pooled = jnp.stack(outs, axis=2)
    y = jnp.einsum('ntgc,gcd->ntgd', pooled.astype(xp.dtype), w_pool).reshape(xp.shape)
    return y * pool_scale, full[:, T:]

def _mlstm_chunk(carry, inp):
    C, n, m = carry
    q, k, v, ig, lf = inp
    L = q.shape[2]
    b = jnp.cumsum(lf, axis=-1)
    causal = jnp.tril(jnp.ones((L, L), dtype=bool))
    D = jnp.where(causal, b[..., :, None] - b[..., None, :] + ig[..., None, :], -jnp.inf)
    inter = b + m[..., None]
    m_t = jnp.maximum(inter, jnp.max(D, axis=-1))
    S = jnp.einsum('nhld,nhsd->nhls', q, k) * jnp.exp(D - m_t[..., None])
    w_inter = jnp.exp(inter - m_t)
    num = jnp.einsum('nhls,nhsd->nhld', S, v) + w_inter[..., None] * jnp.einsum('nhed,nhld->nhle', C, q)
    den = jnp.sum(S, axis=-1) + w_inter * jnp.einsum('nhd,nhld->nhl', n, q)
    h = num / jnp.maximum(jnp.abs(den), jnp.exp(-m_t))[..., None]
    m_new = m_t[..., -1]
    w_end = jnp.exp(b[..., -1:] - b + ig - m_new[..., None])
    decay = jnp.exp(b[..., -1] + m - m_new)
    C_new = decay[..., None, None] * C + jnp.einsum('nhl,nhle,nhld->nhed', w_end, v, k)
    n_new = decay[..., None] * n + jnp.einsum('nhl,nhld->nhd', w_end, k)
    return (C_new, n_new, m_new), h

def _mlstm(q, k, v, ig, lf, C0, n0, m0):
    N, T, H, d = q.shape
    L = C_CHUNK if T % C_CHUNK == 0 else T
    nc = T // L

    def chunks(a):
        a = a.astype(jnp.float32).reshape((N, nc, L, H) + a.shape[3:])
        return jnp.moveaxis(a, (1, 3), (0, 2))

    carry0 = (C0.astype(jnp.float32), n0.astype(jnp.float32), m0.astype(jnp.float32))
    (C, n, m), h = lax.scan(_mlstm_chunk, carry0, (chunks(q), chunks(k), chunks(v), chunks(ig), chunks(lf)))
    h = jnp.moveaxis(h, (0, 2), (1, 3)).reshape(N, T, H, d)
    return h, C, n, m

def _peer(x, wq, k1, k2, u, v):
    N, T, D = x.shape
    n_tok = N * T
    blk = min(PEER_BLOCK, n_tok)
    n_blk = -(-n_tok // blk)
    xt = jnp.pad(x.reshape(n_tok, D), ((0, n_blk * blk - n_tok), (0, 0)))

    def block(xb):
        q = (xb @ wq).reshape(blk, PEER_HEADS, 2, PEER_DK // 2)
        s1 = jnp.einsum('thd,kd->thk', q[:, :, 0], k1).astype(jnp.float32)
        s2 = jnp.einsum('thd,kd->thk', q[:, :, 1], k2).astype(jnp.float32)
        v1, i1 = lax.top_k(s1, PEER_TOPK)
        v2, i2 = lax.top_k(s2, PEER_TOPK)
        cand = (v1[..., :, None] + v2[..., None, :]).reshape(blk, PEER_HEADS, PEER_TOPK * PEER_TOPK)
        cidx = (i1[..., :, None] * N_KEYS + i2[..., None, :]).reshape(blk, PEER_HEADS, PEER_TOPK * PEER_TOPK)
        top_v, top_pos = lax.top_k(cand, PEER_TOPK)
        experts = jnp.take_along_axis(cidx, top_pos, axis=-1)
        gates = jax.nn.softmax(top_v, axis=-1)
        act = jax.nn.gelu(jnp.einsum('td,thkd->thk', xb, u[experts]).astype(jnp.float32), approximate=False)
        return jnp.einsum('thk,thkd->td', (gates * act).astype(xb.dtype), v[experts])

    y = lax.map(block, xt.reshape(n_blk, blk, D))
    return y.reshape(n_blk * blk, D)[:n_tok].reshape(N, T, D)

def _layer(x, is_prompt, st, p, rel_bias):
    N, T, _ = x.shape
    xn = _rmsnorm(x, p['norm1_g'])
    z = xn @ p['w_in']
    aq, ak, av, pin, cq, ck, cv, ci, cf, co, ga, gb, gc = jnp.split(z, _split_points(), axis=-1)
    q = _rmsnorm(aq.reshape(N, T, A_KV_HEADS, A_GROUP, A_HEAD_DIM), p['q_norm_g'])
    k = _rmsnorm(ak.reshape(N, T, A_KV_HEADS, A_HEAD_DIM), p['k_norm_g'])
    v = av.reshape(N, T, A_KV_HEADS, A_HEAD_DIM)
    if is_prompt:
        ya, k_buf, v_buf = _swa_prompt(q, k, v, p['sink'], rel_bias)
        pos0 = 0
    else:
        ya, k_buf, v_buf = _swa_sample(q, k, v, st['k'], st['v'], p['sink'], rel_bias)
        pos0 = PAST_LEN
    yb, pool_buf = _pool_mixer(pin, st['pool'], pos0, p['w_pool'], p['pool_scale'])
    qc = cq.reshape(N, T, C_HEADS, C_HEAD_DIM)
    kc = ck.reshape(N, T, C_HEADS, C_HEAD_DIM) * (C_HEAD_DIM ** -0.5)
    vc = cv.reshape(N, T, C_HEADS, C_HEAD_DIM)
    ig = ci.astype(jnp.float32) + p['b_igate'].astype(jnp.float32)
    lf = jax.nn.log_sigmoid(cf.astype(jnp.float32) + p['b_fgate'].astype(jnp.float32))
    h, C, n, m = _mlstm(qc, kc, vc, ig, lf, st['c'], st['n'], st['m'])
    h = _rmsnorm(h.astype(x.dtype), p['h_norm_g'])
    yc = (h * jax.nn.sigmoid(co).reshape(N, T, C_HEADS, C_HEAD_DIM)).reshape(N, T, C_W)
    merged = (jax.nn.sigmoid(ga) * (ya @ p['w_br_a']) + jax.nn.sigmoid(gb) * (yb @ p['w_br_b'])
              + jax.nn.sigmoid(gc) * (yc @ p['w_br_c']))
    x = x + merged @ p['w_out']
    x = x + _peer(_rmsnorm(x, p['norm2_g']), p['peer_wq'], p['peer_k1'], p['peer_k2'], p['peer_u'], p['peer_v'])
    return x, (k_buf, v_buf, pool_buf, C, n, m)

def setup_inputs(seed: int = 0) -> dict:
    key = jax.random.key(seed)
    ks = jax.random.split(key, 32)
    f32 = jnp.float32
    nrm = lambda i, shape, s: jax.random.normal(ks[i], shape, f32) * s
    gain = lambda i, shape: 1.0 + 0.01 * jax.random.normal(ks[i], shape, f32)
    return {
        "x_prompt": nrm(0, (BATCH, SEQ, D_MODEL), 1.0),
        "x_sample": nrm(1, (DEC_BATCH, DEC_SEQ, D_MODEL), 1.0),
        "cache_k": nrm(2, (DEPTH, DEC_BATCH, WINDOW, A_KV_HEADS, A_HEAD_DIM), 1.0),
        "cache_v": nrm(3, (DEPTH, DEC_BATCH, WINDOW, A_KV_HEADS, A_HEAD_DIM), 1.0),
        "state_pool": nrm(4, (DEPTH, DEC_BATCH, POOL_BUF, POOL_W), 1.0),
        "state_mlstm_c": nrm(5, (DEPTH, DEC_BATCH, C_HEADS, C_HEAD_DIM, C_HEAD_DIM), 0.1),
        "state_mlstm_n": nrm(6, (DEPTH, DEC_BATCH, C_HEADS, C_HEAD_DIM), 0.5),
        "state_mlstm_m": nrm(7, (DEPTH, DEC_BATCH, C_HEADS), 1.0),
        "rel_bias": nrm(8, (N_BUCKETS, A_HEADS), 0.5),
        "norm1_g": gain(9, (DEPTH, D_MODEL)),
        "w_in": nrm(10, (DEPTH, D_MODEL, IN_COLS), D_MODEL ** -0.5),
        "q_norm_g": gain(11, (DEPTH, A_HEAD_DIM)),
        "k_norm_g": gain(12, (DEPTH, A_HEAD_DIM)),
        "attn_sink": nrm(13, (DEPTH, A_HEADS), 0.5),
        "w_pool": nrm(14, (DEPTH, POOL_GROUPS, POOL_GROUP_W, POOL_GROUP_W), POOL_GROUP_W ** -0.5),
        "pool_scale": 0.5 + nrm(15, (DEPTH, POOL_W), 0.1),
        "b_igate": nrm(16, (DEPTH, C_HEADS), 0.1),
        "b_fgate": 3.0 + nrm(17, (DEPTH, C_HEADS), 0.5),
        "h_norm_g": gain(18, (DEPTH, C_HEAD_DIM)),
        "w_br_a": nrm(19, (DEPTH, A_Q_COLS, D_MODEL), A_Q_COLS ** -0.5),
        "w_br_b": nrm(20, (DEPTH, POOL_W, D_MODEL), POOL_W ** -0.5),
        "w_br_c": nrm(21, (DEPTH, C_W, D_MODEL), C_W ** -0.5),
        "w_out": nrm(22, (DEPTH, D_MODEL, D_MODEL), D_MODEL ** -0.5),
        "norm2_g": gain(23, (DEPTH, D_MODEL)),
        "peer_wq": nrm(24, (DEPTH, D_MODEL, PEER_HEADS * PEER_DK), D_MODEL ** -0.5),
        "peer_k1": nrm(25, (DEPTH, N_KEYS, PEER_DK // 2), (PEER_DK // 2) ** -0.5),
        "peer_k2": nrm(26, (DEPTH, N_KEYS, PEER_DK // 2), (PEER_DK // 2) ** -0.5),
        "peer_u": nrm(27, (DEPTH, N_EXPERTS, D_MODEL), D_MODEL ** -0.5),
        "peer_v": nrm(28, (DEPTH, N_EXPERTS, D_MODEL), PEER_TOPK ** -0.5),
    }

def reference(x_prompt, x_sample, cache_k, cache_v, state_pool, state_mlstm_c, state_mlstm_n, state_mlstm_m,
              rel_bias, norm1_g, w_in, q_norm_g, k_norm_g, attn_sink, w_pool, pool_scale, b_igate, b_fgate,
              h_norm_g, w_br_a, w_br_b, w_br_c, w_out, norm2_g, peer_wq, peer_k1, peer_k2, peer_u, peer_v):
    B = x_prompt.shape[0]
    xp, xs = x_prompt, x_sample
    new_p = [[] for _ in range(6)]
    new_s = [[] for _ in range(6)]
    for l in range(DEPTH):
        p = dict(norm1_g=norm1_g[l], w_in=w_in[l], q_norm_g=q_norm_g[l], k_norm_g=k_norm_g[l], sink=attn_sink[l],
                 w_pool=w_pool[l], pool_scale=pool_scale[l], b_igate=b_igate[l], b_fgate=b_fgate[l],
                 h_norm_g=h_norm_g[l], w_br_a=w_br_a[l], w_br_b=w_br_b[l], w_br_c=w_br_c[l], w_out=w_out[l],
                 norm2_g=norm2_g[l], peer_wq=peer_wq[l], peer_k1=peer_k1[l], peer_k2=peer_k2[l],
                 peer_u=peer_u[l], peer_v=peer_v[l])
        st_p = dict(pool=jnp.zeros((B, POOL_BUF, POOL_W), xp.dtype),
                    c=jnp.zeros((B, C_HEADS, C_HEAD_DIM, C_HEAD_DIM), jnp.float32),
                    n=jnp.zeros((B, C_HEADS, C_HEAD_DIM), jnp.float32),
                    m=jnp.zeros((B, C_HEADS), jnp.float32))
        st_s = dict(k=cache_k[l], v=cache_v[l], pool=state_pool[l], c=state_mlstm_c[l], n=state_mlstm_n[l],
                    m=state_mlstm_m[l])
        xp, sp = _layer(xp, True, st_p, p, rel_bias)
        xs, ss = _layer(xs, False, st_s, p, rel_bias)
        for i in range(6):
            new_p[i].append(sp[i])
            new_s[i].append(ss[i])
    kp, vp, poolp, cp, np_, mp = [jnp.stack(a) for a in new_p]
    ks, vs, pools, cs, ns, ms = [jnp.stack(a) for a in new_s]
    return (xp, xs, kp, vp, poolp, cp, np_, mp, ks, vs, pools, cs, ns, ms)


_drawn_inputs = setup_inputs


def setup_inputs(seed=0):
    import zlib

    import numpy as np

    out = dict(_drawn_inputs(seed))
    spreads = {}
    factors = {'norm1_g': 3.545,
     'q_norm_g': 8.0,
     'k_norm_g': 6.341,
     'attn_sink': 64.0,
     'h_norm_g': 38.153,
     'norm2_g': 27.113}
    for name, (base, spread) in spreads.items():
        noise = np.random.default_rng([zlib.crc32(name.encode()), seed]).standard_normal(out[name].shape)
        drawn = base * np.exp(spread * noise) if base else spread * noise
        out[name] = __import__('jax').numpy.asarray(drawn.astype(out[name].dtype))
    for name, factor in factors.items():
        out[name] = (out[name] * factor).astype(out[name].dtype)
    return out
```

```python
import math
from contextlib import ExitStack

import numpy as np

import concourse.bass as bass
from concourse import mybir

F32, U32 = mybir.dt.float32, mybir.dt.uint32
ALU, ACT, AX = mybir.AluOpType, mybir.ActivationFunctionType, mybir.AxisListType

P = 128
D = 1024
KC = D // P
SEQ, NS = 1024, 8
PASSES = 2
TOK = SEQ // PASSES
NT = TOK // P
AH, AKV, AD = 8, 2, 64
AG = AH // AKV
W = 128
POOLW = (2, 4, 8, 16)
HIST = 15
CH, CD = 4, 128
CD1 = CD + 1
PH, PK = 8, 16
NKEY = 128
EPS = 1e-6
NEG = -1e30
LOWEST = -3e38

QK0, V0, G0, PIN0, CQ0, CK0, CO0, CV0 = 0, 640, 768, 776, 1288, 1800, 2312, 2824
ZC = 420
NZ = 8
ZW = ZC * NZ
OC = 256
NO = D // OC
UNITS = NZ + 3 * KC + NO + 2 * PH
RING = 8

C_ID, C_TRI, C_MASK, C_LAST, C_IOTA, C_CNT, C_BUCK, C_SBUCK = 0, 128, 256, 384, 512, 528, 592, 976
C_KEEP = 592
C_ALL = 1104
R_QK, R_HN, R_GB, R_SINK = 0, 640, 768, 776
R_ALL = 784

STEPS = """qks_ready pcs_ready kcs_ready qT_ready pinT_ready kcT_ready E_ready exps_ready P_exp esink_ready PTa_ready
yaT_done kT_ready qcT_ready diag_ready am0_ready M_ready am_ready bml_ready args_ready L_ready Sm_ready
interw_ready ST_ready wk_ready nd_ready CT_ready PTd_ready arden_ready ya_ready poolT_done kT_shift v_shift
pooled_ready hist_done qk_tr pin_tr cq_tr ck_tr cs_mm arow_mm S_mm scores_mm bcast_mm inter_mm ST_tr intra_mm
state_mm PT_tr PV_mm pooly_mm yaT_tr""".split()
OTHERS = """setup scratch_w bias_in g_in x_in ssq ms_ready inv_ready rstd_ready xs_ready xs_tr xT_ready z_mm ones_set
inv40 r40 qkn absf expf lnf lf_ready co_sig hinv hr16 hy3 hyT_tr ycT_done gate_mm br_mm sig_done prod o_mm
kq_mm esub eexp cur_ready idx_slot gelud diagd y_out init_v init_p buck_mm buck_sb state_out_tr state_out_sb
outs w_in0 w_in1 topk_pass state_stored state_c_stored b_n c_load c_load2 c_scr k_load kscr smp_a smp_p smp_v
stats_v topk_v pool_p""".split()
class Steps:

    def __init__(self, *order):
        self.order, self.n = order, len(order)

    def step(self, name):
        return 1 if name in self.order else 0

    def at(self, name, rounds=0):
        return self.n * rounds + self.order.index(name) + 1


stats = Steps("sq_ready", "ss_ready", "ms40", "gates_in", "minf", "qk_scaled", "hsq", "hss", "hms", "hy1", "hy2")
tile = Steps("b_ready", "a_ready", "rmax_ready", "m_new", "L0_ready", "L1_ready", "mx_ready", "mx2_ready",
    "den_abs", "den_ready", "h_done", "h_ready", "aden_ready")
find_steps = Steps("top1", "rep1", "top2", "idx2", "cand", "idxf", "ctop1", "crep", "cidx1", "ctop2", "cidx2",
    "pos_ab", "pos_f", "eq_a", "eq_ab", "e_a", "e_ab", "esum", "erec")
pooling = Steps("sum2", "sum4", "sum8", "sum16", "scaled")
SMP = {"p": Steps("c_tr", "b_xtr", "b_tr", "a_bmm", "a_qtr", "a_ktr", "b_mm", "c_bc", "a_smm", "a_str", "c_hmm",
    "a_ptr", "a_pv", "sample_s", "xb_mm"),
       "a": Steps("m_sig", "c_T", "b_T", "a_kT", "c_e", "c_ln", "c_x", "a_s", "a_es", "a_p", "c_hr", "a_ya", "t_sel",
    "t_xb"),
       "v": Steps("q_sq_ready", "q_ss_ready", "q_ms40", "q_qk_scaled", "b_s1", "b_p", "c_m0", "c_abs", "c_lf0", "c_qk", "c_qk1", "c_nq", "c_nq1", "c_lf", "c_i", "c_mt",
    "c_d", "c_S", "c_den0", "c_den1", "c_denabs", "c_den2", "c_rd", "c_dg", "c_nn1", "c_nn2", "a_qT", "a_b",
    "c_cq", "b_y", "c_cqr", "c_bcs", "a_l", "a_m1", "a_m2", "a_m3", "c_n1", "c_n2", "c_h", "c_h2",
    "c_u", "a_den", "a_rd", "a_pn", "c_hms", "c_hinv", "a_PT", "c_hy", "c_hy2", "c_y", "c_t1",
    "c_t2", "c_cn")}


PRIMED = {
    "evac_a": 4, "evac_v": 4, "x2_done": 32, "slot_free": RING, "gated": 3, "merged": 1,
    "q_evac": 2, "s_evac": 2, "s_mm": 2, "idx1": 1, "y_final": 1, "tile_v": tile.n, "dotted": 1, "gate_ready": 1,
}


def build(nc, x_prompt, x_sample, cache_k, cache_v, state_pool, st_c, st_n, st_m, rel, relr, consts, rows, cols,
          gains, keysT, w_pool, sinkcol, w_z, w_merge, w_o, w_q, uv, selmat,
          y_p, y_s, k_p, v_p, pool_p, c_p, n_p, m_p, k_s, v_s, pool_s, c_s, n_s, m_s):
    biasfull = nc.dram_tensor("biasfull", [P, AH * 2 * P], F32).ap()
    scr_qk = nc.dram_tensor("scr_qk", [NS, 2, CH * CD], F32).ap()
    scr_g = nc.dram_tensor("scr_g", [2, NS, CH], F32).ap()
    ctx = ExitStack()
    with ctx:
        def sb(name, shape, dt=F32):
            return ctx.enter_context(nc.sbuf_tensor(name, shape, dt))

        names = STEPS + list(PRIMED) + OTHERS + [f"got{i}" for i in range(RING)]
        s = {n: ctx.enter_context(nc.semaphore(n)) for n in names}
        got = [s[f"got{r}"] for r in range(RING)]
        w_in = [s["w_in0"], s["w_in1"]]

        ps = ctx.enter_context(nc.psum_tensor("ps", [P, 8, 512], F32))
        psf = ps[:, :, :].rearrange("p b n -> p (b n)")

        cst = sb("cst", [P, C_KEEP])
        ident = cst[:, C_ID:C_ID + P]
        tri = cst[:, C_TRI:C_TRI + P]
        cmask = cst[:, C_MASK:C_MASK + P]
        last_row = cst[:, C_LAST:C_LAST + P]
        iota16 = cst[:, C_IOTA:C_IOTA + 16]
        ones = sb("ones", [P, P])
        row = sb("row", [P, R_ALL])
        col = sb("col", [P, 8])
        grow = sb("grow", [P, D])
        keys = sb("keys", [P, 2, NKEY])
        wpool = sb("wpool", [P, 4, P])
        pmask = sb("pmask", [P, NT])
        xin = sb("xin", [P, NT, D])
        xT = sb("xT", [P, KC, TOK])
        yT = sb("yT", [P, 12, TOK])
        arena = sb("arena", [P, RING * 2 * D])
        R = sb("R", [P, 4 * D])
        wbuf = sb("wbuf", [P, 2, KC * ZC])
        T = sb("T", [P, 3888])
        kTr = sb("kTr", [P, 2 * P])
        vprev = sb("vprev", [P, P])
        pinT = sb("pinT", [P, 4, 16 + P])
        tab = sb("tab", [P, 4, P])
        CT = sb("CT", [P, CH, CD1])
        mprev = sb("mprev", [P, CH])

        z = arena[:, 0:NT * ZW].rearrange("p (t n) -> p t n", t=NT)
        bias = arena[:, NT * ZW:NT * ZW + 2048]
        ring = arena[:, :].rearrange("p (r n) -> p r n", r=RING)
        xs = R[:, :].rearrange("p (t n) -> p t n", t=NT)
        L = R[:, 0:2048].rearrange("p (h n) -> p h n", h=AH)
        PT = R[:, 2048:4096].rearrange("p (i n) -> p i n", i=16)
        mT = R[:, :].rearrange("p (c n) -> p c n", c=KC)
        qks = T[:, 0:640]
        pcs = T[:, 640:1664]
        kcs = T[:, 1664:2176]
        qTs = T[:, 2176:2688].rearrange("p (j n) -> p j n", j=4)
        tmpi = T[:, 2688:3204]
        sm = T[:, 3204:3888]
        qcT = yT[:, 8, :]
        kcT = yT[:, 9, :]
        Am = yT[:, 10, :]
        STs = yT[:, 11, :]
        pA = sb("pA", [P, 4, 16 + P])
        pB = sb("pB", [P, 4, 16 + P])

        sgs = T[:, 0:1536].rearrange("p (b n) -> p b n", b=3)
        pr = T[:, 1536:2048]
        gates = T[:, 0:512].rearrange("p (t n) -> p t n", t=NT)
        eidx = T[:, 512:1024].bitcast(U32).rearrange("p (t n) -> p t n", t=NT)
        v16, i16, f16 = T[:, 1024:1216], T[:, 1216:1408].bitcast(U32), T[:, 1408:1536]
        ew = T[:, 1536:1600]
        pab = T[:, 1600:1728].bitcast(U32).rearrange("p (k m) -> p k m", k=2)
        pabf = T[:, 1728:1856].rearrange("p (k m) -> p k m", k=2)
        eab = T[:, 1856:2048].rearrange("p (k m) -> p k m", k=3)
        esm, esr = T[:, 2048:2052], T[:, 2052:2056]
        ssb = yT[:, 2:4, :].rearrange("p k (t n) -> p k t n", t=NT)
        srep = yT[:, 4:6, :].rearrange("p k (t n) -> p k t n", t=NT)
        cand = yT[:, 6:8, :].rearrange("p k n -> p (k n)")
        crep = yT[:, 8:10, :].rearrange("p k n -> p (k n)")
        xcur = T[:, 1024:2048]
        dgs = T[:, 2048:3072].rearrange("p (r n) -> p r n", r=8)
        dots, gel, islot = T[:, 3072:3080], T[:, 3080:3088], T[:, 3088:3120].bitcast(U32)
        zs = arena[0:NS, 0:ZW]
        NP = NS * CH
        qb, kb, Cs = (arena[:, ZW + 4096 * i:ZW + 4096 * (i + 1)].rearrange("p (m d) -> p m d", m=NP) for i in range(3))
        Ks, Vs, KTs = yT[:, 0:NS, P:2 * P], yT[:, 0:NS, 2 * P:3 * P], yT[:, 0:NS, 3 * P:4 * P]
        spool, full = xin[:, 1, 0:512], xin[:, 1, 512:1024].rearrange("p (c n r) -> p c n r", c=4, n=NS)
        X = xin[:, 2:4, :].rearrange("p t n -> p (t n)")
        relrep, sbuck, misc = X[0:32, 0:64], X[0:32, 64:192], X[0:64, 192:196]
        qTn, Sn, bias_s, Ls, PTs = X[:, 196:228], X[:, 228:292], X[0:64, 292:420], X[0:64, 420:548], X[:, 548:612]
        am, amx, anm, asd, aes, ars, adn, ard = (X[0:64, 612 + i:613 + i] for i in range(8))
        psum_s, pool_s_in = X[:, 620:652].rearrange("p (c n) -> p c n", c=4), X[:, 652:684].rearrange("p (c n) -> p c n", c=4)
        vT, coT, bc = X[:, 684:716], X[:, 716:748], X[:, 748:876].rearrange("p (k m) -> p k m", k=4)
        q32, k32, n32, t32 = (X[0:NP, 876 + P * i:876 + P * (i + 1)] for i in range(4))
        g32 = X[0:NP, 1388:1390]
        c1 = X[0:NP, 1390:1420]
        dg32 = X[0:NP, 1420:1548].rearrange("p (k m) -> p k m", k=4)
        cq, num, num2, hh, hq, hms_s, hinv_s, hr_s, us = (X[:, 1548 + 32 * i:1580 + 32 * i] for i in range(9))
        qTsmp = X[:, 1836:1964].rearrange("p (k m) -> p k m", k=2)
        selT, sel = X[0:64, 1964:1972], X[0:NS, 1972:2036]

        def small(a, n):
            return sm[:, a:a + n]

        ssq, ms4, inv4, rstd = small(0, 4), small(4, 4), small(8, 4), small(12, 4)
        ss40, ms40, inv40, r40 = small(16, 40), small(56, 40), small(96, 40), small(136, 40)
        gts, absf, expf, lnf, minf = small(176, 32), small(208, 16), small(224, 16), small(240, 16), small(256, 16)
        lf = small(272, 16)
        bM, asb, rmax, bml, args, exps = small(288, 8), small(296, 4), small(300, 4), small(304, 8), small(312, 16), small(328, 16)
        mx8, mxs, negmx, sinkd, esink, rsum, aden, arden = (small(344 + 8 * i, 8) for i in range(8))
        dn, rd = small(408, 4), small(412, 4)
        hss, hms, hinv, hr = small(416, 16), small(432, 16), small(448, 16), small(464, 16)

        block = ctx.enter_context(nc.Block())

        def hold(engine, sem, value):
            engine.wait_ge(sem, value)
            engine.nop(nofuse=True)

        def tokens(p):
            return (P, NT) if p < PASSES else (NS, 1)

        def tiles_a(p):
            return 2 if p < PASSES else 1

        def norms(p, which, t):
            return p * 2 * NT + which * NT + t if p < PASSES else 2 * PASSES * NT + which


        def sample_loads(sp, at):
            sp.dma_start(k_s[:, 0:W - 1, :], cache_k[:, 1:W, :]).then_inc(s["kscr"], 16)
            sp.dma_start(v_s[:, 0:W - 1, :], cache_v[:, 1:W, :]).then_inc(s["kscr"], 16)
            sp.dma_start(pool_s[:, 0:HIST - 1, :], state_pool[:, 1:HIST, :]).then_inc(s["outs"], 16)
            sp.dma_start(spool[0:NS * HIST, :], state_pool.rearrange("n r c -> (n r) c")).then_inc(s["b_n"], 16)
            sp.dma_start(relrep, relr).then_inc(s["c_load"], 16)
            sp.dma_start(sbuck, consts[0:32, C_SBUCK:C_ALL]).then_inc(s["c_load"], 16)
            sp.dma_start(misc, sinkcol).then_inc(s["c_load"], 16)
            sp.dma_start(selT, selmat[:, 0:NS]).then_inc(s["c_load"], 16)
            sp.dma_start(sel, selmat[0:NS, NS:NS + 64]).then_inc(s["c_load"], 16)
            sp.dma_start(n32, st_n).then_inc(s["c_load"], 16)
            sp.dma_start(c1[:, 2:3], st_m).then_inc(s["c_load"], 16)
            sp.dma_start(Cs, st_c).then_inc(s["c_load"], 16)
            sp.wait_ge(s["evac_a"], 2 * NZ * PASSES + 4 + NZ)
            sp.dma_start(scr_qk, zs[:, CQ0:CQ0 + 1024].rearrange("n (k m) -> n k m", k=2)).then_inc(s["c_scr"], 16)
            sp.dma_start(scr_g.rearrange("k n h -> n k h"), zs[:, G0:G0 + 8].rearrange("n (k h) -> n k h", k=2)).then_inc(s["c_scr"], 16)
            sp.dma_start(pool_s[:, HIST - 1, :], zs[:, PIN0:PIN0 + 512]).then_inc(s["outs"], 16)
            sp.wait_ge(s["c_scr"], 32)
            sp.dma_start(g32, scr_g.rearrange("k n h -> (n h) k"), allow_slow_non_contiguous=True).then_inc(s["c_load2"], 16)
            for i, t in enumerate((q32, k32)):
                sp.dma_start(t, at(scr_qk, i * CH * CD, [[2 * CH * CD, NS], [CD, CH], [1, CD]])).then_inc(s["c_load2"], 16)
            for i, t in enumerate((qb, kb)):
                sp.dma_start(t.rearrange("p (n h) d -> p n (h d)", n=NS), at(scr_qk, i * CH * CD, [[0, P], [2 * CH * CD, NS], [1, CH * CD]])
                             ).then_inc(s["c_load2"], 16)
            sp.wait_ge(s["qkn"], PASSES + 1)
            sp.dma_start(k_s[:, W - 1, :], zs[:, 512:640]).then_inc(s["kscr"], 16)
            sp.dma_start(v_s[:, W - 1, :], zs[:, V0:V0 + P]).then_inc(s["kscr"], 16)
            sp.wait_ge(s["kscr"], 64)
            sp.dma_start(Ks, k_s.rearrange("n k c -> k n c")).then_inc(s["k_load"], 16)
            sp.dma_start(Vs, v_s.rearrange("n k c -> k n c")).then_inc(s["k_load"], 16)
            sp.wait_ge(s["smp_v"], SMP["v"].at("c_mt"))
            sp.dma_start(m_s, c1[:, 8:9]).then_inc(s["outs"], 16)
            sp.wait_ge(s["smp_v"], SMP["v"].at("c_nn2"))
            sp.dma_start(n_s, n32).then_inc(s["outs"], 16)
            sp.wait_ge(s["smp_v"], SMP["v"].at("c_cn"))
            sp.dma_start(c_s, Cs).then_inc(s["state_c_stored"], 16)

        def sample_tensor(pe):
            mm, tr = nc.tensor.matmul, nc.tensor.transpose
            id8 = ident[0:NS, 0:NS]
            for h in range(CH):
                tr(ps[:, 0, h * NS:(h + 1) * NS], zs[:, CV0 + h * CD1:CV0 + h * CD1 + CD], id8)
            for h in range(CH):
                last = tr(ps[:, 0, 32 + h * NS:32 + (h + 1) * NS], zs[:, CO0 + h * CD:CO0 + (h + 1) * CD], id8)
            last.then_inc(s["smp_p"], SMP["p"].step("c_tr"))
            for c in range(4):
                last = tr(ps[:, 1, c * NS:(c + 1) * NS], zs[:, PIN0 + c * P:PIN0 + (c + 1) * P], id8)
            last.then_inc(s["smp_p"], SMP["p"].step("b_xtr"))
            pe.wait_ge(s["b_n"], 16)
            for c in range(4):
                last = tr(ps[:, 2, c * P:c * P + NS * HIST], spool[0:NS * HIST, c * P:(c + 1) * P], ident[0:NS * HIST, 0:NS * HIST])
            last.then_inc(s["smp_p"], SMP["p"].step("b_tr"))
            pe.wait_ge(s["c_load"], 16 * 8)
            mm(ps[0:64, 3, 0:P], relrep, sbuck, start=True, stop=True).then_inc(s["smp_p"], SMP["p"].step("a_bmm"))
            pe.wait_ge(s["qkn"], PASSES + 1)
            for j in range(4):
                last = tr(ps[:, 4, j * NS:(j + 1) * NS], zs[:, j * P:(j + 1) * P], id8)
            last.then_inc(s["smp_p"], SMP["p"].step("a_qtr"))
            pe.wait_ge(s["k_load"], 32)
            for n in range(NS):
                last = tr(ps[:, 5 + n // 4, (n % 4) * P:(n % 4 + 1) * P], Ks[:, n, :], ident)
            last.then_inc(s["smp_p"], SMP["p"].step("a_ktr"))
            pe.wait_ge(s["smp_v"], SMP["v"].at("b_p"))
            for c in range(4):
                last = mm(ps[:, 7, c * NS:(c + 1) * NS], wpool[:, c, :], pool_s_in[:, c, :], start=True, stop=True)
            last.then_inc(s["smp_p"], SMP["p"].step("b_mm"))
            pe.wait_ge(s["smp_v"], SMP["v"].at("c_dg"))
            mm(ps[:, 0, 0:P], ones[0:NP, :], dg32.rearrange("p k m -> p (k m)"), start=True, stop=True).then_inc(s["smp_p"], SMP["p"].step("c_bc"))
            pe.wait_ge(s["smp_a"], SMP["a"].at("a_kT"))
            pe.wait_ge(s["smp_v"], SMP["v"].at("a_qT"))
            for n in range(NS):
                for kv in range(2):
                    last = mm(ps[:, 1 + kv, n * AG:(n + 1) * AG], KTs[64 * kv:64 * kv + 64, n, :], qTn[64 * kv:64 * kv + 64, n * AG:(n + 1) * AG],
                              start=True, stop=True)
            last.then_inc(s["smp_p"], SMP["p"].step("a_smm"))
            pe.wait_ge(s["smp_a"], SMP["a"].at("a_s"))
            tr(ps[0:64, 4, 0:P], Sn, ident).then_inc(s["smp_p"], SMP["p"].step("a_str"))
            pe.wait_ge(s["smp_v"], SMP["v"].at("c_h2"))
            mm(ps[:, 5, 0:NP], ones[:, :], hq, start=True, stop=True).then_inc(s["smp_p"], SMP["p"].step("c_hmm"))
            pe.wait_ge(s["smp_v"], SMP["v"].at("a_pn"))
            tr(ps[:, 6, 0:64], Ls, ident[0:64, 0:64]).then_inc(s["smp_p"], SMP["p"].step("a_ptr"))
            pe.wait_ge(s["smp_v"], SMP["v"].at("a_PT"))
            for n in range(NS):
                for kv in range(2):
                    c = n * AH + kv * AG
                    last = mm(ps[64 * kv:64 * kv + 64, 4, n * AG:(n + 1) * AG], Vs[:, n, 64 * kv:64 * kv + 64], PTs[:, c:c + AG],
                              start=True, stop=True)
            last.then_inc(s["smp_p"], SMP["p"].step("a_pv"))
            pe.wait_ge(s["smp_a"], SMP["a"].at("a_ya"))
            pe.wait_ge(s["smp_v"], SMP["v"].at("b_y"))
            pe.wait_ge(s["smp_v"], SMP["v"].at("c_y"))

        def sample_scalar(act):
            f = nc.scalar.activation
            act.wait_ge(s["inv40"], PASSES + 1)
            f(r40[0:NS, 0:10], inv40[0:NS, 0:10], ACT.Sqrt).then_inc(s["r40"], 1)
            act.wait_ge(s["smp_p"], SMP["p"].at("c_tr"))
            f(coT.rearrange("p (n h) -> p h n", h=CH), ps[:, 0, 32:64].rearrange("p (h n) -> p h n", h=CH), ACT.Sigmoid).then_inc(s["smp_a"], SMP["a"].step("m_sig"))
            f(vT.rearrange("p (n h) -> p h n", h=CH), ps[:, 0, 0:32].rearrange("p (h n) -> p h n", h=CH), ACT.Copy).then_inc(s["smp_a"], SMP["a"].step("c_T"))
            act.wait_ge(s["smp_p"], SMP["p"].at("b_tr"))
            f(full[:, :, :, 0:HIST], ps[:, 2, :].rearrange("p (c m) -> p c m", c=4)[:, :, 0:NS * HIST].rearrange("p c (n r) -> p c n r", n=NS),
              ACT.Copy)
            act.wait_ge(s["smp_p"], SMP["p"].at("b_xtr"))
            f(full[:, :, :, HIST], ps[:, 1, 0:32].rearrange("p (c n) -> p c n", c=4), ACT.Copy).then_inc(s["smp_a"], SMP["a"].step("b_T"))
            act.wait_ge(s["smp_p"], SMP["p"].at("a_ktr"))
            f(KTs, ps[:, 5:7, :].rearrange("p b (n k) -> p (b n) k", n=4), ACT.Copy).then_inc(s["smp_a"], SMP["a"].step("a_kT"))
            act.wait_ge(s["smp_v"], SMP["v"].at("c_abs"))
            f(c1[:, 4:5], c1[:, 3:4], ACT.Exp, scale=-1.0).then_inc(s["smp_a"], SMP["a"].step("c_e"))
            act.wait_ge(s["smp_a"], SMP["a"].at("c_e"))
            f(c1[:, 5:6], c1[:, 4:5], ACT.Ln, bias=1.0).then_inc(s["smp_a"], SMP["a"].step("c_ln"))
            act.wait_ge(s["smp_v"], SMP["v"].at("c_d"))
            f(c1[:, 12:15], c1[:, 9:12], ACT.Exp).then_inc(s["smp_a"], SMP["a"].step("c_x"))
            act.wait_ge(s["smp_p"], SMP["p"].at("a_smm"))
            f(Sn.rearrange("p (n k j) -> p k n j", k=AKV, j=AG), ps[:, 1:3, 0:32].rearrange("p k (n j) -> p k n j", j=AG), ACT.Copy).then_inc(s["smp_a"], SMP["a"].step("a_s"))
            act.wait_ge(s["smp_v"], SMP["v"].at("a_m3"))
            f(aes, asd, ACT.Exp).then_inc(s["smp_a"], SMP["a"].step("a_es"))
            f(Ls, Ls, ACT.Exp, bias=anm, accum_out=ars).then_inc(s["smp_a"], SMP["a"].step("a_p"))
            act.wait_ge(s["smp_v"], SMP["v"].at("c_hinv"))
            f(hr_s, hinv_s, ACT.Sqrt).then_inc(s["smp_a"], SMP["a"].step("c_hr"))
            act.wait_ge(s["smp_p"], SMP["p"].at("a_pv"))
            act.wait_ge(s["smp_p"], SMP["p"].at("a_ktr"))
            f(yT[:, 0:4, 0:NS], ps[:, 4, 0:32].rearrange("p (n j) -> p j n", j=AG), ACT.Copy).then_inc(s["smp_a"], SMP["a"].step("a_ya"))

        def sample_vector(dve):
            v = nc.vector
            n = PASSES + 1
            scale = float(CD) ** -0.5
            dve.wait_ge(s["evac_a"], 2 * NZ * PASSES + 4 + NZ)
            sq = R[0:NS, 0:640]
            v.tensor_tensor(sq, zs[:, 0:640], zs[:, 0:640], ALU.mult).then_inc(s["smp_v"], SMP["v"].step("q_sq_ready"))
            dve.wait_ge(s["smp_v"], SMP["v"].at("q_sq_ready"))
            v.tensor_reduce(ss40[0:NS, 0:10], sq.rearrange("p (h d) -> p h d", d=AD), AX.X, ALU.add).then_inc(s["smp_v"], SMP["v"].step("q_ss_ready"))
            dve.wait_ge(s["smp_v"], SMP["v"].at("q_ss_ready"))
            v.tensor_scalar(ms40[0:NS, 0:10], ss40[0:NS, 0:10], 1.0 / AD, EPS, ALU.mult, ALU.add).then_inc(s["smp_v"], SMP["v"].step("q_ms40"))
            dve.wait_ge(s["smp_v"], SMP["v"].at("q_ms40"))
            v.reciprocal(inv40[0:NS, 0:10], ms40[0:NS, 0:10]).then_inc(s["inv40"], 1)
            dve.wait_ge(s["r40"], n)
            zq = zs[:, 0:640].rearrange("p (h d) -> p h d", d=AD)
            v.tensor_tensor(zq, zq, r40[0:NS, 0:10].unsqueeze(2).broadcast_to([NS, 10, AD]), ALU.mult).then_inc(s["smp_v"], SMP["v"].step("q_qk_scaled"))
            dve.wait_ge(s["smp_v"], SMP["v"].at("q_qk_scaled"))
            v.tensor_tensor(zs[:, 0:640], zs[:, 0:640], row[0:NS, R_QK:R_QK + 640], ALU.mult).then_inc(s["qkn"], 1)
            dve.wait_ge(s["smp_a"], SMP["a"].at("b_T"))
            for c, w in enumerate(POOLW):
                last = v.tensor_reduce(psum_s[:, c, :], full[:, c, :, 16 - w:16], AX.X, ALU.add)
            last.then_inc(s["smp_v"], SMP["v"].step("b_s1"))
            dve.wait_ge(s["smp_v"], SMP["v"].at("b_s1"))
            for c, w in enumerate(POOLW):
                last = v.scalar_tensor_tensor(pool_s_in[:, c, :], psum_s[:, c, :], 1.0 / w, full[:, c, :, HIST], ALU.mult, ALU.subtract)
            last.then_inc(s["smp_v"], SMP["v"].step("b_p"))
            dve.wait_ge(s["c_load"], 16 * 8)
            dve.wait_ge(s["c_load2"], 16 * 5)
            v.tensor_tensor(c1[:, 0:2], g32, misc[0:NP, 1:3], ALU.add).then_inc(s["smp_v"], SMP["v"].step("c_m0"))
            dve.wait_ge(s["smp_v"], SMP["v"].at("c_m0"))
            v.scalar_tensor_tensor(c1[:, 3:4], c1[:, 1:2], -1.0, c1[:, 1:2], ALU.mult, ALU.max).then_inc(s["smp_v"], SMP["v"].step("c_abs"))
            v.tensor_scalar(c1[:, 6:7], c1[:, 1:2], 0.0, None, ALU.min).then_inc(s["smp_v"], SMP["v"].step("c_lf0"))
            v.tensor_tensor(t32, q32, k32, ALU.mult).then_inc(s["smp_v"], SMP["v"].step("c_qk"))
            dve.wait_ge(s["smp_v"], SMP["v"].at("c_qk"))
            v.tensor_reduce(c1[:, 16:17], t32, AX.X, ALU.add).then_inc(s["smp_v"], SMP["v"].step("c_qk1"))
            dve.wait_ge(s["smp_v"], SMP["v"].at("c_qk1"))
            v.tensor_tensor(t32, q32, n32, ALU.mult).then_inc(s["smp_v"], SMP["v"].step("c_nq"))
            dve.wait_ge(s["smp_v"], SMP["v"].at("c_nq"))
            v.tensor_reduce(c1[:, 17:18], t32, AX.X, ALU.add).then_inc(s["smp_v"], SMP["v"].step("c_nq1"))
            dve.wait_ge(s["smp_a"], SMP["a"].at("c_ln"))
            dve.wait_ge(s["smp_v"], SMP["v"].at("c_lf0"))
            v.tensor_tensor(c1[:, 7:8], c1[:, 6:7], c1[:, 5:6], ALU.subtract).then_inc(s["smp_v"], SMP["v"].step("c_lf"))
            dve.wait_ge(s["smp_v"], SMP["v"].at("c_lf"))
            v.tensor_tensor(c1[:, 18:19], c1[:, 7:8], c1[:, 2:3], ALU.add).then_inc(s["smp_v"], SMP["v"].step("c_i"))
            dve.wait_ge(s["smp_v"], SMP["v"].at("c_i"))
            v.tensor_tensor(c1[:, 8:9], c1[:, 18:19], c1[:, 0:1], ALU.max).then_inc(s["smp_v"], SMP["v"].step("c_mt"))
            dve.wait_ge(s["smp_v"], SMP["v"].at("c_mt"))
            v.tensor_tensor(c1[:, 9:10], c1[:, 18:19], c1[:, 8:9], ALU.subtract)
            v.tensor_tensor(c1[:, 10:11], c1[:, 0:1], c1[:, 8:9], ALU.subtract)
            v.tensor_scalar(c1[:, 11:12], c1[:, 8:9], -1.0, None, ALU.mult).then_inc(s["smp_v"], SMP["v"].step("c_d"))
            dve.wait_ge(s["smp_a"], SMP["a"].at("c_x"))
            v.tensor_copy(c1[:, 19:20], c1[:, 12:13])
            v.tensor_scalar(c1[:, 20:21], c1[:, 13:14], scale, None, ALU.mult).then_inc(s["smp_v"], SMP["v"].step("c_S"))
            dve.wait_ge(s["smp_v"], SMP["v"].at("c_S"))
            dve.wait_ge(s["smp_v"], SMP["v"].at("c_nq1"))
            v.tensor_tensor(c1[:, 21:22], c1[:, 20:21], c1[:, 16:17], ALU.mult).then_inc(s["smp_v"], SMP["v"].step("c_den0"))
            dve.wait_ge(s["smp_v"], SMP["v"].at("c_den0"))
            v.scalar_tensor_tensor(c1[:, 23:24], c1[:, 17:18], c1[:, 19:20], c1[:, 21:22], ALU.mult, ALU.add).then_inc(s["smp_v"], SMP["v"].step("c_den1"))
            dve.wait_ge(s["smp_v"], SMP["v"].at("c_den1"))
            v.scalar_tensor_tensor(c1[:, 25:26], c1[:, 23:24], -1.0, c1[:, 23:24], ALU.mult, ALU.max).then_inc(s["smp_v"], SMP["v"].step("c_denabs"))
            dve.wait_ge(s["smp_v"], SMP["v"].at("c_denabs"))
            v.tensor_tensor(c1[:, 24:25], c1[:, 25:26], c1[:, 14:15], ALU.max).then_inc(s["smp_v"], SMP["v"].step("c_den2"))
            dve.wait_ge(s["smp_v"], SMP["v"].at("c_den2"))
            v.reciprocal(c1[:, 22:23], c1[:, 24:25]).then_inc(s["smp_v"], SMP["v"].step("c_rd"))
            dve.wait_ge(s["smp_v"], SMP["v"].at("c_rd"))
            v.tensor_tensor(dg32, ident[0:NP, 0:NP].unsqueeze(1).broadcast_to([NP, 4, NP]), c1[:, 19:23].unsqueeze(2).broadcast_to([NP, 4, NP]),
                            ALU.mult).then_inc(s["smp_v"], SMP["v"].step("c_dg"))
            v.tensor_scalar(t32, k32, c1[:, 20:21], None, ALU.mult).then_inc(s["smp_v"], SMP["v"].step("c_nn1"))
            dve.wait_ge(s["smp_v"], SMP["v"].at("c_nn1"))
            v.scalar_tensor_tensor(n32, n32, c1[:, 19:20], t32, ALU.mult, ALU.add).then_inc(s["smp_v"], SMP["v"].step("c_nn2"))
            dve.wait_ge(s["smp_p"], SMP["p"].at("a_qtr"))
            v.tensor_copy(qTn.rearrange("p (n j) -> p j n", j=AG), ps[:, 4, 0:32].rearrange("p (j n) -> p j n", j=AG)).then_inc(s["smp_v"], SMP["v"].step("a_qT"))
            dve.wait_ge(s["smp_p"], SMP["p"].at("a_bmm"))
            v.tensor_copy(bias_s, ps[0:64, 3, 0:P]).then_inc(s["smp_v"], SMP["v"].step("a_b"))
            Rv = R[:, :].rearrange("p (m d) -> p m d", m=NP)
            v.tensor_tensor(Rv, Cs, qb, ALU.mult).then_inc(s["smp_v"], SMP["v"].step("c_cq"))
            dve.wait_ge(s["smp_p"], SMP["p"].at("b_mm"))
            v.tensor_tensor(yT[:, 4:8, 0:NS], ps[:, 7, 0:32].rearrange("p (c n) -> p c n", c=4), col[:, 0:4].unsqueeze(2).broadcast_to([P, 4, NS]),
                            ALU.mult).then_inc(s["smp_v"], SMP["v"].step("b_y"))
            dve.wait_ge(s["smp_v"], SMP["v"].at("c_cq"))
            v.tensor_reduce(cq, Rv, AX.X, ALU.add).then_inc(s["smp_v"], SMP["v"].step("c_cqr"))
            dve.wait_ge(s["smp_p"], SMP["p"].at("c_bc"))
            v.tensor_copy(bc, ps[:, 0, 0:P].rearrange("p (k m) -> p k m", k=4)).then_inc(s["smp_v"], SMP["v"].step("c_bcs"))
            dve.wait_ge(s["smp_p"], SMP["p"].at("a_str"))
            dve.wait_ge(s["smp_v"], SMP["v"].at("a_b"))
            v.scalar_tensor_tensor(Ls, ps[0:64, 4, 0:P], float(AD) ** -0.5, bias_s, ALU.mult, ALU.add).then_inc(s["smp_v"], SMP["v"].step("a_l"))
            dve.wait_ge(s["smp_v"], SMP["v"].at("a_l"))
            v.tensor_reduce(am, Ls, AX.X, ALU.max).then_inc(s["smp_v"], SMP["v"].step("a_m1"))
            dve.wait_ge(s["smp_v"], SMP["v"].at("a_m1"))
            v.tensor_tensor(amx, am, misc[:, 0:1], ALU.max).then_inc(s["smp_v"], SMP["v"].step("a_m2"))
            dve.wait_ge(s["smp_v"], SMP["v"].at("a_m2"))
            v.tensor_scalar(anm, amx, -1.0, None, ALU.mult)
            v.tensor_tensor(asd, misc[:, 0:1], amx, ALU.subtract).then_inc(s["smp_v"], SMP["v"].step("a_m3"))
            dve.wait_ge(s["smp_v"], SMP["v"].at("c_bcs"))
            dve.wait_ge(s["smp_v"], SMP["v"].at("c_cqr"))
            dve.wait_ge(s["smp_a"], SMP["a"].at("c_T"))
            v.tensor_tensor(num, cq, bc[:, 0, :], ALU.mult)
            v.tensor_tensor(num2, vT, bc[:, 2, :], ALU.mult).then_inc(s["smp_v"], SMP["v"].step("c_n1"))
            dve.wait_ge(s["smp_v"], SMP["v"].at("c_n1"))
            v.tensor_tensor(num, num, num2, ALU.add).then_inc(s["smp_v"], SMP["v"].step("c_n2"))
            dve.wait_ge(s["smp_v"], SMP["v"].at("c_n2"))
            v.tensor_tensor(hh, num, bc[:, 3, :], ALU.mult).then_inc(s["smp_v"], SMP["v"].step("c_h"))
            dve.wait_ge(s["smp_v"], SMP["v"].at("c_h"))
            v.tensor_tensor(hq, hh, hh, ALU.mult).then_inc(s["smp_v"], SMP["v"].step("c_h2"))
            v.tensor_tensor(us, vT, bc[:, 1, :], ALU.mult).then_inc(s["smp_v"], SMP["v"].step("c_u"))
            dve.wait_ge(s["smp_a"], SMP["a"].at("a_es"))
            dve.wait_ge(s["smp_a"], SMP["a"].at("a_p"))
            v.tensor_tensor(adn, ars, aes, ALU.add).then_inc(s["smp_v"], SMP["v"].step("a_den"))
            dve.wait_ge(s["smp_v"], SMP["v"].at("a_den"))
            v.reciprocal(ard, adn).then_inc(s["smp_v"], SMP["v"].step("a_rd"))
            dve.wait_ge(s["smp_v"], SMP["v"].at("a_rd"))
            v.tensor_scalar(Ls, Ls, ard, None, ALU.mult).then_inc(s["smp_v"], SMP["v"].step("a_pn"))
            dve.wait_ge(s["smp_p"], SMP["p"].at("c_hmm"))
            v.tensor_scalar(hms_s, ps[:, 5, 0:NP], 1.0 / CD, EPS, ALU.mult, ALU.add).then_inc(s["smp_v"], SMP["v"].step("c_hms"))
            dve.wait_ge(s["smp_v"], SMP["v"].at("c_hms"))
            v.reciprocal(hinv_s, hms_s).then_inc(s["smp_v"], SMP["v"].step("c_hinv"))
            dve.wait_ge(s["smp_p"], SMP["p"].at("a_ptr"))
            v.tensor_copy(PTs, ps[:, 6, 0:64]).then_inc(s["smp_v"], SMP["v"].step("a_PT"))
            dve.wait_ge(s["smp_a"], SMP["a"].at("c_hr"))
            v.tensor_tensor(hh, hh, hr_s, ALU.mult).then_inc(s["smp_v"], SMP["v"].step("c_hy"))
            dve.wait_ge(s["smp_v"], SMP["v"].at("c_hy"))
            dve.wait_ge(s["smp_a"], SMP["a"].at("m_sig"))
            v.scalar_tensor_tensor(hq, hh, col[:, 4:5], coT, ALU.mult, ALU.mult).then_inc(s["smp_v"], SMP["v"].step("c_hy2"))
            dve.wait_ge(s["smp_v"], SMP["v"].at("c_hy2"))
            v.tensor_copy(yT[:, 8:12, 0:NS], hq.rearrange("p (n h) -> p h n", h=CH)).then_inc(s["smp_v"], SMP["v"].step("c_y"))
            dve.wait_ge(s["smp_v"], SMP["v"].at("c_u"))
            v.tensor_tensor(kb, kb, us.unsqueeze(2).broadcast_to([P, NP, CD]), ALU.mult).then_inc(s["smp_v"], SMP["v"].step("c_t1"))
            v.tensor_tensor(Cs, Cs, bc[:, 0, :].unsqueeze(2).broadcast_to([P, NP, CD]), ALU.mult).then_inc(s["smp_v"], SMP["v"].step("c_t2"))
            dve.wait_ge(s["smp_v"], SMP["v"].at("c_t1"))
            dve.wait_ge(s["smp_v"], SMP["v"].at("c_t2"))
            v.tensor_tensor(Cs, Cs, kb, ALU.add).then_inc(s["smp_v"], SMP["v"].step("c_cn"))

        BASE = PASSES * NT * P

        def sample_experts_tensor(pe):
            mm = nc.tensor.matmul
            pe.wait_ge(s["q_evac"], 2 * PH * (PASSES + 1) + 2)
            for k in range(2):
                last = mm(ps[0:64, 2 + k, 0:NKEY], qTsmp[:, k, :], keys[:, k, :], start=True, stop=True)
            last.then_inc(s["smp_p"], SMP["p"].step("sample_s"))
            for q in range(2):
                last = mm(ps[0:64, 4 + q, :], sel, xs[0:NS, 0, q * 512:(q + 1) * 512], start=True, stop=True)
            last.then_inc(s["smp_p"], SMP["p"].step("xb_mm"))
            for j in range(PK):
                pe.wait_ge(s["diagd"], BASE + j + 1)
                for q in range(2):
                    last = mm(ps[0:NS, q, :], dgs[0:64, j % 8, 0:NS], ring[0:64, j % RING, D + q * 512:D + (q + 1) * 512],
                              start=(j == 0), stop=(j == PK - 1))
                last.then_inc(s["slot_free"], 1)

        def sample_experts_scalar(act):
            f = nc.scalar.activation
            act.wait_ge(s["smp_p"], SMP["p"].at("sample_s"))
            f(ssb[0:64, :, 0, :], ps[0:64, 2:4, 0:NKEY], ACT.Copy).then_inc(s["smp_a"], SMP["a"].step("t_sel"))
            act.wait_ge(s["esub"], PH * PASSES + 1)
            f(ew[0:64, 0:16], ew[0:64, 0:16], ACT.Exp).then_inc(s["eexp"], 1)
            act.wait_ge(s["smp_p"], SMP["p"].at("xb_mm"))
            act.wait_ge(s["gate_ready"], PH * PASSES + 2)
            f(xcur[0:64, :].rearrange("p (q n) -> p q n", q=2), ps[0:64, 4:6, :], ACT.Copy).then_inc(s["smp_a"], SMP["a"].step("t_xb"))
            for j in range(PK // 2):
                act.wait_ge(s["dotted"], BASE + 2 * j + 3)
                k = 2 * j % 8
                f(gel[0:64, k:k + 2], dots[0:64, k:k + 2], ACT.Gelu).then_inc(s["gelud"], 1)

        def sample_experts_vector(dve, topk):
            v = nc.vector
            dve.wait_ge(s["smp_a"], SMP["a"].at("t_sel"))

            def write(e, experts_f):
                v.tensor_copy(eidx[0:64, 0:1, 0:PK], experts_f)
                v.tensor_tensor(gates[0:64, 0:1, 0:PK], e, esr[0:64, 0:1].unsqueeze(2).broadcast_to([64, 1, PK]), ALU.mult
                                ).then_inc(s["gate_ready"], 1)
            topk(PH * PASSES + 1, ssb, srep, 64, 1, write)
            dve.wait_ge(s["smp_a"], SMP["a"].at("t_xb"))
            for j in range(PK):
                r = j % RING
                dve.wait_ge(got[r], 16 * ((BASE + j) // RING + 1))
                v.tensor_tensor_reduce(ring[0:64, r, 0:D], ring[0:64, r, 0:D], xcur[0:64, :], 1.0, 0.0, ALU.mult, ALU.add,
                                       dots[0:64, r:r + 1]).then_inc(s["dotted"], 1)
                if j % 2 == 1:
                    dve.wait_ge(s["gelud"], (BASE + j + 1) // 2)
                    dve.wait_ge(s["slot_free"], BASE + j + 1)
                    for q in (j - 1, j):
                        v.tensor_scalar(dgs[0:64, q % 8, 0:NS], selT, gel[0:64, q % 8:q % 8 + 1], gates[0:64, 0, q:q + 1],
                                        ALU.mult, ALU.mult).then_inc(s["diagd"], 1)
            dve.wait_ge(s["slot_free"], BASE + PK + RING)
            v.tensor_tensor(xin[0:NS, 0, :].rearrange("p (q n) -> p q n", q=2), xin[0:NS, 0, :].rearrange("p (q n) -> p q n", q=2),
                            ps[0:NS, 0:2, :], ALU.add).then_inc(s["y_final"], 1)

        def sample_gpsimd(pool):
            pool.wait_ge(s["gate_ready"], PH * PASSES + 2)
            pool.wait_ge(s["smp_v"], SMP["v"].at("c_cn"))
            pool.wait_ge(s["state_c_stored"], 16)
            for j in range(PK):
                pool.wait_ge(s["slot_free"], BASE + j + 1)
                nc.gpsimd.indirect_dma_start(ring[0:64, j % RING, :], None, uv,
                                             bass.IndirectOffsetOnAxis(ap=eidx[0:64, 0, j:j + 1], axis=0)).then_inc(got[j % RING], 16)

        @block.sync
        def _(sp):
            def at(t, off, ap):
                return bass.AP(tensor=t.tensor, offset=off, ap=ap)

            sp.dma_start(cst[:, :], consts[:, 0:C_KEEP]).then_inc(s["setup"], 16)
            sp.dma_start(T[:, 0:512], consts[:, C_KEEP:C_ALL]).then_inc(s["setup"], 16)
            sp.dma_start(row[:, :], at(rows, 0, [[0, P], [1, R_ALL]])).then_inc(s["setup"], 16)
            sp.dma_start(col[:, :], cols).then_inc(s["setup"], 16)
            sp.dma_start(keys[:, :, :], keysT).then_inc(s["setup"], 16)
            sp.dma_start(wpool[:, :, :], w_pool).then_inc(s["setup"], 16)
            sp.wait_ge(s["init_v"], 1)
            sp.dma_start(T[0:32, 512:520], rel).then_inc(s["setup"], 16)

            def gain(which, n):
                if n:
                    sp.wait_ge(s["xs_ready"], norms((n - 1) // 2, (n - 1) % 2, (NT if (n - 1) // 2 < PASSES else 1) - 1) + 1)
                sp.dma_start(grow[:, :], at(gains, which * D, [[0, P], [1, D]])).then_inc(s["g_in"], 16)

            used = [None]

            def weights(src, shape, count, sem, base, per):
                width = int(np.prod(shape))

                def load(i, k):
                    sp.dma_start(wbuf[:, k, 0:width], src[bass.ds(i, 1), :, :].rearrange("a p n -> (a p) n")).then_inc(w_in[k], 16)

                for k in range(2):
                    if used[0]:
                        sp.wait_ge(used[0][0], used[0][1 + k])
                    load(k, k)
                with sp.Fori(1, count // 2) as i:
                    for k in range(2):
                        sp.wait_ge(sem, base + per * (k - 1) + 2 * per * i)
                        load(2 * i + k, k)
                used[0] = (sem, base + per * (count - 1), base + per * count)

            for p in range(PASSES + 1):
                tiles = tokens(p)[1]
                if p < PASSES:
                    if p:
                        sp.wait_ge(s["y_out"], 16 * NT * p)
                    sp.dma_start(xin[:, :, :], x_prompt[p]).then_inc(s["x_in"], 16)
                else:
                    sp.wait_ge(s["y_out"], 16 * NT * p)
                    sp.dma_start(xin[0:NS, 0, :], x_sample).then_inc(s["x_in"], 16)
                gain(0, 2 * p)
                weights(w_z, (KC, ZC), NZ, s["z_mm"], NT * NZ * p, tiles)
                if p < PASSES:
                    if p == 0:
                        sp.wait_ge(s["buck_sb"], 1)
                        table = T[0:AH, 1024:1408]
                        sp.dma_start(bass.AP(tensor=biasfull.tensor, offset=0, ap=[[2 * P, AH], [AH * 2 * P, P], [1, 2 * P]]),
                                     bass.AP(tensor=table.tensor, offset=table.offset + P - 1, ap=[table.ap[0], [-1, P], [1, 2 * P]])
                                     ).then_inc(s["scratch_w"], 16)
                        sp.wait_ge(s["scratch_w"], 16)
                    sp.dma_start(bias, biasfull).then_inc(s["bias_in"], 16)
                else:
                    sample_loads(sp, at)
                if p == PASSES - 1:
                    last = NT - 1
                    sp.wait_ge(s["qkn"], PASSES)
                    sp.dma_start(k_p, z[:, last, 512:640]).then_inc(s["outs"], 16)
                    sp.dma_start(v_p, z[:, last, V0:V0 + P]).then_inc(s["outs"], 16)
                    sp.dma_start(pool_p, z[P - HIST:P, last, PIN0:PIN0 + 512]).then_inc(s["outs"], 16)
                    sp.wait_ge(s["state_out_sb"], 1)
                    sp.dma_start(c_p.rearrange("h e d -> e h d"), T[:, 0:512].rearrange("p (h d) -> p h d", h=CH)).then_inc(s["state_stored"], 16)
                    sp.dma_start(n_p.rearrange("h d -> d h"), CT[:, :, CD], allow_slow_non_contiguous=True).then_inc(s["outs"], 16)
                    sp.dma_start(m_p, mprev[0:1, :]).then_inc(s["outs"], 16)
                weights(w_merge, (12, P), 3 * KC, s["br_mm"], 3 * KC * p, 1)
                weights(w_o, (KC, OC), NO, s["o_mm"], NT * NO * p, tiles)
                gain(1, 2 * p + 1)
                weights(w_q, (KC, P), 2 * PH, s["kq_mm"], 2 * PH * p, 1)
                if p < PASSES:
                    with sp.Fori(0, NT) as t:
                        sp.wait_ge(s["y_final"], p * NT + t + 2)
                        sp.dma_start(y_p[p][:, bass.ds(t, 1), :], xin[:, bass.ds(t, 1), :]).then_inc(s["y_out"], 16)
                else:
                    sp.wait_ge(s["y_final"], p * NT + 2)
                    sp.dma_start(y_s, xin[0:NS, 0, :]).then_inc(s["y_out"], 16)
            sp.wait_ge(s["outs"], 16 * 9)
            sp.wait_ge(s["state_stored"], 16)
            sp.wait_ge(s["state_c_stored"], 16)
            sp.wait_ge(s["y_out"], 16 * (NT * PASSES + 1))

        @block.tensor
        def _(pe):
            mm = nc.tensor.matmul
            tr = nc.tensor.transpose
            pe.wait_ge(s["setup"], 16 * 7)
            pe.wait_ge(s["init_v"], 2)
            pe.wait_ge(s["init_p"], 2)
            mm(ps[0:AH, 0, 0:384], T[0:33, 512:520], T[0:33, 0:384], start=True, stop=True).then_inc(s["buck_mm"], 1)
            pe.wait_ge(s["buck_sb"], 1)

            def norm(p, which):
                rows_, tiles = tokens(p)
                for t in range(tiles):
                    n = norms(p, which, t)
                    pe.wait_ge(s["xs_ready"], n + 1)
                    if t >= 2:
                        pe.wait_ge(s["xT_ready"], n - 1)
                    for c in range(KC):
                        b = 2 * (t % 2) + c // 4
                        last = tr(ps[:, b, (c % 4) * P:(c % 4) * P + rows_], xs[0:rows_, t, c * P:(c + 1) * P],
                                  ident[0:rows_, 0:rows_])
                    last.then_inc(s["xs_tr"], 1)
                pe.wait_ge(s["xT_ready"], norms(p, which, tiles - 1) + 1)

            def project(p):
                rows_, tiles = tokens(p)
                with pe.Fori(0, NZ // 2) as i:
                    for k in range(2):
                        pe.wait_ge(w_in[k], 16 * (p * UNITS // 2 + 1) + 16 * i)
                        wv = wbuf[:, k, :].rearrange("p (c n) -> p c n", c=KC)
                        for t in range(tiles):
                            if t < 2:
                                pe.wait_ge(s["evac_a"], 2 * NZ * p + (t + 1 if p < PASSES else 3) + k * tiles_a(p) + 2 * tiles_a(p) * i)
                            else:
                                pe.wait_ge(s["evac_v"], 2 * NZ * p + t - 1 + 2 * k + 4 * i)
                            for c in range(KC):
                                last = mm(ps[0:rows_, 4 * k + t, 0:ZC], xT[:, c, t * P:t * P + rows_], wv[:, c, :],
                                          start=(c == 0), stop=(c == KC - 1))
                            last.then_inc(s["z_mm"], 1)

            def branches(p):
                pe.wait_ge(s["evac_a"], 2 * NZ * (p + 1) + 4)
                pe.wait_ge(s["evac_v"], 2 * NZ * (p + 1) + 4)
                pe.wait_ge(s["lf_ready"], p + 1)
                pe.wait_ge(s["ones_set"], p + 1)
                with pe.Fori(0, NT) as t:
                    here, before = p * NT + 2 + t, p * NT + 1 + t
                    pe.wait_ge(s["qks_ready"], here)
                    pe.wait_ge(s["ya_ready"], before)
                    pe.wait_ge(s["yaT_done"], before)
                    for j in range(4):
                        tr(ps[:, 0, j * P:(j + 1) * P], qks[:, j * P:(j + 1) * P], ident)
                    tr(ps[:, 1, 0:P], qks[:, 512:640], ident).then_inc(s["qk_tr"], 1)
                    pe.wait_ge(s["pcs_ready"], here)
                    pe.wait_ge(s["poolT_done"], before)
                    for j in range(4):
                        last = tr(ps[:, 2, j * P:(j + 1) * P], pcs[:, j * P:(j + 1) * P], ident)
                    last.then_inc(s["pin_tr"], 1)
                    pe.wait_ge(s["CT_ready"], before)
                    for j in range(4):
                        last = tr(ps[:, 4, j * P:(j + 1) * P], pcs[:, 512 + j * P:512 + (j + 1) * P], ident)
                    last.then_inc(s["cq_tr"], 1)
                    pe.wait_ge(s["kcs_ready"], here)
                    pe.wait_ge(s["nd_ready"], before)
                    for j in range(4):
                        last = tr(ps[:, 5, j * P:(j + 1) * P], kcs[:, j * P:(j + 1) * P], ident)
                    last.then_inc(s["ck_tr"], 1)
                    mm(ps[:, 7, 0:CH], tri, lf[:, bass.ds(CH * t, CH)], start=True, stop=True).then_inc(s["cs_mm"], 1)
                    pe.wait_ge(s["diag_ready"], here)
                    mm(ps[:, 6, :], ones[:, :], tmpi[:, 0:512], start=True, stop=True).then_inc(s["arow_mm"], 1)
                    pe.wait_ge(s["qcT_ready"], here)
                    pe.wait_ge(s["kcT_ready"], here)
                    for h in range(CH):
                        last = mm(ps[:, 4, h * P:(h + 1) * P], qcT[:, h * P:(h + 1) * P], kcT[:, h * P:(h + 1) * P],
                                  start=True, stop=True)
                    last.then_inc(s["S_mm"], 1)
                    pe.wait_ge(s["qT_ready"], here)
                    pe.wait_ge(s["kT_ready"], here)
                    pe.wait_ge(s["kT_shift"], before)
                    pe.wait_ge(s["pinT_ready"], here)
                    pe.wait_ge(s["PTd_ready"], before)
                    for h in range(AH):
                        j, kv = h // 2, h % 2
                        last = mm(ps[:, 2 * kv + j // 2, (j % 2) * 256:(j % 2) * 256 + 256], qTs[64 * kv:64 * kv + 64, j, :],
                                  kTr[64 * kv:64 * kv + 64, :], start=True, stop=True)
                    last.then_inc(s["scores_mm"], 1)
                    pe.wait_ge(s["M_ready"], here)
                    mm(ps[:, 7, 0:8], last_row, bM, start=True, stop=True).then_inc(s["bcast_mm"], 1)
                    pe.wait_ge(s["am0_ready"], here)
                    for h in range(CH):
                        last = mm(ps[:, 5 + h // 2, (h % 2) * CD1:(h % 2 + 1) * CD1], qcT[:, h * P:(h + 1) * P],
                                  CT[:, h, :], start=True, stop=True)
                    last.then_inc(s["inter_mm"], 1)
                    pe.wait_ge(s["Sm_ready"], here)
                    for h in range(CH):
                        last = tr(ps[:, 4, h * P:(h + 1) * P], Am[:, h * P:(h + 1) * P], ident)
                    last.then_inc(s["ST_tr"], 1)
                    pe.wait_ge(s["ST_ready"], here)
                    pe.wait_ge(s["interw_ready"], here)
                    for h in range(CH):
                        last = mm(ps[:, 5 + h // 2, (h % 2) * CD1:(h % 2 + 1) * CD1], STs[:, h * P:(h + 1) * P],
                                  z[:, t, CV0 + h * CD1:CV0 + (h + 1) * CD1], start=True, stop=True)
                    last.then_inc(s["intra_mm"], 1)
                    pe.wait_ge(s["wk_ready"], here)
                    pe.wait_ge(s["bml_ready"], here)
                    for h in range(CH):
                        last = mm(ps[:, 4 + 3 * (h // 2), (h % 2) * CD1:(h % 2 + 1) * CD1], kcs[:, h * P:(h + 1) * P],
                                  z[:, t, CV0 + h * CD1:CV0 + (h + 1) * CD1], start=True, stop=True)
                    last.then_inc(s["state_mm"], 1)
                    pe.wait_ge(s["P_exp"], here)
                    for i in range(16):
                        last = tr(ps[:, i // 4, (i % 4) * P:(i % 4 + 1) * P], L[:, i // 2, (i % 2) * P:(i % 2 + 1) * P], ident)
                    last.then_inc(s["PT_tr"], 1)
                    pe.wait_ge(s["PTa_ready"], here)
                    pe.wait_ge(s["PTd_ready"], here)
                    pe.wait_ge(s["v_shift"], before)
                    for h in range(AH):
                        kv, j = h // AG, h % AG
                        o = (2 * j + kv) * AD
                        mm(ps[:, 0, o:o + AD], PT[:, 2 * h, :], vprev[:, 64 * kv:64 * kv + 64], start=True, stop=False)
                        last = mm(ps[:, 0, o:o + AD], PT[:, 2 * h + 1, :],
                                  z[:, t, V0 + 64 * kv:V0 + 64 * kv + 64], start=False, stop=True)
                    last.then_inc(s["PV_mm"], 1)
                    pe.wait_ge(s["pooled_ready"], here)
                    for c in range(4):
                        last = mm(ps[:, 2, c * P:(c + 1) * P], wpool[:, c, :], pcs[:, c * P:(c + 1) * P], start=True, stop=True)
                    last.then_inc(s["pooly_mm"], 1)
                    pe.wait_ge(s["ya_ready"], here)
                    for j in range(4):
                        last = tr(ps[:, 1, j * P:(j + 1) * P], qks[:, j * P:(j + 1) * P], ident)
                    last.then_inc(s["yaT_tr"], 1)
                pe.wait_ge(s["hy3"], p + 1)
                pe.wait_ge(s["poolT_done"], NT * (p + 1) + 1)
                pe.wait_ge(s["yaT_done"], NT * (p + 1) + 1)
                pe.wait_ge(s["nd_ready"], NT * (p + 1) + 1)
                pe.wait_ge(s["CT_ready"], NT * (p + 1) + 1)
                for t in range(NT):
                    for h in range(CH):
                        last = tr(ps[:, t, h * P:(h + 1) * P], z[:, t, CQ0 + h * P:CQ0 + (h + 1) * P], ident)
                    last.then_inc(s["hyT_tr"], 1)
                if p == PASSES - 1:
                    for h in range(CH):
                        last = tr(ps[:, 4, h * P:(h + 1) * P], CT[:, h, 0:CD], ident)
                    last.then_inc(s["state_out_tr"], 1)
                pe.wait_ge(s["ycT_done"], NT * (p + 1))
                if p == PASSES - 1:
                    pe.wait_ge(s["state_out_sb"], 1)

            def merge(p):
                rows_, tiles = tokens(p)
                tok = rows_ * tiles
                with pe.Fori(0, KC // 2) as i:
                    for k in range(6):
                        b = k % 3
                        n = p * UNITS + NZ + k
                        pe.wait_ge(w_in[k % 2], 16 * (n // 2 + 1) + 48 * i)
                        pe.wait_ge(s["gated"], 3 * KC * p + k + 1 + 6 * i)
                        wv = wbuf[:, k % 2, 0:12 * P].rearrange("p (c n) -> p c n", c=12)
                        for c in range(KC):
                            last = mm(ps[:, 2 * b, 0:tok], wv[:, c, :], xT[:, c, 0:tok], start=(c == 0), stop=(c == KC - 1))
                        last.then_inc(s["gate_mm"], 1)
                        for c in range(4):
                            last = mm(ps[:, 2 * b + 1, 0:tok], wv[:, 8 + c, :], yT[:, 4 * b + c, 0:tok],
                                      start=(c == 0), stop=(c == 3))
                        last.then_inc(s["br_mm"], 1)

            def output(p):
                rows_, tiles = tokens(p)
                pe.wait_ge(s["merged"], KC * (p + 1) + 1)
                with pe.Fori(0, NO // 2) as i:
                    for k in range(2):
                        n = p * UNITS + NZ + 3 * KC + k
                        pe.wait_ge(w_in[k], 16 * (n // 2 + 1) + 16 * i)
                        wv = wbuf[:, k, 0:KC * OC].rearrange("p (c n) -> p c n", c=KC)
                        for t in range(tiles):
                            pe.wait_ge(s["x2_done"], 4 * NO * p + 32 - 2 * tiles + t + 1 + tiles * k + 2 * tiles * i)
                            for c in range(KC):
                                last = mm(ps[0:rows_, 4 * k + t, 0:OC], mT[:, c, t * P:t * P + rows_], wv[:, c, :],
                                          start=(c == 0), stop=(c == KC - 1))
                            last.then_inc(s["o_mm"], 1)
                pe.wait_ge(s["x2_done"], 4 * NO * p + 32 + tiles * NO)

            def find(p):
                rows_, tiles = tokens(p)
                tok = rows_ * tiles
                with pe.Fori(0, PH) as h:
                    for k in range(2):
                        n = p * UNITS + NZ + 3 * KC + NO + k
                        pe.wait_ge(w_in[k], 16 * (n // 2 + 1) + 16 * h)
                        wv = wbuf[:, k, 0:KC * P].rearrange("p (c n) -> p c n", c=KC)
                        pe.wait_ge(s["q_evac"], 2 * PH * p + k + 1 + 2 * h)
                        for c in range(KC):
                            last = mm(ps[:, k, 0:tok], wv[:, c, :], xT[:, c, 0:tok], start=(c == 0), stop=(c == KC - 1))
                        last.then_inc(s["kq_mm"], 1)
                    if p < PASSES:
                        for k in range(2):
                            pe.wait_ge(s["q_evac"], 2 * PH * p + 2 + k + 1 + 2 * h)
                            pe.wait_ge(s["s_evac"], 2 * PH * p + k + 1 + 2 * h)
                            for t in range(NT):
                                last = mm(ps[:, 2 + k, t * P:(t + 1) * P], yT[:, k, t * P:(t + 1) * P], keys[:, k, :],
                                          start=True, stop=True)
                            last.then_inc(s["s_mm"], 1)

            def experts(p):
                with pe.Fori(0, NT) as t:
                    pe.wait_ge(s["y_final"], p * NT + t + 1)
                    for q in range(2):
                        last = mm(ps[:, q, :], ident, xin[:, t, q * 512:(q + 1) * 512], start=True, stop=True)
                    with pe.Fori(0, PH // 2) as i:
                        for j in range(2 * PK):
                            pe.wait_ge(s["diagd"], p * NT * P + j + 1 + P * t + 2 * PK * i)
                            for q in range(2):
                                last = mm(ps[:, q, :], dgs[:, j % 8, :], ring[:, j % RING, D + q * 512:D + (q + 1) * 512],
                                          start=False, stop=False, skip_group_check=True)
                            last.then_inc(s["slot_free"], 1)

            for p in range(PASSES):
                norm(p, 0)
                project(p)
                branches(p)
                merge(p)
                output(p)
                norm(p, 1)
                find(p)
                pe.wait_ge(s["topk_pass"], p + 1)
                experts(p)
            pe.wait_ge(s["y_final"], PASSES * NT + 1)
            p = PASSES
            norm(p, 0)
            project(p)
            pe.wait_ge(s["evac_a"], 2 * NZ * p + 4 + NZ)
            sample_tensor(pe)
            merge(p)
            output(p)
            norm(p, 1)
            find(p)
            sample_experts_tensor(pe)

        @block.scalar
        def _(act):
            f = nc.scalar.activation

            def norm(p, which):
                rows_, tiles = tokens(p)
                if which == 0:
                    act.wait_ge(s["x_in"], 16 * (p + 1))
                    if p:
                        act.wait_ge(s["slot_free"], RING + p * NT * P)
                        act.wait_ge(s["y_final"], p * NT + 1)
                else:
                    act.wait_ge(s["x2_done"], 4 * NO * p + 32 + tiles * NO)
                for t in range(tiles):
                    last = f(arena[0:rows_, t * D:(t + 1) * D],
                             xin[0:rows_, t, :], ACT.Square, accum_out=ssq[0:rows_, t:t + 1])
                last.then_inc(s["ssq"], 1)
                act.wait_ge(s["inv_ready"], 2 * p + which + 1)
                f(rstd[0:rows_, 0:tiles], inv4[0:rows_, 0:tiles], ACT.Sqrt).then_inc(s["rstd_ready"], 1)
                for t in range(tiles):
                    act.wait_ge(s["xs_tr"], norms(p, which, t) + 1)
                    b = 2 * (t % 2)
                    f(xT[:, :, t * P:t * P + rows_].rearrange("p (a c) n -> p a c n", a=2),
                      ps[:, b:b + 2, :].rearrange("p a (c n) -> p a c n", c=4)[:, :, :, 0:rows_], ACT.Copy).then_inc(s["xT_ready"], 1)

            def project(p):
                rows_, tiles = tokens(p)
                mine = tiles_a(p)
                with act.Fori(0, NZ // 2) as i:
                    for k in range(2):
                        for t in range(mine):
                            act.wait_ge(s["z_mm"], NT * NZ * p + k * tiles + t + 1 + 2 * tiles * i)
                            f(z[0:rows_, t, bass.ds(2 * ZC * i + k * ZC, ZC)], ps[0:rows_, 4 * k + t, 0:ZC], ACT.Copy
                              ).then_inc(s["evac_a"], 1)

            def branches(p):
                act.wait_ge(s["inv40"], p + 1)
                f(r40, inv40, ACT.Sqrt).then_inc(s["r40"], 1)
                act.wait_ge(s["evac_a"], 2 * NZ * (p + 1) + 4)
                act.wait_ge(s["evac_v"], 2 * NZ * (p + 1) + 4)
                f(z[:, :, CO0:CO0 + 512], z[:, :, CO0:CO0 + 512], ACT.Sigmoid).then_inc(s["co_sig"], 1)
                act.wait_ge(s["absf"], p + 1)
                f(expf, absf, ACT.Exp, scale=-1.0).then_inc(s["expf"], 1)
                act.wait_ge(s["expf"], p + 1)
                f(lnf, expf, ACT.Ln, bias=1.0).then_inc(s["lnf"], 1)
                act.wait_ge(s["qkn"], p + 1)
                act.wait_ge(s["bias_in"], 16 * (p + 1))
                with act.Fori(0, NT) as t:
                    here, before = p * NT + 2 + t, p * NT + 1 + t
                    act.wait_ge(s["yaT_tr"], before)
                    f(qks, z[:, t, 0:640], ACT.Copy).then_inc(s["qks_ready"], 1)
                    act.wait_ge(s["cq_tr"], before)
                    act.wait_ge(s["pooly_mm"], before)
                    f(pcs, z[:, t, PIN0:PIN0 + 1024], ACT.Copy).then_inc(s["pcs_ready"], 1)
                    act.wait_ge(s["state_mm"], before)
                    f(kcs, z[:, t, CK0:CK0 + 512], ACT.Copy, scale=float(CD) ** -0.5).then_inc(s["kcs_ready"], 1)
                    act.wait_ge(s["qk_tr"], here)
                    act.wait_ge(s["scores_mm"], before)
                    f(qTs, ps[:, 0, :].rearrange("p (j n) -> p j n", j=4), ACT.Copy).then_inc(s["qT_ready"], 1)
                    act.wait_ge(s["pin_tr"], here)
                    act.wait_ge(s["hist_done"], before)
                    f(pinT[:, :, 16:16 + P], ps[:, 2, :].rearrange("p (j n) -> p j n", j=4), ACT.Copy).then_inc(s["pinT_ready"], 1)
                    act.wait_ge(s["ck_tr"], here)
                    act.wait_ge(s["S_mm"], before)
                    f(kcT, ps[:, 5, :], ACT.Copy).then_inc(s["kcT_ready"], 1)
                    act.wait_ge(s["am_ready"], here)
                    f(Am, Am, ACT.Exp).then_inc(s["E_ready"], 1)
                    act.wait_ge(s["args_ready"], here)
                    act.wait_ge(s["CT_ready"], before)
                    f(exps, args, ACT.Exp).then_inc(s["exps_ready"], 1)
                    act.wait_ge(s["L_ready"], here)
                    act.wait_ge(s["arden_ready"], before)
                    f(esink, sinkd, ACT.Exp).then_inc(s["esink_ready"], 1)
                    for h in range(AH):
                        last = f(L[:, h, :], L[:, h, :], ACT.Exp, bias=negmx[:, h:h + 1], accum_out=rsum[:, h:h + 1])
                    last.then_inc(s["P_exp"], 1)
                    act.wait_ge(s["PT_tr"], here)
                    act.wait_ge(s["PV_mm"], before)
                    f(PT[:, 0:8, :], ps[:, 0:2, :].rearrange("p b (i n) -> p (b i) n", i=4), ACT.Copy).then_inc(s["PTa_ready"], 1)
                    act.wait_ge(s["yaT_tr"], here)
                    f(yT[:, 0:4, bass.ds(P * t, P)], ps[:, 1, :].rearrange("p (j n) -> p j n", j=4), ACT.Copy).then_inc(s["yaT_done"], 1)
                act.wait_ge(s["hinv"], p + 1)
                f(hr, hinv, ACT.Sqrt).then_inc(s["hr16"], 1)
                act.wait_ge(s["intra_mm"], NT * (p + 1) + 1)
                for t in range(NT):
                    act.wait_ge(s["hyT_tr"], NT * p + t + 1)
                    f(yT[:, 8:12, t * P:(t + 1) * P], ps[:, t, :].rearrange("p (j n) -> p j n", j=4), ACT.Copy).then_inc(s["ycT_done"], 1)
                if p == PASSES - 1:
                    act.wait_ge(s["state_out_tr"], 1)
                    f(T[:, 0:512], ps[:, 4, :], ACT.Copy).then_inc(s["state_out_sb"], 1)

            def merge(p):
                rows_, tiles = tokens(p)
                tok = rows_ * tiles
                with act.Fori(0, KC // 2) as i:
                    for k in range(6):
                        b = k % 3
                        act.wait_ge(s["gate_mm"], 3 * KC * p + k + 1 + 6 * i)
                        act.wait_ge(s["merged"], KC * p + k // 3 + 1 + 2 * i)
                        f(sgs[:, b, 0:tok], ps[:, 2 * b, 0:tok], ACT.Sigmoid).then_inc(s["sig_done"], 1)

            def find(p):
                rows_, tiles = tokens(p)
                tok = rows_ * tiles
                with act.Fori(0, PH) as h:
                    for k in range(2):
                        act.wait_ge(s["kq_mm"], 2 * PH * p + k + 1 + 2 * h)
                        if p < PASSES:
                            act.wait_ge(s["s_mm"], 2 * PH * p + k + 1 + 2 * h)
                            f(yT[:, k, :], ps[:, k, :], ACT.Copy).then_inc(s["q_evac"], 1)
                        else:
                            f(qTsmp[:, k, bass.ds(NS * h, NS)], ps[:, k, 0:tok], ACT.Copy).then_inc(s["q_evac"], 1)
                    if p < PASSES:
                        act.wait_ge(s["idx1"], PH * p + 1 + h)
                        for k in range(2):
                            act.wait_ge(s["s_mm"], 2 * PH * p + k + 3 + 2 * h)
                            f(ssb[:, k, :, :], ps[:, 2 + k, :].rearrange("p (t n) -> p t n", t=NT), ACT.Copy).then_inc(s["s_evac"], 1)
                        act.wait_ge(s["esub"], PH * p + 1 + h)
                        f(ew, ew, ACT.Exp).then_inc(s["eexp"], 1)

            def experts(p):
                with act.Fori(0, NT) as t:
                    act.wait_ge(s["dotted"], p * NT * P + P * t + 1)
                    f(xcur, xs[:, t, :], ACT.Copy).then_inc(s["cur_ready"], 1)
                    with act.Fori(0, PH // 2) as i:
                        for j in range(PK):
                            act.wait_ge(s["dotted"], p * NT * P + 2 * j + 3 + P * t + 2 * PK * i)
                            k = 2 * j % 8
                            f(gel[:, k:k + 2], dots[:, k:k + 2], ACT.Gelu).then_inc(s["gelud"], 1)

            for p in range(PASSES):
                norm(p, 0)
                project(p)
                branches(p)
                merge(p)
                norm(p, 1)
                find(p)
                act.wait_ge(s["topk_pass"], p + 1)
                experts(p)
            p = PASSES
            norm(p, 0)
            project(p)
            sample_scalar(act)
            merge(p)
            norm(p, 1)
            find(p)
            sample_experts_scalar(act)

        @block.vector
        def _(dve):
            v = nc.vector
            dve.memset(T[0:33, 512:520], NEG).then_inc(s["init_v"], 1)
            dve.memset(ones[:, :], 1.0)
            dve.memset(CT[:, :, :], 0.0)
            dve.memset(pmask[:, 1:NT], 0.0)
            dve.memset(pmask[:, 0:1], NEG)
            dve.memset(mprev[:, :], 0.0).then_inc(s["init_v"], 1)
            dve.wait_ge(s["init_v"], 2)
            dve.wait_ge(s["setup"], 16 * 7)
            dve.wait_ge(s["buck_mm"], 1)
            v.tensor_copy(T[0:AH, 1024:1408], ps[0:AH, 0, 0:384]).then_inc(s["buck_sb"], 1)

            def norm(p, which):
                rows_, tiles = tokens(p)
                n = 2 * p + which + 1
                dve.wait_ge(s["ssq"], n)
                v.tensor_scalar(ms4[0:rows_, 0:tiles], ssq[0:rows_, 0:tiles], 1.0 / D, EPS, ALU.mult, ALU.add).then_inc(s["ms_ready"], 1)
                dve.wait_ge(s["ms_ready"], n)
                v.reciprocal(inv4[0:rows_, 0:tiles], ms4[0:rows_, 0:tiles]).then_inc(s["inv_ready"], 1)
                dve.wait_ge(s["rstd_ready"], n)
                dve.wait_ge(s["g_in"], 16 * n)
                for t in range(tiles):
                    v.scalar_tensor_tensor(xs[0:rows_, t, :], xin[0:rows_, t, :], rstd[0:rows_, t:t + 1], grow[0:rows_, :],
                                           ALU.mult, ALU.mult).then_inc(s["xs_ready"], 1)

            def project(p):
                with dve.Fori(0, NZ // 2) as i:
                    for k in range(2):
                        for t in range(2, NT):
                            dve.wait_ge(s["z_mm"], NT * NZ * p + k * NT + t + 1 + 2 * NT * i)
                            v.tensor_copy(z[:, t, bass.ds(2 * ZC * i + k * ZC, ZC)], ps[:, 4 * k + t, 0:ZC]).then_inc(s["evac_v"], 1)

            def branches(p):
                n = p + 1
                dve.wait_ge(s["evac_a"], 2 * NZ * n + 4)
                dve.wait_ge(s["evac_v"], 2 * NZ * n + 4)
                sq = R[:, 0:NT * 640].rearrange("p (t n) -> p t n", t=NT)
                v.tensor_tensor(sq, z[:, :, 0:640], z[:, :, 0:640], ALU.mult).then_inc(s["stats_v"], stats.step("sq_ready"))
                dve.wait_ge(s["stats_v"], stats.at("sq_ready", p))
                v.tensor_reduce(ss40, sq.rearrange("p t (h d) -> p (t h) d", d=AD), AX.X, ALU.add).then_inc(s["stats_v"], stats.step("ss_ready"))
                dve.wait_ge(s["stats_v"], stats.at("ss_ready", p))
                v.tensor_scalar(ms40, ss40, 1.0 / AD, EPS, ALU.mult, ALU.add).then_inc(s["stats_v"], stats.step("ms40"))
                dve.wait_ge(s["stats_v"], stats.at("ms40", p))
                v.reciprocal(inv40, ms40).then_inc(s["inv40"], 1)
                g4 = gts.rearrange("p (t n) -> p t n", t=NT)
                v.tensor_tensor(g4, z[:, :, G0:G0 + 8], row[:, R_GB:R_GB + 8].unsqueeze(1).broadcast_to([P, NT, 8]), ALU.add
                                ).then_inc(s["stats_v"], stats.step("gates_in"))
                dve.wait_ge(s["stats_v"], stats.at("gates_in", p))
                v.scalar_tensor_tensor(absf.rearrange("p (t n) -> p t n", t=NT), g4[:, :, CH:2 * CH], -1.0, g4[:, :, CH:2 * CH], ALU.mult, ALU.max).then_inc(s["absf"], 1)
                v.tensor_scalar(minf.rearrange("p (t n) -> p t n", t=NT), g4[:, :, CH:2 * CH], 0.0, None, ALU.min).then_inc(s["stats_v"], stats.step("minf"))
                v.memset(z[:, :, CV0:CV0 + CH * CD1].rearrange("p t (h d) -> p t h d", h=CH)[:, :, :, CD:CD1], 1.0).then_inc(s["ones_set"], 1)
                dve.wait_ge(s["r40"], n)
                zq = z[:, :, 0:640].rearrange("p t (h d) -> p t h d", d=AD)
                for t in range(NT):
                    last = v.tensor_tensor(zq[:, t], zq[:, t], r40[:, 10 * t:10 * t + 10].unsqueeze(2).broadcast_to([P, 10, AD]), ALU.mult)
                last.then_inc(s["stats_v"], stats.step("qk_scaled"))
                dve.wait_ge(s["stats_v"], stats.at("qk_scaled", p))
                v.tensor_tensor(z[:, :, 0:640], z[:, :, 0:640], row[:, R_QK:R_QK + 640].unsqueeze(1).broadcast_to([P, NT, 640]), ALU.mult
                                ).then_inc(s["qkn"], 1)
                dve.wait_ge(s["stats_v"], stats.at("minf", p))
                dve.wait_ge(s["lnf"], n)
                v.tensor_tensor(lf, minf, lnf, ALU.subtract).then_inc(s["lf_ready"], 1)
                dve.wait_ge(s["bias_in"], 16 * n)
                ident4 = ident.unsqueeze(1).broadcast_to([P, CH, P])
                with dve.Fori(0, NT) as t:
                    here, before = p * NT + 2 + t, p * NT + 1 + t
                    dve.wait_ge(s["qk_tr"], here)
                    dve.wait_ge(s["kT_shift"], before)
                    v.tensor_copy(kTr[:, P:2 * P], ps[:, 1, 0:P]).then_inc(s["kT_ready"], 1)
                    dve.wait_ge(s["cq_tr"], here)
                    dve.wait_ge(s["inter_mm"], before)
                    v.tensor_copy(qcT, ps[:, 4, :]).then_inc(s["qcT_ready"], 1)
                    dve.wait_ge(s["cs_mm"], here)
                    dve.wait_ge(s["bcast_mm"], before)
                    v.tensor_copy(bM[:, 0:CH], ps[:, 7, 0:CH]).then_inc(s["tile_v"], tile.step("b_ready"))
                    dve.wait_ge(s["tile_v"], tile.at("b_ready", p * NT + 1) + tile.n * t)
                    v.tensor_tensor(asb, gts[:, bass.ds(8 * t, CH)], bM[:, 0:CH], ALU.subtract).then_inc(s["tile_v"], tile.step("a_ready"))
                    dve.wait_ge(s["tile_v"], tile.at("a_ready", p * NT + 1) + tile.n * t)
                    dve.wait_ge(s["tile_v"], tile.at("h_ready", p * NT) + tile.n * t)
                    v.tensor_tensor(tmpi[:, 0:512].rearrange("p (h n) -> p h n", h=CH), ident4, asb.unsqueeze(2).broadcast_to([P, CH, P]),
                                    ALU.mult).then_inc(s["diag_ready"], 1)
                    Am4 = Am.rearrange("p (h n) -> p h n", h=CH)
                    dve.wait_ge(s["arow_mm"], here)
                    dve.wait_ge(s["ST_tr"], before)
                    v.tensor_tensor(Am4, ps[:, 6, :].rearrange("p (h n) -> p h n", h=CH), cmask.unsqueeze(1).broadcast_to([P, CH, P]),
                                    ALU.add).then_inc(s["am0_ready"], 1)
                    dve.wait_ge(s["am0_ready"], here)
                    v.tensor_reduce(rmax, Am4, AX.X, ALU.max).then_inc(s["tile_v"], tile.step("rmax_ready"))
                    dve.wait_ge(s["tile_v"], tile.at("rmax_ready", p * NT + 1) + tile.n * t)
                    dve.wait_ge(s["tile_v"], tile.at("m_new", p * NT) + tile.n * t)
                    v.tensor_tensor(bM[:, CH:2 * CH], rmax, mprev[:, :], ALU.max).then_inc(s["M_ready"], 1)
                    dve.wait_ge(s["M_ready"], here)
                    v.tensor_tensor(Am4, Am4, bM[:, CH:2 * CH].unsqueeze(2).broadcast_to([P, CH, P]), ALU.subtract).then_inc(s["am_ready"], 1)
                    dve.wait_ge(s["exps_ready"], before)
                    v.tensor_tensor(args[:, 0:4], mprev[:, :], bM[:, CH:2 * CH], ALU.subtract)
                    v.scalar_tensor_tensor(args[:, 4:8], bM[:, 0:CH], -1.0, bM[:, CH:2 * CH], ALU.mult, ALU.subtract)
                    dve.wait_ge(s["bcast_mm"], here)
                    v.tensor_copy(bml, ps[:, 7, 0:8]).then_inc(s["bml_ready"], 1)
                    dve.wait_ge(s["bml_ready"], here)
                    v.tensor_tensor(args[:, 8:12], mprev[:, :], bml[:, 4:8], ALU.subtract)
                    v.tensor_tensor(args[:, 12:16], asb, bml[:, 4:8], ALU.subtract).then_inc(s["args_ready"], 1)
                    dve.wait_ge(s["args_ready"], here)
                    v.tensor_tensor(mprev[:, :], bml[:, 0:4], bml[:, 4:8], ALU.add).then_inc(s["tile_v"], tile.step("m_new"))
                    dve.wait_ge(s["scores_mm"], here)
                    dve.wait_ge(s["PT_tr"], before)
                    v.scalar_tensor_tensor(R[:, 0:2048], psf[:, 0:2048], float(AD) ** -0.5, bias, ALU.mult, ALU.add).then_inc(s["tile_v"], 1 if p == 0 else 2)
                    dve.wait_ge(s["tile_v"], tile.at("L0_ready", p * NT + 1) + tile.n * t)
                    if p == 0:
                        v.tensor_scalar(L[:, :, 0:P], L[:, :, 0:P], pmask[:, bass.ds(t, 1)], None, ALU.add).then_inc(s["tile_v"], tile.step("L1_ready"))
                        dve.wait_ge(s["tile_v"], tile.at("L1_ready", p * NT + 1) + tile.n * t)
                    v.tensor_reduce(mx8, L, AX.X, ALU.max).then_inc(s["tile_v"], tile.step("mx_ready"))
                    dve.wait_ge(s["tile_v"], tile.at("mx_ready", p * NT + 1) + tile.n * t)
                    v.tensor_tensor(mxs, mx8, row[:, R_SINK:R_SINK + 8], ALU.max).then_inc(s["tile_v"], tile.step("mx2_ready"))
                    dve.wait_ge(s["tile_v"], tile.at("mx2_ready", p * NT + 1) + tile.n * t)
                    dve.wait_ge(s["P_exp"], before)
                    v.tensor_scalar(negmx, mxs, -1.0, None, ALU.mult)
                    v.tensor_tensor(sinkd, row[:, R_SINK:R_SINK + 8], mxs, ALU.subtract).then_inc(s["L_ready"], 1)
                    dve.wait_ge(s["S_mm"], here)
                    dve.wait_ge(s["E_ready"], here)
                    v.tensor_tensor(Am, ps[:, 4, :], Am, ALU.mult).then_inc(s["Sm_ready"], 1)
                    dve.wait_ge(s["exps_ready"], here)
                    dve.wait_ge(s["ck_tr"], here)
                    kc4 = kcs.rearrange("p (h n) -> p h n", h=CH)
                    v.tensor_tensor(kc4, kc4, exps[:, 12:16].unsqueeze(2).broadcast_to([P, CH, P]), ALU.mult).then_inc(s["wk_ready"], 1)
                    dve.wait_ge(s["inter_mm"], here)
                    tmp4 = tmpi.rearrange("p (a h n) -> p a h n", a=2, h=2)
                    num56 = ps[:, 5:7, 0:2 * CD1].rearrange("p a (h n) -> p a h n", h=2)
                    v.tensor_tensor(tmp4, num56, exps[:, 0:4].rearrange("p (a h) -> p a h", a=2).unsqueeze(3).broadcast_to([P, 2, 2, CD1]),
                                    ALU.mult).then_inc(s["interw_ready"], 1)
                    dve.wait_ge(s["ST_tr"], here)
                    dve.wait_ge(s["intra_mm"], before)
                    v.tensor_copy(STs, ps[:, 4, :]).then_inc(s["ST_ready"], 1)
                    dve.wait_ge(s["intra_mm"], here)
                    dve.wait_ge(s["interw_ready"], here)
                    v.tensor_tensor(tmp4, num56, tmp4, ALU.add).then_inc(s["nd_ready"], 1)
                    dve.wait_ge(s["nd_ready"], here)
                    nd = tmpi.rearrange("p (h n) -> p h n", h=CH)
                    v.scalar_tensor_tensor(dn.unsqueeze(2), nd[:, :, CD:CD1], -1.0, nd[:, :, CD:CD1], ALU.mult, ALU.max
                                           ).then_inc(s["tile_v"], tile.step("den_abs"))
                    dve.wait_ge(s["tile_v"], tile.at("den_abs", p * NT + 1) + tile.n * t)
                    v.tensor_tensor(dn, dn, exps[:, 4:8], ALU.max).then_inc(s["tile_v"], tile.step("den_ready"))
                    dve.wait_ge(s["tile_v"], tile.at("den_ready", p * NT + 1) + tile.n * t)
                    v.reciprocal(rd, dn).then_inc(s["tile_v"], tile.step("h_done"))
                    dve.wait_ge(s["tile_v"], tile.at("h_done", p * NT + 1) + tile.n * t)
                    v.tensor_tensor(z[:, t, CQ0:CQ0 + 512].rearrange("p (h n) -> p h n", h=CH), nd[:, :, 0:CD],
                                    rd.unsqueeze(2).broadcast_to([P, CH, CD]), ALU.mult).then_inc(s["tile_v"], tile.step("h_ready"))
                    dve.wait_ge(s["state_mm"], here)
                    for h in range(CH):
                        last = v.scalar_tensor_tensor(CT[:, h, :], CT[:, h, :], exps[:, 8 + h:9 + h],
                                                      ps[:, 4 + 3 * (h // 2), (h % 2) * CD1:(h % 2 + 1) * CD1], ALU.mult, ALU.add)
                    last.then_inc(s["CT_ready"], 1)
                    dve.wait_ge(s["PT_tr"], here)
                    dve.wait_ge(s["PV_mm"], before)
                    v.tensor_copy(R[:, 3072:4096], psf[:, 1024:2048]).then_inc(s["PTd_ready"], 1)
                    dve.wait_ge(s["P_exp"], here)
                    v.tensor_tensor(aden, rsum, esink, ALU.add).then_inc(s["tile_v"], tile.step("aden_ready"))
                    dve.wait_ge(s["tile_v"], tile.at("aden_ready", p * NT + 1) + tile.n * t)
                    v.reciprocal(arden, aden).then_inc(s["arden_ready"], 1)
                    dve.wait_ge(s["arden_ready"], here)
                    dve.wait_ge(s["PV_mm"], here)
                    v.tensor_tensor(qks[:, 0:512].rearrange("p (j k n) -> p k j n", k=AKV, n=AD),
                                    ps[:, 0, :].rearrange("p (j k n) -> p k j n", k=AKV, n=AD),
                                    arden.rearrange("p (k j) -> p k j", k=AKV).unsqueeze(3).broadcast_to([P, AKV, AG, AD]), ALU.mult).then_inc(s["ya_ready"], 1)
                    dve.wait_ge(s["pooly_mm"], here)
                    v.tensor_tensor(yT[:, 4:8, bass.ds(P * t, P)], ps[:, 2, :].rearrange("p (h n) -> p h n", h=4),
                                    col[:, 0:4].unsqueeze(2).broadcast_to([P, 4, P]), ALU.mult).then_inc(s["poolT_done"], 1)
                hz = z[:, :, CQ0:CQ0 + 512]
                dve.wait_ge(s["tile_v"], tile.at("h_ready", NT * n))
                dve.wait_ge(s["PV_mm"], NT * n + 1)
                hs = R[:, 0:2048].rearrange("p (t n) -> p t n", t=NT)
                v.tensor_tensor(hs, hz, hz, ALU.mult).then_inc(s["stats_v"], stats.step("hsq"))
                dve.wait_ge(s["stats_v"], stats.at("hsq", p))
                v.tensor_reduce(hss, hs.rearrange("p t (h d) -> p (t h) d", d=CD), AX.X, ALU.add).then_inc(s["stats_v"], stats.step("hss"))
                dve.wait_ge(s["stats_v"], stats.at("hss", p))
                v.tensor_scalar(hms, hss, 1.0 / CD, EPS, ALU.mult, ALU.add).then_inc(s["stats_v"], stats.step("hms"))
                dve.wait_ge(s["stats_v"], stats.at("hms", p))
                v.reciprocal(hinv, hms).then_inc(s["hinv"], 1)
                dve.wait_ge(s["co_sig"], n)
                v.tensor_tensor(hz, hz, z[:, :, CO0:CO0 + 512], ALU.mult).then_inc(s["stats_v"], stats.step("hy1"))
                dve.wait_ge(s["stats_v"], stats.at("hy1", p))
                hz4 = hz.rearrange("p t (h d) -> p t h d", h=CH)
                for t in range(NT):
                    last = v.tensor_tensor(hz4[:, t], hz4[:, t], row[:, R_HN:R_HN + CD].unsqueeze(1).broadcast_to([P, CH, CD]), ALU.mult)
                last.then_inc(s["stats_v"], stats.step("hy2"))
                dve.wait_ge(s["stats_v"], stats.at("hy2", p))
                dve.wait_ge(s["hr16"], n)
                for t in range(NT):
                    last = v.tensor_tensor(hz4[:, t], hz4[:, t], hr[:, CH * t:CH * t + CH].unsqueeze(2).broadcast_to([P, CH, CD]), ALU.mult)
                last.then_inc(s["hy3"], 1)

            def merge(p):
                rows_, tiles = tokens(p)
                tok = rows_ * tiles
                if p < PASSES:
                    dve.wait_ge(s["ycT_done"], NT * (p + 1))
                if p == PASSES - 1:
                    dve.wait_ge(s["state_stored"], 16)
                with dve.Fori(0, KC // 2) as i:
                    for k in range(6):
                        b = k % 3
                        n = 3 * KC * p + k
                        dve.wait_ge(s["sig_done"], n + 1 + 6 * i)
                        dve.wait_ge(s["br_mm"], n + 1 + 6 * i)
                        v.tensor_tensor(sgs[:, b, 0:tok], sgs[:, b, 0:tok], ps[:, 2 * b + 1, 0:tok], ALU.mult).then_inc(s["gated"], 1)
                        if b == 0:
                            continue
                        dve.wait_ge(s["gated"], n + 4 + 6 * i)
                        if b == 1:
                            v.tensor_tensor(pr[:, 0:tok], sgs[:, 0, 0:tok], sgs[:, 1, 0:tok], ALU.add).then_inc(s["prod"], 1)
                        else:
                            dve.wait_ge(s["prod"], KC * p + k // 3 + 1 + 2 * i)
                            v.tensor_tensor(mT[:, bass.ds(2 * i + k // 3, 1), 0:tok].rearrange("p a n -> p (a n)"), pr[:, 0:tok], sgs[:, 2, 0:tok], ALU.add
                                            ).then_inc(s["merged"], 1)

            def output(p):
                rows_, tiles = tokens(p)
                with dve.Fori(0, NO // 2) as i:
                    for k in range(2):
                        for t in range(tiles):
                            dve.wait_ge(s["o_mm"], NT * NO * p + k * tiles + t + 1 + 2 * tiles * i)
                            o = xin[0:rows_, t, bass.ds(2 * OC * i + k * OC, OC)]
                            v.tensor_tensor(o, o, ps[0:rows_, 4 * k + t, 0:OC], ALU.add).then_inc(s["x2_done"], 1)

            def topk(n, side_in, side_rep, rows_, tiles, write):
                pairs = [(k, t) for k in range(2) for t in range(tiles)]
                vv = v16[0:rows_, 0:2 * tiles * 16].rearrange("p (k t n) -> p k t n", k=2, t=tiles)
                ii = i16[0:rows_, 0:2 * tiles * 16].rearrange("p (k t n) -> p k t n", k=2, t=tiles)
                fi = f16[0:rows_, 0:2 * tiles * 16].rearrange("p (k t n) -> p k t n", k=2, t=tiles)
                for k, t in pairs:
                    last = v.max(vv[:, k, t, 0:8], side_in[0:rows_, k, t, :])
                last.then_inc(s["topk_v"], find_steps.step("top1"))
                hold(dve, s["topk_v"], find_steps.at("top1", n - 1))
                for k, t in pairs:
                    last = v.match_replace(side_rep[0:rows_, k, t, :], vv[:, k, t, 0:8], side_in[0:rows_, k, t, :], LOWEST)
                last.then_inc(s["topk_v"], find_steps.step("rep1"))
                for k, t in pairs:
                    last = v.max_index(ii[:, k, t, 0:8], vv[:, k, t, 0:8], side_in[0:rows_, k, t, :])
                last.then_inc(s["idx1"], 1)
                hold(dve, s["topk_v"], find_steps.at("rep1", n - 1))
                for k, t in pairs:
                    last = v.max(vv[:, k, t, 8:16], side_rep[0:rows_, k, t, :])
                last.then_inc(s["topk_v"], find_steps.step("top2"))
                hold(dve, s["topk_v"], find_steps.at("top2", n - 1))
                for k, t in pairs:
                    last = v.max_index(ii[:, k, t, 8:16], vv[:, k, t, 8:16], side_rep[0:rows_, k, t, :])
                last.then_inc(s["topk_v"], find_steps.step("idx2"))
                cd = cand[0:rows_, 0:tiles * 256].rearrange("p (t n) -> p t n", t=tiles)
                cr = crep[0:rows_, 0:tiles * 256].rearrange("p (t n) -> p t n", t=tiles)
                for t in range(tiles):
                    last = v.tensor_tensor(cd[:, t].rearrange("p (a b) -> p a b", a=16), vv[:, 0, t].unsqueeze(2).broadcast_to([rows_, 16, 16]),
                                           vv[:, 1, t].unsqueeze(1).broadcast_to([rows_, 16, 16]), ALU.add)
                last.then_inc(s["topk_v"], find_steps.step("cand"))
                dve.wait_ge(s["topk_v"], find_steps.at("idx2", n - 1))
                v.tensor_copy(fi, ii).then_inc(s["topk_v"], find_steps.step("idxf"))
                tv = v16[0:rows_, 128:128 + tiles * 16].rearrange("p (t n) -> p t n", t=tiles)
                tp = i16[0:rows_, 128:128 + tiles * 16].rearrange("p (t n) -> p t n", t=tiles)
                hold(dve, s["topk_v"], find_steps.at("cand", n - 1))
                for t in range(tiles):
                    last = v.max(tv[:, t, 0:8], cd[:, t])
                last.then_inc(s["topk_v"], find_steps.step("ctop1"))
                hold(dve, s["topk_v"], find_steps.at("ctop1", n - 1))
                for t in range(tiles):
                    last = v.match_replace(cr[:, t], tv[:, t, 0:8], cd[:, t], LOWEST)
                last.then_inc(s["topk_v"], find_steps.step("crep"))
                for t in range(tiles):
                    last = v.max_index(tp[:, t, 0:8], tv[:, t, 0:8], cd[:, t])
                last.then_inc(s["topk_v"], find_steps.step("cidx1"))
                hold(dve, s["topk_v"], find_steps.at("crep", n - 1))
                for t in range(tiles):
                    last = v.max(tv[:, t, 8:16], cr[:, t])
                last.then_inc(s["topk_v"], find_steps.step("ctop2"))
                hold(dve, s["topk_v"], find_steps.at("ctop2", n - 1))
                for t in range(tiles):
                    last = v.max_index(tp[:, t, 8:16], tv[:, t, 8:16], cr[:, t])
                last.then_inc(s["topk_v"], find_steps.step("cidx2"))
                e = ew[0:rows_, 0:tiles * 16].rearrange("p (t n) -> p t n", t=tiles)
                v.tensor_tensor(e, tv, tv[:, :, 0:1].broadcast_to([rows_, tiles, 16]), ALU.subtract).then_inc(s["esub"], 1)
                m = tiles * 16
                tpf = i16[0:rows_, 128:128 + m]
                dve.wait_ge(s["topk_v"], find_steps.at("cidx2", n - 1))
                v.tensor_scalar(pab[0:rows_, 0, 0:m], tpf, 4, None, ALU.logical_shift_right)
                v.tensor_scalar(pab[0:rows_, 1, 0:m], tpf, 15, None, ALU.bitwise_and).then_inc(s["topk_v"], find_steps.step("pos_ab"))
                dve.wait_ge(s["topk_v"], find_steps.at("pos_ab", n - 1))
                v.tensor_copy(pabf[0:rows_, :, 0:m], pab[0:rows_, :, 0:m]).then_inc(s["topk_v"], find_steps.step("pos_f"))
                dve.wait_ge(s["topk_v"], find_steps.at("pos_f", n - 1))
                dve.wait_ge(s["topk_v"], find_steps.at("idxf", n - 1))
                eqs = [cand, crep]
                for k in range(2):
                    eq = eqs[k][0:rows_, 0:m * 16].rearrange("p (m a) -> p m a", a=16)
                    last = v.tensor_tensor(eq, pabf[0:rows_, k, 0:m].unsqueeze(2).broadcast_to([rows_, m, 16]),
                                           iota16[0:rows_].unsqueeze(1).broadcast_to([rows_, m, 16]), ALU.is_equal)
                last.then_inc(s["topk_v"], find_steps.step("eq_a"))
                dve.wait_ge(s["topk_v"], find_steps.at("eq_a", n - 1))
                for k in range(2):
                    for t in range(tiles):
                        eq = eqs[k][0:rows_, t * 256:(t + 1) * 256].rearrange("p (m a) -> p m a", a=16)
                        last = v.tensor_tensor(eq, eq, fi[:, k, t].unsqueeze(1).broadcast_to([rows_, 16, 16]), ALU.mult)
                last.then_inc(s["topk_v"], find_steps.step("eq_ab"))
                dve.wait_ge(s["topk_v"], find_steps.at("eq_ab", n - 1))
                for k in range(2):
                    eq = eqs[k][0:rows_, 0:m * 16].rearrange("p (m a) -> p m a", a=16)
                    last = v.tensor_reduce(eab[0:rows_, k, 0:m], eq, AX.X, ALU.add)
                last.then_inc(s["topk_v"], find_steps.step("e_a"))
                dve.wait_ge(s["topk_v"], find_steps.at("e_a", n - 1))
                v.scalar_tensor_tensor(eab[0:rows_, 2, 0:m], eab[0:rows_, 0, 0:m], float(NKEY), eab[0:rows_, 1, 0:m],
                                       ALU.mult, ALU.add).then_inc(s["topk_v"], find_steps.step("e_ab"))
                dve.wait_ge(s["eexp"], n)
                v.tensor_reduce(esm[0:rows_, 0:tiles], e, AX.X, ALU.add).then_inc(s["topk_v"], find_steps.step("esum"))
                dve.wait_ge(s["topk_v"], find_steps.at("esum", n - 1))
                v.reciprocal(esr[0:rows_, 0:tiles], esm[0:rows_, 0:tiles]).then_inc(s["topk_v"], find_steps.step("erec"))
                dve.wait_ge(s["topk_v"], find_steps.at("e_ab", n - 1))
                dve.wait_ge(s["topk_v"], find_steps.at("erec", n - 1))
                write(e, eab[0:rows_, 2, 0:m].rearrange("p (t n) -> p t n", t=tiles))

            def find(p):
                with dve.Fori(0, PH) as h:
                    dve.wait_ge(s["gate_ready"], PH * p + 1 + h)
                    hold(dve, s["s_evac"], 2 * PH * p + 4 + 2 * h)

                    def write(e, experts_f):
                        v.tensor_copy(eidx[:, :, bass.ds(PK * h, PK)], experts_f)
                        v.tensor_tensor(gates[:, :, bass.ds(PK * h, PK)], e, esr[:, 0:NT].unsqueeze(2).broadcast_to([P, NT, PK]), ALU.mult
                                        ).then_inc(s["gate_ready"], 1)
                    topk(PH * p + 1 + h, ssb, srep, P, NT, write)
                dve.wait_ge(s["gate_ready"], PH * (p + 1) + 1)
                dve.sem_inc(s["topk_pass"], 1)

            def experts(p):
                with dve.Fori(0, NT) as t:
                    hold(dve, s["cur_ready"], p * NT + t + 1)
                    with dve.Fori(0, PH // 2) as i:
                        for j in range(2 * PK):
                            r = j % RING
                            base = p * NT * P
                            dve.wait_ge(got[r], 16 * (base // RING + j // RING + 1) + 16 * P // RING * t + 64 * i)
                            v.tensor_tensor_reduce(ring[:, r, 0:D], ring[:, r, 0:D], xcur, 1.0, 0.0, ALU.mult, ALU.add,
                                                   dots[:, r:r + 1]).then_inc(s["dotted"], 1)
                            if j % 2 == 1:
                                dve.wait_ge(s["gelud"], base // 2 + j // 2 + 1 + P // 2 * t + PK * i)
                                dve.wait_ge(s["slot_free"], base + j + 1 + P * t + 2 * PK * i)
                                for q in (j - 1, j):
                                    v.tensor_scalar(dgs[:, q % 8, :], ident, gel[:, q % 8:q % 8 + 1],
                                                    gates[:, t, bass.ds(2 * PK * i + q, 1)], ALU.mult, ALU.mult).then_inc(s["diagd"], 1)
                    dve.wait_ge(s["slot_free"], p * NT * P + RING + P + P * t)
                    v.tensor_copy(xin[:, t, :], psf[:, 0:D]).then_inc(s["y_final"], 1)

            for p in range(PASSES):
                norm(p, 0)
                project(p)
                branches(p)
                merge(p)
                output(p)
                norm(p, 1)
                find(p)
                experts(p)
            p = PASSES
            norm(p, 0)
            sample_vector(dve)
            merge(p)
            output(p)
            norm(p, 1)
            sample_experts_vector(dve, topk)

        @block.gpsimd
        def _(pool):
            for n in STEPS:
                pool.sem_inc(s[n], 1)
            for n, k in PRIMED.items():
                pool.sem_inc(s[n], k)
            g = nc.gpsimd
            g.memset(kTr[:, 0:P], 0.0)
            g.memset(vprev[:, :], 0.0)
            g.memset(pinT[:, :, 0:16], 0.0)
            for c, w in enumerate(POOLW):
                last = g.memset(tab[:, c, :], 1.0 / w)
            last.then_inc(s["init_p"], 1)
            pool.wait_ge(s["init_p"], 1)
            pool.wait_ge(s["setup"], 16 * 7)
            g.tensor_copy(tab[:, :, 0:16], cst[:, C_CNT:C_CNT + 64].rearrange("p (c n) -> p c n", c=4)).then_inc(s["init_p"], 1)
            pool.wait_ge(s["init_p"], 2)

            def branches(p):
                with pool.Fori(0, NT) as t:
                    here, before = p * NT + 2 + t, p * NT + 1 + t
                    pool.wait_ge(s["pinT_ready"], here)
                    g.tensor_tensor(pA[:, :, 2:144], pinT[:, :, 2:144], pinT[:, :, 1:143], ALU.add).then_inc(s["pool_p"], pooling.step("sum2"))
                    pool.wait_ge(s["pool_p"], pooling.at("sum2", p * NT) + pooling.n * t)
                    g.tensor_tensor(pB[:, 1:4, 4:144], pA[:, 1:4, 4:144], pA[:, 1:4, 2:142], ALU.add).then_inc(s["pool_p"], pooling.step("sum4"))
                    pool.wait_ge(s["pool_p"], pooling.at("sum4", p * NT) + pooling.n * t)
                    g.tensor_tensor(pA[:, 2:4, 8:144], pB[:, 2:4, 8:144], pB[:, 2:4, 4:140], ALU.add).then_inc(s["pool_p"], pooling.step("sum8"))
                    pool.wait_ge(s["pool_p"], pooling.at("sum8", p * NT) + pooling.n * t)
                    g.tensor_tensor(pB[:, 3:4, 16:144], pA[:, 3:4, 16:144], pA[:, 3:4, 8:136], ALU.add).then_inc(s["pool_p"], pooling.step("sum16"))
                    pool.wait_ge(s["pool_p"], pooling.at("sum16", p * NT) + pooling.n * t)
                    g.tensor_tensor(pA[:, 0:4:2, 16:144], pA[:, 0:4:2, 16:144], tab[:, 0:4:2, :], ALU.mult)
                    g.tensor_tensor(pB[:, 1:4:2, 16:144], pB[:, 1:4:2, 16:144], tab[:, 1:4:2, :], ALU.mult).then_inc(s["pool_p"], pooling.step("scaled"))
                    pool.wait_ge(s["pool_p"], pooling.at("scaled", p * NT) + pooling.n * t)
                    pool.wait_ge(s["pin_tr"], here)
                    po = pcs[:, 0:512].rearrange("p (c n) -> p c n", c=4)
                    g.tensor_tensor(po[:, 0:4:2, :], pA[:, 0:4:2, 16:144], pinT[:, 0:4:2, 16:144], ALU.subtract)
                    g.tensor_tensor(po[:, 1:4:2, :], pB[:, 1:4:2, 16:144], pinT[:, 1:4:2, 16:144], ALU.subtract).then_inc(s["pooled_ready"], 1)
                    hold(pool, s["pooled_ready"], here)
                    g.tensor_copy(tab[:, :, 0:16], tab[:, :, 16:32])
                    g.tensor_copy(pinT[:, :, 1:16], pinT[:, :, 129:144]).then_inc(s["hist_done"], 1)
                    pool.wait_ge(s["hist_done"], here)
                    hold(pool, s["scores_mm"], here)
                    g.tensor_copy(kTr[:, 0:P], kTr[:, P:2 * P]).then_inc(s["kT_shift"], 1)
                    hold(pool, s["PV_mm"], here)
                    g.tensor_copy(vprev[:, :], z[:, t, V0:V0 + P]).then_inc(s["v_shift"], 1)

            def experts(p):
                pool.wait_ge(s["topk_pass"], p + 1)
                with pool.Fori(0, NT) as t:
                    with pool.Fori(0, PH // 2) as i:
                        for b in range(2):
                            g.tensor_copy(islot[:, b * PK:(b + 1) * PK], eidx[:, t, bass.ds(2 * PK * i + b * PK, PK)]).then_inc(s["idx_slot"], 1)
                            pool.wait_ge(s["idx_slot"], p * NT * PH + b + 1 + PH * t + 2 * i)
                            for j in range(PK):
                                q = b * PK + j
                                hold(pool, s["slot_free"], p * NT * P + q + 1 + P * t + 2 * PK * i)
                                g.indirect_dma_start(ring[:, q % RING, :], None, uv,
                                                     bass.IndirectOffsetOnAxis(ap=islot[:, q:q + 1], axis=0)).then_inc(got[q % RING], 16)

            for p in range(PASSES):
                branches(p)
                experts(p)
            sample_gpsimd(pool)


def kernel(x_prompt, x_sample, cache_k, cache_v, state_pool, state_mlstm_c, state_mlstm_n, state_mlstm_m, rel_bias,
           norm1_g, w_in, q_norm_g, k_norm_g, attn_sink, w_pool, pool_scale, b_igate, b_fgate, h_norm_g,
           w_br_a, w_br_b, w_br_c, w_out, norm2_g, peer_wq, peer_k1, peer_k2, peer_u, peer_v):
    import concourse.bacc as bacc
    from concourse.bass_utils import run_bass_kernel_spmd

    a = np.ascontiguousarray
    f = np.float32

    C = np.zeros((P, C_ALL), f)
    r = np.arange(P)
    C[:, C_ID:C_ID + P] = np.eye(P)
    C[:, C_TRI:C_TRI + P] = r[:, None] <= r[None, :]
    C[:, C_MASK:C_MASK + P] = np.where(r[None, :] <= r[:, None], 0.0, NEG)
    C[P - 1, C_LAST:C_LAST + P] = 1.0
    C[:, C_IOTA:C_IOTA + 16] = np.arange(16)
    for c, w in enumerate(POOLW):
        C[:, C_CNT + 16 * c:C_CNT + 16 * (c + 1)] = 1.0 / np.minimum(np.arange(16) + 1, w).astype(f)
    exact = 16
    d = np.arange(W)
    large = exact + (np.log(np.maximum(d, 1).astype(f) / f(exact)) / f(math.log(128 / exact)) * f(32 - exact)).astype(np.int32)
    bucket = np.where(d < exact, d, np.minimum(large, 31))
    for i in range(384):
        dist = 255 - i
        C[bucket[dist] if 0 <= dist < W else 32, C_BUCK + i] = 1.0
    for i in range(W):
        C[bucket[W - 1 - i], C_SBUCK + i] = 1.0
    selmat = np.zeros((64, NS + 64), f)
    for h in range(PH):
        for n in range(NS):
            selmat[h * NS + n, n] = 1.0
            selmat[n, NS + h * NS + n] = 1.0

    perm = np.array([kv * AG + j for j in range(AG) for kv in range(AKV)])
    w1 = np.asarray(w_in)[0]
    pts = np.cumsum([512, 128, 128, 512, 512, 512, 512, 4, 4, 512, 1024, 1024, 1024])
    aq, ak, av, pin, cq, ck, cv, ci, cf, co, ga, gb, gc = np.split(w1, pts[:-1], axis=1)
    aq = aq.reshape(D, AH, AD)[:, perm].reshape(D, 512)
    cv = np.concatenate([cv.reshape(D, CH, CD), np.zeros((D, CH, 1), f)], 2).reshape(D, CH * CD1)
    wz = np.concatenate([aq, ak, av, ci, cf, pin, cq, ck, co, cv], 1)
    wz = np.concatenate([wz, np.zeros((D, ZW - wz.shape[1]), f)], 1)
    wz = a(wz.reshape(KC, P, NZ, ZC).transpose(2, 1, 0, 3)).reshape(NZ, P, KC * ZC)
    bra = np.asarray(w_br_a)[0].reshape(AH, AD, D)[perm].reshape(512, D)
    parts = []
    for gw, bw in ((ga, bra), (gb, np.asarray(w_br_b)[0]), (gc, np.asarray(w_br_c)[0])):
        parts.append(np.concatenate([gw, bw], 0).reshape(12, P, KC, P).transpose(2, 1, 0, 3))
    wm = a(np.stack(parts, 1)).reshape(3 * KC, P, 12 * P)
    wo = a(np.asarray(w_out)[0].reshape(KC, P, NO, OC).transpose(2, 1, 0, 3)).reshape(NO, P, KC * OC)
    wq = a(np.asarray(peer_wq)[0].reshape(KC, P, 2 * PH, P).transpose(2, 1, 0, 3)).reshape(2 * PH, P, KC * P)
    uv = np.concatenate([np.asarray(peer_u)[0], np.asarray(peer_v)[0]], 1)

    rel_bias = np.asarray(rel_bias)
    sink = np.asarray(attn_sink)[0]
    rows = np.concatenate([np.tile(np.asarray(q_norm_g)[0], AH), np.tile(np.asarray(k_norm_g)[0], AKV), np.asarray(h_norm_g)[0],
                           np.asarray(b_igate)[0], np.asarray(b_fgate)[0], sink])[None]
    cols = np.zeros((P, 8), f)
    cols[:, 0:4] = np.asarray(pool_scale)[0].reshape(4, P).T
    cols[:, 4] = np.asarray(h_norm_g)[0]
    sinkcol = np.zeros((64, 4), f)
    sinkcol[:, 0] = np.tile(sink, NS)
    sinkcol[0:32, 1] = np.tile(np.asarray(b_igate)[0], NS)
    sinkcol[0:32, 2] = np.tile(np.asarray(b_fgate)[0], NS)

    arrays = {
        "x_prompt": a(np.asarray(x_prompt).reshape(PASSES, NT, P, D).transpose(0, 2, 1, 3)),
        "x_sample": a(np.asarray(x_sample).reshape(NS, D)),
        "cache_k": a(np.asarray(cache_k).reshape(NS, W, P)), "cache_v": a(np.asarray(cache_v).reshape(NS, W, P)),
        "state_pool": a(np.asarray(state_pool).reshape(NS, HIST, 512)),
        "st_c": a(np.asarray(state_mlstm_c).reshape(NS * CH, CD, CD).transpose(1, 0, 2)), "st_n": a(np.asarray(state_mlstm_n).reshape(NS * CH, CD)),
        "st_m": a(np.asarray(state_mlstm_m).reshape(NS * CH, 1)),
        "rel": rel_bias, "relr": a(np.tile(rel_bias, (1, NS))), "consts": C, "rows": a(rows), "cols": cols,
        "gains": a(np.concatenate([np.asarray(norm1_g), np.asarray(norm2_g)], 0)),
        "keysT": a(np.stack([np.asarray(peer_k1)[0].T, np.asarray(peer_k2)[0].T], 1)),
        "w_pool": a(np.asarray(w_pool)[0].transpose(1, 0, 2)), "sinkcol": sinkcol,
        "w_z": wz, "w_merge": wm, "w_o": wo, "w_q": wq, "uv": a(uv), "selmat": selmat,
    }
    outs = {
        "y_p": (PASSES, P, NT, D), "y_s": (NS, D), "k_p": (P, P), "v_p": (P, P), "pool_p": (HIST, 512), "c_p": (CH, CD, CD),
        "n_p": (CH, CD), "m_p": (1, CH), "k_s": (NS, W, P), "v_s": (NS, W, P), "pool_s": (NS, HIST, 512),
        "c_s": (CD, NS * CH, CD), "n_s": (NS * CH, CD), "m_s": (NS * CH, 1),
    }
    nc = bacc.Bacc("TRN2", target_bir_lowering=False, num_devices=1)
    args = [nc.dram_tensor(n, x.shape, F32, kind="ExternalInput").ap() for n, x in arrays.items()]
    args += [nc.dram_tensor(n, x, F32, kind="ExternalOutput").ap() for n, x in outs.items()]
    build(nc, *args)
    res = run_bass_kernel_spmd(nc, [arrays], core_ids=[0]).results[0]
    o = {n: res[n] for n in outs}
    kv = (1, 1, W, AKV, AD)
    skv = (1, NS, W, AKV, AD)
    return (a(o["y_p"].transpose(0, 2, 1, 3)).reshape(1, SEQ, D), o["y_s"].reshape(NS, 1, D), o["k_p"].reshape(kv), o["v_p"].reshape(kv),
            o["pool_p"].reshape(1, 1, HIST, 512), o["c_p"].reshape(1, 1, CH, CD, CD), o["n_p"].reshape(1, 1, CH, CD),
            o["m_p"].reshape(1, 1, CH), o["k_s"].reshape(skv), o["v_s"].reshape(skv), o["pool_s"].reshape(1, NS, HIST, 512),
            a(o["c_s"].transpose(1, 0, 2)).reshape(1, NS, CH, CD, CD), o["n_s"].reshape(1, NS, CH, CD), o["m_s"].reshape(1, NS, CH))
```

```python
import math
from contextlib import ExitStack

import numpy as np

import concourse.bass as bass
from concourse import mybir

F32, U32, BF16 = mybir.dt.float32, mybir.dt.uint32, mybir.dt.bfloat16
ALU, ACT, AX = mybir.AluOpType, mybir.ActivationFunctionType, mybir.AxisListType

P = 128
D = 1024
KC = D // P
SEQ, NS = 1024, 8
PASSES = 4
TOK = SEQ // PASSES
NT = TOK // P
AH, AKV, AD = 8, 2, 64
AG = AH // AKV
W = 128
POOLW = (2, 4, 8, 16)
HIST = 15
CH, CD = 4, 128
CD1 = CD + 1
PH, PK = 8, 16
NKEY = 128
EPS = 1e-6
NEG = -1e30
LOWEST = -3e38

QK0, V0, G0, PIN0, CQ0, CK0, CO0, CV0 = 0, 640, 768, 776, 1288, 1800, 2312, 2824
ZC = 210
NZ = 16
ZW = ZC * NZ
OC = 128
NO = D // OC
UNITS = NZ + 3 * KC + NO + 2 * PH
RING = 8
BLOCKS = P // RING
BRB = 1
PRB = BLOCKS - BRB * NT
PRG = 8
BSHARE = [(0, 2), (2, 4), (4, 8)]
SHARE = [(0, 2), (2, 6), (6, 8)]

C_ID, C_TRI, C_MASK, C_LAST, C_IOTA, C_CNT, C_BUCK, C_SBUCK = 0, 128, 256, 384, 512, 528, 592, 976
C_KEEP = 592
C_ALL = 1104
R_QK, R_HN, R_GB, R_SINK = 0, 640, 768, 776
R_ALL = 784

STEPS = """qks_ready pcs_ready kcs_ready qT_ready pinT_ready kcT_ready E_ready exps_ready P_exp esink_ready PTa_ready
yaT_done kT_ready qcT_ready diag_ready am0_ready M_ready am_ready bml_ready args_ready L_ready Sm_ready
interw_ready ST_ready wk_ready nd_ready CT_ready PTd_ready arden_ready ya_ready poolT_done kT_shift v_shift
pooled_ready hist_done qk_tr pin_tr cq_tr ck_tr cs_mm arow_mm S_mm scores_a scores_mm bcast_mm inter_mm ST_tr intra_mm
state_mm PTa_tr PT_tr PV_mm pooly_mm yaT_tr""".split()
OTHERS = """setup scratch_w scr_out cur_in res_in gcur_ready ecur_ready bias_in g_in x_in ssq ms_ready inv_ready rstd_ready xs_ready xs_tr xT_ready z_mm ones_set
inv40 r40 qkn absf expf lnf lf_ready co_sig hinv hr16 hy3 hyT_tr ycT_done gate_mm br_mm sig_done prod o_mm
kq_mm esub eexp idx_slot gelud diagd y_out init_v init_p buck_mm buck_sb state_out_tr state_out_sb
outs w_in0 w_in1 state_stored state_c_stored b_n c_load c_load2 c_round0 c_round1 c_scr k_load kscr smp_a smp_p smp_v
stats_v topk_v pool_p""".split()
class Steps:

    def __init__(self, *order):
        self.order, self.n = order, len(order)

    def step(self, name):
        return 1 if name in self.order else 0

    def at(self, name, rounds=0):
        return self.n * rounds + self.order.index(name) + 1


stats = Steps("sq_ready", "ss_ready", "ms40", "gates_in", "minf", "qk_scaled", "hsq", "hss", "hms", "hy1", "hy2",
    "esum", "erec")
tile = Steps("b_ready", "a_ready", "rmax_ready", "m_new", "La_ready", "L0_ready", "L1_ready", "mx_ready", "mx2_ready",
    "den_abs", "den_ready", "h_done", "h_ready", "aden_ready")
find_steps = Steps("top1", "rep1", "top2", "idx2", "cand", "idxf", "ctop1", "crep", "cidx1", "ctop2", "cidx2",
    "pos_ab", "pos_f", "eq_a", "eq_ab", "e_a", "e_ab")
pooling = Steps("sum2", "sum4", "sum8", "sum16", "scaled")
SMP = {"p": Steps("c_tr", "b_xtr", "b_tr", "a_bmm", "a_qtr", "a_ktr", "b_mm", "c_bc", "a_smm", "a_str", "c_hmm",
    "a_ptr", "a_pv", "sample_s", "xb_mm"),
       "a": Steps("m_sig", "c_T", "b_T", "a_kT", "c_e", "c_ln", "c_x", "a_s", "a_es", "a_p", "c_hr", "a_ya", "t_sel",
    "t_xb"),
       "v": Steps("q_sq_ready", "q_ss_ready", "q_ms40", "q_qk_scaled", "b_s1", "b_p", "c_m0", "c_abs", "c_lf0", "c_qk", "c_qk1", "c_nq", "c_nq1", "c_lf", "c_i", "c_mt",
    "c_d", "c_S", "c_den0", "c_den1", "c_denabs", "c_den2", "c_rd", "c_dg", "c_nn1", "c_nn2", "a_qT", "a_b",
    "b_y", "c_bcs", "a_l", "a_m1", "a_m2", "a_m3", "c_u",
    *(f"{step}{r}" for r in range(4) for step in ("c_cq", "c_t1", "c_t2", "c_cqr", "c_cn")), "c_n1", "c_n2", "c_h", "c_h2",
    "a_den", "a_rd", "a_pn", "c_hms", "c_hinv", "a_PT", "c_hy", "c_hy2", "c_y", "t_esum", "t_erec")}


PRIMED = {
    "evac_a": 4, "x2_done": 32, "slot_free": RING, "gated": 3, "merged": 1,
    "q_evac": 2, "s_evac": 2, "s_mm": 2, "idx1": 1, "y_final": 1, "tile_v": tile.n, "dotted": 1, "gate_ready": 1,
}


def build(nc, x_prompt, x_sample, cache_k, cache_v, state_pool, st_c, st_n, st_m, rel, relr, consts, rows, cols,
          gains, keysT, w_pool, sinkcol, w_z, w_merge, w_o, w_q, uv, selmat,
          y_p, y_s, k_p, v_p, pool_p, c_p, n_p, m_p, k_s, v_s, pool_s, c_s, n_s, m_s):
    biasfull = nc.dram_tensor("biasfull", [P, AH * 2 * P], F32).ap()
    scr_qk = nc.dram_tensor("scr_qk", [NS, 2, CH * CD], F32).ap()
    scr_g = nc.dram_tensor("scr_g", [2, NS, CH], F32).ap()
    xs_scr = nc.dram_tensor("xs_scr", [PASSES, P, NT, D], F32).ap()
    x2_scr = nc.dram_tensor("x2_scr", [PASSES, P, NT, D], F32).ap()
    ctx = ExitStack()
    with ctx:
        def sb(name, shape, dt=F32):
            return ctx.enter_context(nc.sbuf_tensor(name, shape, dt))

        names = STEPS + list(PRIMED) + OTHERS + [f"got{i}" for i in range(RING)]
        s = {n: ctx.enter_context(nc.semaphore(n)) for n in names}
        got = [s[f"got{r}"] for r in range(RING)]
        w_in = [s["w_in0"], s["w_in1"]]

        ps = ctx.enter_context(nc.psum_tensor("ps", [P, 8, 512], F32))
        psf = ps[:, :, :].rearrange("p b n -> p (b n)")

        cst = sb("cst", [P, C_KEEP])
        ident = cst[:, C_ID:C_ID + P]
        tri = cst[:, C_TRI:C_TRI + P]
        cmask = cst[:, C_MASK:C_MASK + P]
        last_row = cst[:, C_LAST:C_LAST + P]
        ones = sb("ones", [P, P])
        iota16 = sb("iota16", [P, 16], BF16)
        row = sb("row", [P, R_ALL])
        gates = sb("gates", [P, NT, P])
        eidx = sb("eidx", [P, NT, P], U32)
        ecur = sb("ecur", [P, P], U32)
        gcur = sb("gcur", [P, P])
        islot = sb("islot", [P, 2 * PK], U32)
        dots = sb("dots", [P, RING])
        gel = sb("gel", [P, RING])
        dgs = sb("dgs", [P, RING, P])
        xx = sb("xx", [P, 2 * D])
        xcur, xres = xx[:, 0:D], xx[:, D:2 * D]
        col = sb("col", [P, 8])
        grow = sb("grow", [P, D])
        keys = sb("keys", [P, 2, NKEY])
        wpool = sb("wpool", [P, 4, P])
        pmask = sb("pmask", [P, NT])
        xin = sb("xin", [P, NT, D])
        xT = sb("xT", [P, KC, TOK])
        yT = sb("yT", [P, 12, TOK])
        arena = sb("arena", [P, NT * ZW + 2048 + RING * 2 * D])
        R = sb("R", [P, 4 * D])
        wbuf = sb("wbuf", [P, 2, KC * ZC])
        T = sb("T", [P, 3204 + 520])
        kTr = sb("kTr", [P, 2 * P])
        vprev = sb("vprev", [P, P])
        pinT = sb("pinT", [P, 4, 16 + P])
        tab = sb("tab", [P, 4, P])
        CT = sb("CT", [P, CH, CD1])
        mprev = sb("mprev", [P, CH])

        z = arena[:, 0:NT * ZW].rearrange("p (t n) -> p t n", t=NT)
        bias = arena[:, NT * ZW:NT * ZW + 2048]
        ring = arena[:, NT * ZW + 2048:NT * ZW + 2048 + RING * 2 * D].rearrange("p (r n) -> p r n", r=RING)
        xs = R[:, 0:NT * D].rearrange("p (t n) -> p t n", t=NT)
        L = R[:, 0:2048].rearrange("p (h n) -> p h n", h=AH)
        PT = R[:, 2048:4096].rearrange("p (i n) -> p i n", i=16)
        mT = R[:, 0:KC * TOK].rearrange("p (c n) -> p c n", c=KC)
        qks = T[:, 0:640]
        pcs = T[:, 640:1664]
        kcs = T[:, 1664:2176]
        qTs = T[:, 2176:2688].rearrange("p (j n) -> p j n", j=4)
        tmpi = T[:, 2688:3204]
        sm = T[:, 3204:3204 + 520]
        qcT = yT[:, 8:10, :].rearrange("p a n -> p (a n)")
        kcT = yT[:, 10:12, :].rearrange("p a n -> p (a n)")
        Am, STs = grow[:, 0:512], grow[:, 512:1024]
        pA, pB = (wbuf[:, 1, i * 576:(i + 1) * 576].rearrange("p (c n) -> p c n", c=4) for i in range(2))

        sgs = T[:, 0:3 * TOK].rearrange("p (b n) -> p b n", b=3)
        pr = T[:, 1536:1536 + TOK]
        v16, i16, f16 = T[:, 1024:1216], T[:, 1216:1408].bitcast(U32), T[:, 1408:1536].bitcast(BF16)
        pab = T[:, 1600:1728].bitcast(U32).rearrange("p (k m) -> p k m", k=2)
        pabf = T[:, 1728:1792].bitcast(BF16).rearrange("p (k m) -> p k m", k=2)
        eab = T[:, 1856:2048].rearrange("p (k m) -> p k m", k=3)
        esm, esr = T[:, 2048:2048 + NT * PH], T[:, 2064:2064 + NT * PH]
        scratch = yT[:, 2:12, :].rearrange("p k n -> p (k n)")
        ssb, srep = (scratch[:, i * 2 * NT * P:(i + 1) * 2 * NT * P].rearrange("p (k t n) -> p k t n", k=2, t=NT) for i in range(2))
        cand, crep = (scratch[:, 4 * NT * P + i * NT * 256:4 * NT * P + (i + 1) * NT * 256] for i in range(2))
        zs = arena[0:NS, 0:ZW]
        NP = NS * CH
        ROUNDS, RP = 4, NP // 4
        rounds = [[a[:, RP * CD * i:RP * CD * (i + 1)].rearrange("p (m d) -> p m d", m=RP) for i in range(3)]
                  for a in (R, arena[:, ZW:2 * ZW])]
        Rv = R[:, 3 * RP * CD:4 * RP * CD].rearrange("p (m d) -> p m d", m=RP)
        Ks, Vs, KTs = (T[:, NS * P * i:NS * P * (i + 1)].rearrange("p (n d) -> p n d", n=NS) for i in range(3))
        spool, full = xin[:, 1, 0:512], xin[:, 1, 512:1024].rearrange("p (c n r) -> p c n r", c=4, n=NS)
        X = bias
        relrep, sbuck, misc = X[0:32, 0:64], X[0:32, 64:192], X[0:64, 192:196]
        qTn, Sn, bias_s, Ls, PTs = X[:, 196:228], X[:, 228:292], X[0:64, 292:420], X[0:64, 420:548], X[:, 548:612]
        am, amx, anm, asd, aes, ars, adn, ard = (X[0:64, 612 + i:613 + i] for i in range(8))
        psum_s, pool_s_in = X[:, 620:652].rearrange("p (c n) -> p c n", c=4), X[:, 652:684].rearrange("p (c n) -> p c n", c=4)
        vT, coT, bc = X[:, 684:716], X[:, 716:748], X[:, 748:876].rearrange("p (k m) -> p k m", k=4)
        q32, k32, n32, t32 = (X[0:NP, 876 + P * i:876 + P * (i + 1)] for i in range(4))
        g32 = X[0:NP, 1388:1390]
        c1 = X[0:NP, 1390:1420]
        dg32 = X[0:NP, 1420:1548].rearrange("p (k m) -> p k m", k=4)
        cq, num, num2, hh, hq, hms_s, hinv_s, hr_s, us = (X[:, 1548 + 32 * i:1580 + 32 * i] for i in range(9))
        qTsmp = X[:, 1836:1964].rearrange("p (k m) -> p k m", k=2)
        selT, sel = X[0:64, 1964:1972], X[0:NS, 1972:2036]

        state_out = T[:, 2560:3072]

        def small(a, n):
            return sm[:, a:a + n]

        ssq, ms4, inv4, rstd = small(0, 4), small(4, 4), small(8, 4), small(12, 4)
        ss40, ms40, inv40, r40 = (small(16 + 20 * i, 10 * NT) for i in range(4))
        gts, absf, expf, lnf, minf, lf = small(96, 8 * NT), *(small(112 + 8 * i, CH * NT) for i in range(5))
        bM, asb, rmax, bml, args, exps = small(152, 8), small(160, 4), small(164, 4), small(168, 8), small(176, 16), small(192, 16)
        mx8, mxs, negmx, sinkd, esink, rsum, aden, arden = (small(208 + 8 * i, 8) for i in range(8))
        dn, rd = small(272, 4), small(276, 4)
        hss, hms, hinv, hr = (small(280 + 8 * i, CH * NT) for i in range(4))

        block = ctx.enter_context(nc.Block())

        def hold(engine, sem, value):
            engine.wait_ge(sem, value)
            engine.nop(nofuse=True)

        def tokens(p):
            return (P, NT) if p < PASSES else (NS, 1)

        def project_block(i):
            return PRB * PRG // NZ * i

        def project_share(c):
            n = PRB * RING // NZ
            return (c * n + 1) // 2 * 2, ((c + 1) * n + 1) // 2 * 2

        def norms(p, which, t):
            return p * 2 * NT + which * NT + t if p < PASSES else 2 * PASSES * NT + which


        def sample_loads(sp, at):
            def load_c(r):
                if r >= 2:
                    sp.wait_ge(s["state_c_stored"], 16 * (r - 1))
                sp.dma_start(rounds[r % 2][2], st_c[:, RP * r:RP * (r + 1), :]).then_inc(s[f"c_round{r % 2}"], 16)

            def load_qk(r):
                for i in range(2):
                    sp.dma_start(rounds[r % 2][i].rearrange("p (n h) d -> p n (h d)", h=CH),
                                 at(scr_qk, r * (NS // ROUNDS) * 2 * CH * CD + i * CH * CD, [[0, P], [2 * CH * CD, NS // ROUNDS], [1, CH * CD]])
                                 ).then_inc(s[f"c_round{r % 2}"], 16)

            sp.dma_start(k_s[:, 0:W - 1, :], cache_k[:, 1:W, :]).then_inc(s["kscr"], 16)
            sp.dma_start(v_s[:, 0:W - 1, :], cache_v[:, 1:W, :]).then_inc(s["kscr"], 16)
            sp.dma_start(pool_s[:, 0:HIST - 1, :], state_pool[:, 1:HIST, :]).then_inc(s["outs"], 16)
            sp.dma_start(spool[0:NS * HIST, :], state_pool.rearrange("n r c -> (n r) c")).then_inc(s["b_n"], 16)
            sp.dma_start(relrep, relr).then_inc(s["c_load"], 16)
            sp.dma_start(sbuck, consts[0:32, C_SBUCK:C_ALL]).then_inc(s["c_load"], 16)
            sp.dma_start(misc, sinkcol).then_inc(s["c_load"], 16)
            sp.dma_start(selT, selmat[:, 0:NS]).then_inc(s["c_load"], 16)
            sp.dma_start(sel, selmat[0:NS, NS:NS + 64]).then_inc(s["c_load"], 16)
            sp.dma_start(n32, st_n).then_inc(s["c_load"], 16)
            sp.dma_start(c1[:, 2:3], st_m).then_inc(s["c_load"], 16)
            load_c(0)
            load_c(1)
            sp.wait_ge(s["evac_a"], NT * NZ * PASSES + 4 + NZ)
            sp.dma_start(scr_qk, zs[:, CQ0:CQ0 + 1024].rearrange("n (k m) -> n k m", k=2)).then_inc(s["c_scr"], 16)
            sp.dma_start(scr_g.rearrange("k n h -> n k h"), zs[:, G0:G0 + 8].rearrange("n (k h) -> n k h", k=2)).then_inc(s["c_scr"], 16)
            sp.dma_start(pool_s[:, HIST - 1, :], zs[:, PIN0:PIN0 + 512]).then_inc(s["outs"], 16)
            sp.wait_ge(s["c_scr"], 32)
            sp.dma_start(g32, scr_g.rearrange("k n h -> (n h) k"), allow_slow_non_contiguous=True).then_inc(s["c_load2"], 16)
            for i, t in enumerate((q32, k32)):
                sp.dma_start(t, at(scr_qk, i * CH * CD, [[2 * CH * CD, NS], [CD, CH], [1, CD]])).then_inc(s["c_load2"], 16)
            load_qk(0)
            load_qk(1)
            sp.wait_ge(s["qkn"], PASSES + 1)
            sp.dma_start(k_s[:, W - 1, :], zs[:, 512:640]).then_inc(s["kscr"], 16)
            sp.dma_start(v_s[:, W - 1, :], zs[:, V0:V0 + P]).then_inc(s["kscr"], 16)
            sp.wait_ge(s["kscr"], 64)
            sp.wait_ge(s["state_stored"], 16)
            sp.dma_start(Ks, k_s.rearrange("n k c -> k n c")).then_inc(s["k_load"], 16)
            sp.dma_start(Vs, v_s.rearrange("n k c -> k n c")).then_inc(s["k_load"], 16)
            sp.wait_ge(s["smp_v"], SMP["v"].at("c_mt"))
            sp.dma_start(m_s, c1[:, 8:9]).then_inc(s["outs"], 16)
            sp.wait_ge(s["smp_v"], SMP["v"].at("c_nn2"))
            sp.dma_start(n_s, n32).then_inc(s["outs"], 16)
            for r in range(ROUNDS):
                sp.wait_ge(s["smp_v"], SMP["v"].at(f"c_cn{r}"))
                sp.dma_start(c_s[:, RP * r:RP * (r + 1), :], rounds[r % 2][2]).then_inc(s["state_c_stored"], 16)
                if r + 2 < ROUNDS:
                    load_c(r + 2)
                    load_qk(r + 2)

        def sample_tensor(pe):
            mm, tr = nc.tensor.matmul, nc.tensor.transpose
            id8 = ident[0:NS, 0:NS]
            for h in range(CH):
                tr(ps[:, 0, h * NS:(h + 1) * NS], zs[:, CV0 + h * CD1:CV0 + h * CD1 + CD], id8)
            for h in range(CH):
                last = tr(ps[:, 0, 32 + h * NS:32 + (h + 1) * NS], zs[:, CO0 + h * CD:CO0 + (h + 1) * CD], id8)
            last.then_inc(s["smp_p"], SMP["p"].step("c_tr"))
            for c in range(4):
                last = tr(ps[:, 1, c * NS:(c + 1) * NS], zs[:, PIN0 + c * P:PIN0 + (c + 1) * P], id8)
            last.then_inc(s["smp_p"], SMP["p"].step("b_xtr"))
            pe.wait_ge(s["b_n"], 16)
            for c in range(4):
                last = tr(ps[:, 2, c * P:c * P + NS * HIST], spool[0:NS * HIST, c * P:(c + 1) * P], ident[0:NS * HIST, 0:NS * HIST])
            last.then_inc(s["smp_p"], SMP["p"].step("b_tr"))
            pe.wait_ge(s["c_load"], 16 * 7)
            mm(ps[0:64, 3, 0:P], relrep, sbuck, start=True, stop=True).then_inc(s["smp_p"], SMP["p"].step("a_bmm"))
            pe.wait_ge(s["qkn"], PASSES + 1)
            for j in range(4):
                last = tr(ps[:, 4, j * NS:(j + 1) * NS], zs[:, j * P:(j + 1) * P], id8)
            last.then_inc(s["smp_p"], SMP["p"].step("a_qtr"))
            pe.wait_ge(s["k_load"], 32)
            for n in range(NS):
                last = tr(ps[:, 5 + n // 4, (n % 4) * P:(n % 4 + 1) * P], Ks[:, n, :], ident)
            last.then_inc(s["smp_p"], SMP["p"].step("a_ktr"))
            pe.wait_ge(s["smp_v"], SMP["v"].at("b_p"))
            for c in range(4):
                last = mm(ps[:, 7, c * NS:(c + 1) * NS], wpool[:, c, :], pool_s_in[:, c, :], start=True, stop=True)
            last.then_inc(s["smp_p"], SMP["p"].step("b_mm"))
            pe.wait_ge(s["smp_v"], SMP["v"].at("c_dg"))
            mm(ps[:, 0, 0:P], ones[0:NP, :], dg32.rearrange("p k m -> p (k m)"), start=True, stop=True).then_inc(s["smp_p"], SMP["p"].step("c_bc"))
            pe.wait_ge(s["smp_a"], SMP["a"].at("a_kT"))
            pe.wait_ge(s["smp_v"], SMP["v"].at("a_qT"))
            for n in range(NS):
                for kv in range(2):
                    last = mm(ps[:, 1 + kv, n * AG:(n + 1) * AG], KTs[64 * kv:64 * kv + 64, n, :], qTn[64 * kv:64 * kv + 64, n * AG:(n + 1) * AG],
                              start=True, stop=True)
            last.then_inc(s["smp_p"], SMP["p"].step("a_smm"))
            pe.wait_ge(s["smp_a"], SMP["a"].at("a_s"))
            tr(ps[0:64, 4, 0:P], Sn, ident).then_inc(s["smp_p"], SMP["p"].step("a_str"))
            pe.wait_ge(s["smp_v"], SMP["v"].at("c_h2"))
            mm(ps[:, 5, 0:NP], ones[:, :], hq, start=True, stop=True).then_inc(s["smp_p"], SMP["p"].step("c_hmm"))
            pe.wait_ge(s["smp_v"], SMP["v"].at("a_pn"))
            tr(ps[:, 6, 0:64], Ls, ident[0:64, 0:64]).then_inc(s["smp_p"], SMP["p"].step("a_ptr"))
            pe.wait_ge(s["smp_v"], SMP["v"].at("a_PT"))
            for n in range(NS):
                for kv in range(2):
                    c = n * AH + kv * AG
                    last = mm(ps[64 * kv:64 * kv + 64, 4, n * AG:(n + 1) * AG], Vs[:, n, 64 * kv:64 * kv + 64], PTs[:, c:c + AG],
                              start=True, stop=True)
            last.then_inc(s["smp_p"], SMP["p"].step("a_pv"))
            pe.wait_ge(s["smp_a"], SMP["a"].at("a_ya"))
            pe.wait_ge(s["smp_v"], SMP["v"].at("b_y"))
            pe.wait_ge(s["smp_v"], SMP["v"].at("c_y"))

        def sample_scalar(act):
            f = nc.scalar.activation
            act.wait_ge(s["inv40"], PASSES + 1)
            f(r40[0:NS, 0:10], inv40[0:NS, 0:10], ACT.Sqrt).then_inc(s["r40"], 1)
            act.wait_ge(s["smp_p"], SMP["p"].at("c_tr"))
            f(coT.rearrange("p (n h) -> p h n", h=CH), ps[:, 0, 32:64].rearrange("p (h n) -> p h n", h=CH), ACT.Sigmoid).then_inc(s["smp_a"], SMP["a"].step("m_sig"))
            f(vT.rearrange("p (n h) -> p h n", h=CH), ps[:, 0, 0:32].rearrange("p (h n) -> p h n", h=CH), ACT.Copy).then_inc(s["smp_a"], SMP["a"].step("c_T"))
            act.wait_ge(s["smp_p"], SMP["p"].at("b_tr"))
            f(full[:, :, :, 0:HIST], ps[:, 2, :].rearrange("p (c m) -> p c m", c=4)[:, :, 0:NS * HIST].rearrange("p c (n r) -> p c n r", n=NS),
              ACT.Copy)
            act.wait_ge(s["smp_p"], SMP["p"].at("b_xtr"))
            f(full[:, :, :, HIST], ps[:, 1, 0:32].rearrange("p (c n) -> p c n", c=4), ACT.Copy).then_inc(s["smp_a"], SMP["a"].step("b_T"))
            act.wait_ge(s["smp_p"], SMP["p"].at("a_ktr"))
            f(KTs, ps[:, 5:7, :].rearrange("p b (n k) -> p (b n) k", n=4), ACT.Copy).then_inc(s["smp_a"], SMP["a"].step("a_kT"))
            act.wait_ge(s["smp_v"], SMP["v"].at("c_abs"))
            f(c1[:, 4:5], c1[:, 3:4], ACT.Exp, scale=-1.0).then_inc(s["smp_a"], SMP["a"].step("c_e"))
            act.wait_ge(s["smp_a"], SMP["a"].at("c_e"))
            f(c1[:, 5:6], c1[:, 4:5], ACT.Ln, bias=1.0).then_inc(s["smp_a"], SMP["a"].step("c_ln"))
            act.wait_ge(s["smp_v"], SMP["v"].at("c_d"))
            f(c1[:, 12:15], c1[:, 9:12], ACT.Exp).then_inc(s["smp_a"], SMP["a"].step("c_x"))
            act.wait_ge(s["smp_p"], SMP["p"].at("a_smm"))
            f(Sn.rearrange("p (n k j) -> p k n j", k=AKV, j=AG), ps[:, 1:3, 0:32].rearrange("p k (n j) -> p k n j", j=AG), ACT.Copy).then_inc(s["smp_a"], SMP["a"].step("a_s"))
            act.wait_ge(s["smp_v"], SMP["v"].at("a_m3"))
            f(aes, asd, ACT.Exp).then_inc(s["smp_a"], SMP["a"].step("a_es"))
            f(Ls, Ls, ACT.Exp, bias=anm, accum_out=ars).then_inc(s["smp_a"], SMP["a"].step("a_p"))
            act.wait_ge(s["smp_v"], SMP["v"].at("c_hinv"))
            f(hr_s, hinv_s, ACT.Sqrt).then_inc(s["smp_a"], SMP["a"].step("c_hr"))
            act.wait_ge(s["smp_p"], SMP["p"].at("a_pv"))
            act.wait_ge(s["smp_p"], SMP["p"].at("a_ktr"))
            f(yT[:, 0:4, 0:NS], ps[:, 4, 0:32].rearrange("p (n j) -> p j n", j=AG), ACT.Copy).then_inc(s["smp_a"], SMP["a"].step("a_ya"))

        def sample_vector(dve):
            v = nc.vector
            n = PASSES + 1
            scale = float(CD) ** -0.5
            dve.wait_ge(s["evac_a"], NT * NZ * PASSES + 4 + NZ)
            sq = yT[0:NS, 0:3, :].rearrange("p a n -> p (a n)")[:, 0:640]
            v.tensor_tensor(sq, zs[:, 0:640], zs[:, 0:640], ALU.mult).then_inc(s["smp_v"], SMP["v"].step("q_sq_ready"))
            dve.wait_ge(s["smp_v"], SMP["v"].at("q_sq_ready"))
            v.tensor_reduce(ss40[0:NS, 0:10], sq.rearrange("p (h d) -> p h d", d=AD), AX.X, ALU.add).then_inc(s["smp_v"], SMP["v"].step("q_ss_ready"))
            dve.wait_ge(s["smp_v"], SMP["v"].at("q_ss_ready"))
            v.tensor_scalar(ms40[0:NS, 0:10], ss40[0:NS, 0:10], 1.0 / AD, EPS, ALU.mult, ALU.add).then_inc(s["smp_v"], SMP["v"].step("q_ms40"))
            dve.wait_ge(s["smp_v"], SMP["v"].at("q_ms40"))
            v.reciprocal(inv40[0:NS, 0:10], ms40[0:NS, 0:10]).then_inc(s["inv40"], 1)
            dve.wait_ge(s["r40"], n)
            zq = zs[:, 0:640].rearrange("p (h d) -> p h d", d=AD)
            v.tensor_tensor(zq, zq, r40[0:NS, 0:10].unsqueeze(2).broadcast_to([NS, 10, AD]), ALU.mult).then_inc(s["smp_v"], SMP["v"].step("q_qk_scaled"))
            dve.wait_ge(s["smp_v"], SMP["v"].at("q_qk_scaled"))
            v.tensor_tensor(zs[:, 0:640], zs[:, 0:640], row[0:NS, R_QK:R_QK + 640], ALU.mult).then_inc(s["qkn"], 1)
            dve.wait_ge(s["smp_a"], SMP["a"].at("b_T"))
            for c, w in enumerate(POOLW):
                last = v.tensor_reduce(psum_s[:, c, :], full[:, c, :, 16 - w:16], AX.X, ALU.add)
            last.then_inc(s["smp_v"], SMP["v"].step("b_s1"))
            dve.wait_ge(s["smp_v"], SMP["v"].at("b_s1"))
            for c, w in enumerate(POOLW):
                last = v.scalar_tensor_tensor(pool_s_in[:, c, :], psum_s[:, c, :], 1.0 / w, full[:, c, :, HIST], ALU.mult, ALU.subtract)
            last.then_inc(s["smp_v"], SMP["v"].step("b_p"))
            dve.wait_ge(s["c_load"], 16 * 7)
            dve.wait_ge(s["c_load2"], 16 * 3)
            v.tensor_tensor(c1[:, 0:2], g32, misc[0:NP, 1:3], ALU.add).then_inc(s["smp_v"], SMP["v"].step("c_m0"))
            dve.wait_ge(s["smp_v"], SMP["v"].at("c_m0"))
            v.scalar_tensor_tensor(c1[:, 3:4], c1[:, 1:2], -1.0, c1[:, 1:2], ALU.mult, ALU.max).then_inc(s["smp_v"], SMP["v"].step("c_abs"))
            v.tensor_scalar(c1[:, 6:7], c1[:, 1:2], 0.0, None, ALU.min).then_inc(s["smp_v"], SMP["v"].step("c_lf0"))
            v.tensor_tensor(t32, q32, k32, ALU.mult).then_inc(s["smp_v"], SMP["v"].step("c_qk"))
            dve.wait_ge(s["smp_v"], SMP["v"].at("c_qk"))
            v.tensor_reduce(c1[:, 16:17], t32, AX.X, ALU.add).then_inc(s["smp_v"], SMP["v"].step("c_qk1"))
            dve.wait_ge(s["smp_v"], SMP["v"].at("c_qk1"))
            v.tensor_tensor(t32, q32, n32, ALU.mult).then_inc(s["smp_v"], SMP["v"].step("c_nq"))
            dve.wait_ge(s["smp_v"], SMP["v"].at("c_nq"))
            v.tensor_reduce(c1[:, 17:18], t32, AX.X, ALU.add).then_inc(s["smp_v"], SMP["v"].step("c_nq1"))
            dve.wait_ge(s["smp_a"], SMP["a"].at("c_ln"))
            dve.wait_ge(s["smp_v"], SMP["v"].at("c_lf0"))
            v.tensor_tensor(c1[:, 7:8], c1[:, 6:7], c1[:, 5:6], ALU.subtract).then_inc(s["smp_v"], SMP["v"].step("c_lf"))
            dve.wait_ge(s["smp_v"], SMP["v"].at("c_lf"))
            v.tensor_tensor(c1[:, 18:19], c1[:, 7:8], c1[:, 2:3], ALU.add).then_inc(s["smp_v"], SMP["v"].step("c_i"))
            dve.wait_ge(s["smp_v"], SMP["v"].at("c_i"))
            v.tensor_tensor(c1[:, 8:9], c1[:, 18:19], c1[:, 0:1], ALU.max).then_inc(s["smp_v"], SMP["v"].step("c_mt"))
            dve.wait_ge(s["smp_v"], SMP["v"].at("c_mt"))
            v.tensor_tensor(c1[:, 9:10], c1[:, 18:19], c1[:, 8:9], ALU.subtract)
            v.tensor_tensor(c1[:, 10:11], c1[:, 0:1], c1[:, 8:9], ALU.subtract)
            v.tensor_scalar(c1[:, 11:12], c1[:, 8:9], -1.0, None, ALU.mult).then_inc(s["smp_v"], SMP["v"].step("c_d"))
            dve.wait_ge(s["smp_a"], SMP["a"].at("c_x"))
            v.tensor_copy(c1[:, 19:20], c1[:, 12:13])
            v.tensor_scalar(c1[:, 20:21], c1[:, 13:14], scale, None, ALU.mult).then_inc(s["smp_v"], SMP["v"].step("c_S"))
            dve.wait_ge(s["smp_v"], SMP["v"].at("c_S"))
            dve.wait_ge(s["smp_v"], SMP["v"].at("c_nq1"))
            v.tensor_tensor(c1[:, 21:22], c1[:, 20:21], c1[:, 16:17], ALU.mult).then_inc(s["smp_v"], SMP["v"].step("c_den0"))
            dve.wait_ge(s["smp_v"], SMP["v"].at("c_den0"))
            v.scalar_tensor_tensor(c1[:, 23:24], c1[:, 17:18], c1[:, 19:20], c1[:, 21:22], ALU.mult, ALU.add).then_inc(s["smp_v"], SMP["v"].step("c_den1"))
            dve.wait_ge(s["smp_v"], SMP["v"].at("c_den1"))
            v.scalar_tensor_tensor(c1[:, 25:26], c1[:, 23:24], -1.0, c1[:, 23:24], ALU.mult, ALU.max).then_inc(s["smp_v"], SMP["v"].step("c_denabs"))
            dve.wait_ge(s["smp_v"], SMP["v"].at("c_denabs"))
            v.tensor_tensor(c1[:, 24:25], c1[:, 25:26], c1[:, 14:15], ALU.max).then_inc(s["smp_v"], SMP["v"].step("c_den2"))
            dve.wait_ge(s["smp_v"], SMP["v"].at("c_den2"))
            v.reciprocal(c1[:, 22:23], c1[:, 24:25]).then_inc(s["smp_v"], SMP["v"].step("c_rd"))
            dve.wait_ge(s["smp_v"], SMP["v"].at("c_rd"))
            v.tensor_tensor(dg32, ident[0:NP, 0:NP].unsqueeze(1).broadcast_to([NP, 4, NP]), c1[:, 19:23].unsqueeze(2).broadcast_to([NP, 4, NP]),
                            ALU.mult).then_inc(s["smp_v"], SMP["v"].step("c_dg"))
            v.tensor_scalar(t32, k32, c1[:, 20:21], None, ALU.mult).then_inc(s["smp_v"], SMP["v"].step("c_nn1"))
            dve.wait_ge(s["smp_v"], SMP["v"].at("c_nn1"))
            v.scalar_tensor_tensor(n32, n32, c1[:, 19:20], t32, ALU.mult, ALU.add).then_inc(s["smp_v"], SMP["v"].step("c_nn2"))
            dve.wait_ge(s["smp_p"], SMP["p"].at("a_qtr"))
            v.tensor_copy(qTn.rearrange("p (n j) -> p j n", j=AG), ps[:, 4, 0:32].rearrange("p (j n) -> p j n", j=AG)).then_inc(s["smp_v"], SMP["v"].step("a_qT"))
            dve.wait_ge(s["smp_p"], SMP["p"].at("a_bmm"))
            v.tensor_copy(bias_s, ps[0:64, 3, 0:P]).then_inc(s["smp_v"], SMP["v"].step("a_b"))
            dve.wait_ge(s["smp_p"], SMP["p"].at("b_mm"))
            v.tensor_tensor(yT[:, 4:8, 0:NS], ps[:, 7, 0:32].rearrange("p (c n) -> p c n", c=4), col[:, 0:4].unsqueeze(2).broadcast_to([P, 4, NS]),
                            ALU.mult).then_inc(s["smp_v"], SMP["v"].step("b_y"))
            dve.wait_ge(s["smp_p"], SMP["p"].at("c_bc"))
            v.tensor_copy(bc, ps[:, 0, 0:P].rearrange("p (k m) -> p k m", k=4)).then_inc(s["smp_v"], SMP["v"].step("c_bcs"))
            dve.wait_ge(s["smp_p"], SMP["p"].at("a_str"))
            dve.wait_ge(s["smp_v"], SMP["v"].at("a_b"))
            v.scalar_tensor_tensor(Ls, ps[0:64, 4, 0:P], float(AD) ** -0.5, bias_s, ALU.mult, ALU.add).then_inc(s["smp_v"], SMP["v"].step("a_l"))
            dve.wait_ge(s["smp_v"], SMP["v"].at("a_l"))
            v.tensor_reduce(am, Ls, AX.X, ALU.max).then_inc(s["smp_v"], SMP["v"].step("a_m1"))
            dve.wait_ge(s["smp_v"], SMP["v"].at("a_m1"))
            v.tensor_tensor(amx, am, misc[:, 0:1], ALU.max).then_inc(s["smp_v"], SMP["v"].step("a_m2"))
            dve.wait_ge(s["smp_v"], SMP["v"].at("a_m2"))
            v.tensor_scalar(anm, amx, -1.0, None, ALU.mult)
            v.tensor_tensor(asd, misc[:, 0:1], amx, ALU.subtract).then_inc(s["smp_v"], SMP["v"].step("a_m3"))
            dve.wait_ge(s["smp_v"], SMP["v"].at("c_bcs"))
            dve.wait_ge(s["smp_a"], SMP["a"].at("c_T"))
            v.tensor_tensor(us, vT, bc[:, 1, :], ALU.mult).then_inc(s["smp_v"], SMP["v"].step("c_u"))
            dve.wait_ge(s["smp_v"], SMP["v"].at("c_u"))
            for r in range(ROUNDS):
                qb, kb, Cs = rounds[r % 2]
                m = slice(RP * r, RP * (r + 1))
                dve.wait_ge(s[f"c_round{r % 2}"], 16 * 3 * (r // 2 + 1))
                if r:
                    dve.wait_ge(s["smp_v"], SMP["v"].at(f"c_cqr{r - 1}"))
                v.tensor_tensor(Rv, Cs, qb, ALU.mult).then_inc(s["smp_v"], SMP["v"].step(f"c_cq{r}"))
                v.tensor_tensor(kb, kb, us[:, m].unsqueeze(2).broadcast_to([P, RP, CD]), ALU.mult).then_inc(s["smp_v"], SMP["v"].step(f"c_t1{r}"))
                dve.wait_ge(s["smp_v"], SMP["v"].at(f"c_cq{r}"))
                v.tensor_tensor(Cs, Cs, bc[:, 0, m].unsqueeze(2).broadcast_to([P, RP, CD]), ALU.mult).then_inc(s["smp_v"], SMP["v"].step(f"c_t2{r}"))
                v.tensor_reduce(cq[:, m], Rv, AX.X, ALU.add).then_inc(s["smp_v"], SMP["v"].step(f"c_cqr{r}"))
                dve.wait_ge(s["smp_v"], SMP["v"].at(f"c_t2{r}"))
                v.tensor_tensor(Cs, Cs, kb, ALU.add).then_inc(s["smp_v"], SMP["v"].step(f"c_cn{r}"))
            dve.wait_ge(s["smp_v"], SMP["v"].at(f"c_cqr{ROUNDS - 1}"))
            v.tensor_tensor(num, cq, bc[:, 0, :], ALU.mult)
            v.tensor_tensor(num2, vT, bc[:, 2, :], ALU.mult).then_inc(s["smp_v"], SMP["v"].step("c_n1"))
            dve.wait_ge(s["smp_v"], SMP["v"].at("c_n1"))
            v.tensor_tensor(num, num, num2, ALU.add).then_inc(s["smp_v"], SMP["v"].step("c_n2"))
            dve.wait_ge(s["smp_v"], SMP["v"].at("c_n2"))
            v.tensor_tensor(hh, num, bc[:, 3, :], ALU.mult).then_inc(s["smp_v"], SMP["v"].step("c_h"))
            dve.wait_ge(s["smp_v"], SMP["v"].at("c_h"))
            v.tensor_tensor(hq, hh, hh, ALU.mult).then_inc(s["smp_v"], SMP["v"].step("c_h2"))
            dve.wait_ge(s["smp_a"], SMP["a"].at("a_es"))
            dve.wait_ge(s["smp_a"], SMP["a"].at("a_p"))
            v.tensor_tensor(adn, ars, aes, ALU.add).then_inc(s["smp_v"], SMP["v"].step("a_den"))
            dve.wait_ge(s["smp_v"], SMP["v"].at("a_den"))
            v.reciprocal(ard, adn).then_inc(s["smp_v"], SMP["v"].step("a_rd"))
            dve.wait_ge(s["smp_v"], SMP["v"].at("a_rd"))
            v.tensor_scalar(Ls, Ls, ard, None, ALU.mult).then_inc(s["smp_v"], SMP["v"].step("a_pn"))
            dve.wait_ge(s["smp_p"], SMP["p"].at("c_hmm"))
            v.tensor_scalar(hms_s, ps[:, 5, 0:NP], 1.0 / CD, EPS, ALU.mult, ALU.add).then_inc(s["smp_v"], SMP["v"].step("c_hms"))
            dve.wait_ge(s["smp_v"], SMP["v"].at("c_hms"))
            v.reciprocal(hinv_s, hms_s).then_inc(s["smp_v"], SMP["v"].step("c_hinv"))
            dve.wait_ge(s["smp_p"], SMP["p"].at("a_ptr"))
            v.tensor_copy(PTs, ps[:, 6, 0:64]).then_inc(s["smp_v"], SMP["v"].step("a_PT"))
            dve.wait_ge(s["smp_a"], SMP["a"].at("c_hr"))
            v.tensor_tensor(hh, hh, hr_s, ALU.mult).then_inc(s["smp_v"], SMP["v"].step("c_hy"))
            dve.wait_ge(s["smp_v"], SMP["v"].at("c_hy"))
            dve.wait_ge(s["smp_a"], SMP["a"].at("m_sig"))
            v.scalar_tensor_tensor(hq, hh, col[:, 4:5], coT, ALU.mult, ALU.mult).then_inc(s["smp_v"], SMP["v"].step("c_hy2"))
            dve.wait_ge(s["smp_v"], SMP["v"].at("c_hy2"))
            v.tensor_copy(yT[:, 8:12, 0:NS], hq.rearrange("p (n h) -> p h n", h=CH)).then_inc(s["smp_v"], SMP["v"].step("c_y"))

        BASE = PASSES * NT * P

        def sample_experts_tensor(pe):
            mm = nc.tensor.matmul
            pe.wait_ge(s["q_evac"], 2 * PH * (PASSES + 1) + 2)
            for k in range(2):
                last = mm(ps[0:64, 2 + k, 0:NKEY], qTsmp[:, k, :], keys[:, k, :], start=True, stop=True)
            last.then_inc(s["smp_p"], SMP["p"].step("sample_s"))
            for q in range(2):
                last = mm(ps[0:64, 4 + q, :], sel, xs[0:NS, 0, q * 512:(q + 1) * 512], start=True, stop=True)
            last.then_inc(s["smp_p"], SMP["p"].step("xb_mm"))
            for j in range(PK):
                pe.wait_ge(s["diagd"], BASE + j + 1)
                for q in range(2):
                    last = mm(ps[0:NS, q, :], dgs[0:64, j % 8, 0:NS], ring[0:64, j % RING, D + q * 512:D + (q + 1) * 512],
                              start=(j == 0), stop=(j == PK - 1))
                last.then_inc(s["slot_free"], 1)

        def sample_experts_scalar(act):
            f = nc.scalar.activation
            act.wait_ge(s["smp_p"], SMP["p"].at("sample_s"))
            f(ssb[0:64, :, 0, :], ps[0:64, 2:4, 0:NKEY], ACT.Copy).then_inc(s["smp_a"], SMP["a"].step("t_sel"))
            act.wait_ge(s["esub"], PH * PASSES + 1)
            f(gates[0:64, 0, 0:PK], gates[0:64, 0, 0:PK], ACT.Exp).then_inc(s["eexp"], 1)
            act.wait_ge(s["smp_p"], SMP["p"].at("xb_mm"))
            act.wait_ge(s["gate_ready"], (PH + 1) * PASSES + 3)
            act.wait_ge(s["y_final"], NT * PASSES + 1)
            f(xcur[0:64, :].rearrange("p (q n) -> p q n", q=2), ps[0:64, 4:6, :], ACT.Copy).then_inc(s["smp_a"], SMP["a"].step("t_xb"))
            for j in range(PK // 2):
                act.wait_ge(s["dotted"], BASE + 2 * j + 3)
                k = 2 * j % 8
                f(gel[0:64, k:k + 2], dots[0:64, k:k + 2], ACT.Gelu).then_inc(s["gelud"], 1)

        def sample_experts_vector(dve, topk, softmax):
            v = nc.vector
            dve.wait_ge(s["smp_a"], SMP["a"].at("t_sel"))

            topk(PH * PASSES + 1, ssb, srep, 64, 1, gates[0:64, 0:1, 0:PK], eidx[0:64, 0:1, 0:PK])
            softmax(PASSES, gates[0:64, 0, 0:PK], 1, 64, s["smp_v"], SMP["v"], 0, ("t_esum", "t_erec"))
            dve.wait_ge(s["smp_a"], SMP["a"].at("t_xb"))
            for j in range(PK):
                r = j % RING
                dve.wait_ge(got[r], 16 * ((BASE + j) // RING + 1))
                v.tensor_tensor_reduce(ring[0:64, r, 0:D], ring[0:64, r, 0:D], xcur[0:64, :], 1.0, 0.0, ALU.mult, ALU.add,
                                       dots[0:64, r:r + 1]).then_inc(s["dotted"], 1)
                if j % 2 == 1:
                    dve.wait_ge(s["gelud"], (BASE + j + 1) // 2)
                    dve.wait_ge(s["slot_free"], BASE + j + 1)
                    for q in (j - 1, j):
                        v.tensor_scalar(dgs[0:64, q % 8, 0:NS], selT, gel[0:64, q % 8:q % 8 + 1], gates[0:64, 0, q:q + 1],
                                        ALU.mult, ALU.mult).then_inc(s["diagd"], 1)
            dve.wait_ge(s["slot_free"], BASE + PK + RING)
            v.tensor_tensor(xin[0:NS, 0, :].rearrange("p (q n) -> p q n", q=2), xin[0:NS, 0, :].rearrange("p (q n) -> p q n", q=2),
                            ps[0:NS, 0:2, :], ALU.add).then_inc(s["y_final"], 1)

        def sample_gpsimd(pool):
            pool.wait_ge(s["gate_ready"], (PH + 1) * PASSES + 3)
            for j in range(PK):
                pool.wait_ge(s["slot_free"], BASE + j + 1)
                nc.gpsimd.indirect_dma_start(ring[0:64, j % RING, :], None, uv,
                                             bass.IndirectOffsetOnAxis(ap=eidx[0:64, 0, j:j + 1], axis=0)).then_inc(got[j % RING], 16)

        @block.sync
        def _(sp):
            def at(t, off, ap):
                return bass.AP(tensor=t.tensor, offset=off, ap=ap)

            sp.dma_start(cst[:, :], consts[:, 0:C_KEEP]).then_inc(s["setup"], 16)
            sp.dma_start(T[:, 0:512], consts[:, C_KEEP:C_ALL]).then_inc(s["setup"], 16)
            sp.dma_start(row[:, :], at(rows, 0, [[0, P], [1, R_ALL]])).then_inc(s["setup"], 16)
            sp.dma_start(col[:, :], cols).then_inc(s["setup"], 16)
            sp.dma_start(keys[:, :, :], keysT).then_inc(s["setup"], 16)
            sp.dma_start(wpool[:, :, :], w_pool).then_inc(s["setup"], 16)
            sp.wait_ge(s["init_v"], 1)
            sp.dma_start(T[0:32, 512:520], rel).then_inc(s["setup"], 16)

            def gain(which, n):
                if n:
                    sp.wait_ge(s["xs_ready"], norms((n - 1) // 2, (n - 1) % 2, (NT if (n - 1) // 2 < PASSES else 1) - 1) + 1)
                sp.dma_start(grow[:, :], at(gains, which * D, [[0, P], [1, D]])).then_inc(s["g_in"], 16)

            used = [None]

            def weights(src, shape, count, sem, base, per, between=(), free=None):
                width = int(np.prod(shape))

                def load(i, k):
                    sp.dma_start(wbuf[:, k, 0:width], src[bass.ds(i, 1), :, :].rearrange("a p n -> (a p) n")).then_inc(w_in[k], 16)

                for k in range(2):
                    if used[0]:
                        sp.wait_ge(used[0][0], used[0][1 + k])
                    if k and free:
                        sp.wait_ge(*free)
                    load(k, k)
                for step in between:
                    step()
                with sp.Fori(1, count // 2) as i:
                    for k in range(2):
                        sp.wait_ge(sem, base + per * (k - 1) + 2 * per * i)
                        load(2 * i + k, k)
                used[0] = (sem, base + per * (count - 1), base + per * count)

            def load_cur(g, t):
                n = g * NT + t
                sp.wait_ge(s["scr_out"], 32 * (g + 1))
                if n:
                    sp.wait_ge(s["dotted"], n * P + 1)
                sp.dma_start(xcur, xs_scr[g][:, t, :]).then_inc(s["cur_in"], 16)

            def load_res(g, t):
                n = g * NT + t
                if n:
                    sp.wait_ge(s["y_out"], 16 * n)
                sp.dma_start(xres, x2_scr[g][:, t, :]).then_inc(s["res_in"], 16)

            def load_x(p):
                if p:
                    sp.wait_ge(s["scr_out"], 32 * p)
                if p < PASSES:
                    sp.dma_start(xin[:, :, :], x_prompt[p]).then_inc(s["x_in"], 16)
                else:
                    sp.dma_start(xin[0:NS, 0, :], x_sample).then_inc(s["x_in"], 16)
                gain(0, 2 * p)

            def store_tile(g, t):
                sp.wait_ge(s["y_final"], g * NT + t + 2)
                sp.dma_start(y_p[g][:, t, :], xres).then_inc(s["y_out"], 16)

            def store_states():
                last = NT - 1
                sp.wait_ge(s["qkn"], PASSES)
                sp.dma_start(k_p, z[:, last, 512:640]).then_inc(s["outs"], 16)
                sp.dma_start(v_p, z[:, last, V0:V0 + P]).then_inc(s["outs"], 16)
                sp.dma_start(pool_p, z[P - HIST:P, last, PIN0:PIN0 + 512]).then_inc(s["outs"], 16)
                sp.wait_ge(s["state_out_sb"], 1)
                sp.dma_start(c_p.rearrange("h e d -> e h d"), state_out.rearrange("p (h d) -> p h d", h=CH)).then_inc(s["state_stored"], 16)
                sp.dma_start(n_p.rearrange("h d -> d h"), CT[:, :, CD], allow_slow_non_contiguous=True).then_inc(s["outs"], 16)
                sp.dma_start(m_p, mprev[0:1, :]).then_inc(s["outs"], 16)

            load_x(0)
            for p in range(PASSES + 1):
                tiles = tokens(p)[1]
                first = []
                if p:
                    first += [lambda: load_cur(p - 1, 0)]
                    if p > 1:
                        first += [lambda: store_tile(p - 2, 1)]
                    first += [lambda: load_res(p - 1, 0)]
                weights(w_z, (KC, ZC), NZ, s["z_mm"], NT * NZ * p, tiles, first)
                if p < PASSES:
                    if p == 0:
                        sp.wait_ge(s["buck_sb"], 1)
                        table = T[0:AH, 1024:1408]
                        sp.dma_start(bass.AP(tensor=biasfull.tensor, offset=0, ap=[[2 * P, AH], [AH * 2 * P, P], [1, 2 * P]]),
                                     bass.AP(tensor=table.tensor, offset=table.offset + P - 1, ap=[table.ap[0], [-1, P], [1, 2 * P]])
                                     ).then_inc(s["scratch_w"], 16)
                        sp.wait_ge(s["scratch_w"], 16)
                        sp.dma_start(bias, biasfull).then_inc(s["bias_in"], 16)
                else:
                    sample_loads(sp, at)
                second = []
                if p:
                    second += [lambda: load_cur(p - 1, 1), lambda: store_tile(p - 1, 0), lambda: load_res(p - 1, 1)]
                if p == PASSES - 1:
                    second += [store_states]
                weights(w_merge, (12, P), 3 * KC, s["br_mm"], 3 * KC * p, 1, second,
                        (s["pooled_ready"], NT * (p + 1) + 1) if p < PASSES else None)
                weights(w_o, (KC, OC), NO, s["o_mm"], NT * NO * p, tiles)
                gain(1, 2 * p + 1)
                if p < PASSES:
                    sp.wait_ge(s["xs_ready"], norms(p, 1, NT - 1) + 1)
                    sp.dma_start(xs_scr[p], xs).then_inc(s["scr_out"], 16)
                    sp.dma_start(x2_scr[p], xin[:, :, :]).then_inc(s["scr_out"], 16)
                weights(w_q, (KC, P), 2 * PH, s["kq_mm"], 2 * PH * p, 1, [lambda: load_x(p + 1)] if p < PASSES else [])
                if p == PASSES:
                    store_tile(p - 1, 1)
                    sp.wait_ge(s["y_final"], p * NT + 2)
                    sp.dma_start(y_s, xin[0:NS, 0, :]).then_inc(s["y_out"], 16)
            sp.wait_ge(s["outs"], 16 * 9)
            sp.wait_ge(s["state_stored"], 16)
            sp.wait_ge(s["state_c_stored"], 16 * 4)
            sp.wait_ge(s["y_out"], 16 * (NT * PASSES + 1))

        @block.tensor
        def _(pe):
            mm = nc.tensor.matmul
            tr = nc.tensor.transpose
            pe.wait_ge(s["setup"], 16 * 7)
            pe.wait_ge(s["init_v"], 2)
            pe.wait_ge(s["init_p"], 2)
            mm(ps[0:AH, 0, 0:384], T[0:33, 512:520], T[0:33, 0:384], start=True, stop=True).then_inc(s["buck_mm"], 1)
            pe.wait_ge(s["buck_sb"], 1)

            def norm(p, which):
                rows_, tiles = tokens(p)
                for t in range(tiles):
                    n = norms(p, which, t)
                    pe.wait_ge(s["xs_ready"], n + 1)
                    for c in range(KC):
                        b = 2 + 2 * t + c // 4
                        last = tr(ps[:, b, (c % 4) * P:(c % 4) * P + rows_], xs[0:rows_, t, c * P:(c + 1) * P],
                                  ident[0:rows_, 0:rows_])
                    last.then_inc(s["xs_tr"], 1)
                pe.wait_ge(s["xT_ready"], norms(p, which, tiles - 1) + 1)

            def project(p):
                rows_, tiles = tokens(p)
                with pe.Fori(0, NZ // PRG) as i:
                    for c in range(PRG):
                        k = c % 2
                        pe.wait_ge(w_in[k], 16 * (p * UNITS // 2 + 1 + c // 2) + 16 * PRG // 2 * i)
                        wv = wbuf[:, k, :].rearrange("p (c n) -> p c n", c=KC)
                        for t in range(tiles):
                            pe.wait_ge(s["evac_a"], NT * NZ * p + 4 - 2 * tiles + t + 1 + c * tiles + PRG * tiles * i)
                            for kc in range(KC):
                                last = mm(ps[0:rows_, 2 + 2 * k + t, 0:ZC], xT[:, kc, t * P:t * P + rows_], wv[:, kc, :],
                                          start=(kc == 0), stop=(kc == KC - 1))
                            last.then_inc(s["z_mm"], 1)
                        if p:
                            experts_block(p - 1, 0, project_block(i), *project_share(c))

            def branches(p):
                pe.wait_ge(s["evac_a"], NT * NZ * (p + 1) + 4)
                pe.wait_ge(s["lf_ready"], p + 1)
                pe.wait_ge(s["ones_set"], p + 1)
                with pe.Fori(0, NT) as t:
                    here, before = p * NT + 2 + t, p * NT + 1 + t

                    def share(i):
                        if p:
                            experts_block(p - 1, 0, PRB + BRB * t, *BSHARE[i])

                    pe.wait_ge(s["qks_ready"], here)
                    pe.wait_ge(s["ya_ready"], before)
                    pe.wait_ge(s["yaT_done"], before)
                    pe.wait_ge(s["poolT_done"], before)
                    for j in range(4):
                        tr(ps[:, 2, j * P:(j + 1) * P], qks[:, j * P:(j + 1) * P], ident)
                    tr(ps[:, 3, 0:P], qks[:, 512:640], ident).then_inc(s["qk_tr"], 1)
                    pe.wait_ge(s["pcs_ready"], here)
                    pe.wait_ge(s["nd_ready"], before)
                    for j in range(4):
                        last = tr(ps[:, 6, j * P:(j + 1) * P], pcs[:, j * P:(j + 1) * P], ident)
                    last.then_inc(s["pin_tr"], 1)
                    pe.wait_ge(s["CT_ready"], before)
                    for j in range(4):
                        last = tr(ps[:, 4, j * P:(j + 1) * P], pcs[:, 512 + j * P:512 + (j + 1) * P], ident)
                    last.then_inc(s["cq_tr"], 1)
                    pe.wait_ge(s["kcs_ready"], here)
                    pe.wait_ge(s["nd_ready"], before)
                    for j in range(4):
                        last = tr(ps[:, 5, j * P:(j + 1) * P], kcs[:, j * P:(j + 1) * P], ident)
                    last.then_inc(s["ck_tr"], 1)
                    mm(ps[:, 7, 0:CH], tri, lf[:, bass.ds(CH * t, CH)], start=True, stop=True).then_inc(s["cs_mm"], 1)
                    share(0)
                    pe.wait_ge(s["diag_ready"], here)
                    pe.wait_ge(s["pinT_ready"], here)
                    mm(ps[:, 6, :], ones[:, :], tmpi[:, 0:512], start=True, stop=True).then_inc(s["arow_mm"], 1)
                    pe.wait_ge(s["qcT_ready"], here)
                    pe.wait_ge(s["kcT_ready"], here)
                    for h in range(CH):
                        last = mm(ps[:, 4, h * P:(h + 1) * P], qcT[:, h * P:(h + 1) * P], kcT[:, h * P:(h + 1) * P],
                                  start=True, stop=True)
                    last.then_inc(s["S_mm"], 1)
                    pe.wait_ge(s["qT_ready"], here)
                    pe.wait_ge(s["kT_ready"], here)
                    pe.wait_ge(s["kT_shift"], before)

                    def scores(kv):
                        for j in range(AG):
                            last = mm(ps[:, 2 + j // 2, (j % 2) * 256:(j % 2) * 256 + 256], qTs[64 * kv:64 * kv + 64, j, :],
                                      kTr[64 * kv:64 * kv + 64, :], start=True, stop=True)
                        return last
                    scores(0).then_inc(s["scores_a"], 1)
                    pe.wait_ge(s["M_ready"], here)
                    mm(ps[:, 7, 0:8], last_row, bM, start=True, stop=True).then_inc(s["bcast_mm"], 1)
                    pe.wait_ge(s["am0_ready"], here)
                    for h in range(CH):
                        last = mm(ps[:, 5 + h // 2, (h % 2) * CD1:(h % 2 + 1) * CD1], qcT[:, h * P:(h + 1) * P],
                                  CT[:, h, :], start=True, stop=True)
                    last.then_inc(s["inter_mm"], 1)
                    pe.wait_ge(s["tile_v"], tile.at("La_ready", p * NT + 1) + tile.n * t)
                    scores(1).then_inc(s["scores_mm"], 1)
                    share(1)
                    pe.wait_ge(s["Sm_ready"], here)
                    for h in range(CH):
                        last = tr(ps[:, 4, h * P:(h + 1) * P], Am[:, h * P:(h + 1) * P], ident)
                    last.then_inc(s["ST_tr"], 1)
                    pe.wait_ge(s["ST_ready"], here)
                    pe.wait_ge(s["interw_ready"], here)
                    for h in range(CH):
                        last = mm(ps[:, 5 + h // 2, (h % 2) * CD1:(h % 2 + 1) * CD1], STs[:, h * P:(h + 1) * P],
                                  z[:, t, CV0 + h * CD1:CV0 + (h + 1) * CD1], start=True, stop=True)
                    last.then_inc(s["intra_mm"], 1)
                    pe.wait_ge(s["wk_ready"], here)
                    pe.wait_ge(s["bml_ready"], here)
                    for h in range(CH):
                        last = mm(ps[:, 4 + 3 * (h // 2), (h % 2) * CD1:(h % 2 + 1) * CD1], kcs[:, h * P:(h + 1) * P],
                                  z[:, t, CV0 + h * CD1:CV0 + (h + 1) * CD1], start=True, stop=True)
                    last.then_inc(s["state_mm"], 1)
                    pe.wait_ge(s["P_exp"], here)
                    for half in range(2):
                        for i in range(8):
                            last = tr(ps[:, 2 + i // 4, (i % 4) * P:(i % 4 + 1) * P], L[:, 4 * half + i // 2, (i % 2) * P:(i % 2 + 1) * P], ident)
                        last.then_inc(s["PT_tr" if half else "PTa_tr"], 1)
                        if half == 0:
                            pe.wait_ge(s["PTa_ready"], here)
                    share(2)
                    pe.wait_ge(s["PTd_ready"], here)
                    pe.wait_ge(s["v_shift"], before)
                    for h in range(AH):
                        kv, j = h // AG, h % AG
                        o = (2 * j + kv) * AD
                        mm(ps[:, 2, o:o + AD], PT[:, 2 * h, :], vprev[:, 64 * kv:64 * kv + 64], start=True, stop=False)
                        last = mm(ps[:, 2, o:o + AD], PT[:, 2 * h + 1, :],
                                  z[:, t, V0 + 64 * kv:V0 + 64 * kv + 64], start=False, stop=True)
                    last.then_inc(s["PV_mm"], 1)
                    pe.wait_ge(s["pooled_ready"], here)
                    for c in range(4):
                        last = mm(ps[:, 3, c * P:(c + 1) * P], wpool[:, c, :], pcs[:, c * P:(c + 1) * P], start=True, stop=True)
                    last.then_inc(s["pooly_mm"], 1)
                    pe.wait_ge(s["ya_ready"], here)
                    for j in range(4):
                        last = tr(ps[:, 2, j * P:(j + 1) * P], qks[:, j * P:(j + 1) * P], ident)
                    last.then_inc(s["yaT_tr"], 1)
                pe.wait_ge(s["hy3"], p + 1)
                pe.wait_ge(s["poolT_done"], NT * (p + 1) + 1)
                pe.wait_ge(s["yaT_done"], NT * (p + 1) + 1)
                pe.wait_ge(s["nd_ready"], NT * (p + 1) + 1)
                pe.wait_ge(s["CT_ready"], NT * (p + 1) + 1)
                for t in range(NT):
                    for h in range(CH):
                        last = tr(ps[:, 2 + t, h * P:(h + 1) * P], z[:, t, CQ0 + h * P:CQ0 + (h + 1) * P], ident)
                    last.then_inc(s["hyT_tr"], 1)
                if p == PASSES - 1:
                    for h in range(CH):
                        last = tr(ps[:, 4, h * P:(h + 1) * P], CT[:, h, 0:CD], ident)
                    last.then_inc(s["state_out_tr"], 1)
                pe.wait_ge(s["ycT_done"], NT * (p + 1))
                if p == PASSES - 1:
                    pe.wait_ge(s["state_out_sb"], 1)

            def merge(p):
                rows_, tiles = tokens(p)
                tok = rows_ * tiles
                with pe.Fori(0, KC // 2) as i:
                    for k in range(6):
                        b = k % 3
                        n = p * UNITS + NZ + k
                        pe.wait_ge(w_in[k % 2], 16 * (n // 2 + 1) + 48 * i)
                        pe.wait_ge(s["gated"], 3 * KC * p + k + 1 + 6 * i)
                        wv = wbuf[:, k % 2, 0:12 * P].rearrange("p (c n) -> p c n", c=12)
                        for c in range(KC):
                            last = mm(ps[:, 2 + 2 * b, 0:tok], wv[:, c, :], xT[:, c, 0:tok], start=(c == 0), stop=(c == KC - 1))
                        last.then_inc(s["gate_mm"], 1)
                        for c in range(4):
                            last = mm(ps[:, 3 + 2 * b, 0:tok], wv[:, 8 + c, :], yT[:, 4 * b + c, 0:tok],
                                      start=(c == 0), stop=(c == 3))
                        last.then_inc(s["br_mm"], 1)
                        if p:
                            experts_block(p - 1, 1, 2 * i + k // 3, *SHARE[b])

            def output(p):
                rows_, tiles = tokens(p)
                pe.wait_ge(s["merged"], KC * (p + 1) + 1)
                with pe.Fori(0, NO // 2) as i:
                    for k in range(2):
                        n = p * UNITS + NZ + 3 * KC + k
                        pe.wait_ge(w_in[k], 16 * (n // 2 + 1) + 16 * i)
                        wv = wbuf[:, k, 0:KC * OC].rearrange("p (c n) -> p c n", c=KC)
                        for t in range(tiles):
                            pe.wait_ge(s["x2_done"], NT * NO * p + 32 - 2 * tiles + t + 1 + tiles * k + 2 * tiles * i)
                            for c in range(KC):
                                last = mm(ps[0:rows_, 2 + 2 * k + t, 0:OC], mT[:, c, t * P:t * P + rows_], wv[:, c, :],
                                          start=(c == 0), stop=(c == KC - 1))
                            last.then_inc(s["o_mm"], 1)
                pe.wait_ge(s["x2_done"], NT * NO * p + 32 + tiles * NO)

            def find(p):
                rows_, tiles = tokens(p)
                tok = rows_ * tiles
                with pe.Fori(0, PH) as h:
                    for k in range(2):
                        n = p * UNITS + NZ + 3 * KC + NO + k
                        pe.wait_ge(w_in[k], 16 * (n // 2 + 1) + 16 * h)
                        wv = wbuf[:, k, 0:KC * P].rearrange("p (c n) -> p c n", c=KC)
                        pe.wait_ge(s["q_evac"], 2 * PH * p + k + 1 + 2 * h)
                        for c in range(KC):
                            last = mm(ps[:, 2 + k, 0:tok], wv[:, c, :], xT[:, c, 0:tok], start=(c == 0), stop=(c == KC - 1))
                        last.then_inc(s["kq_mm"], 1)
                    if p:
                        experts_block(p - 1, 1, BLOCKS // 2 + h, 0, 2)
                    if p < PASSES:
                        for k in range(2):
                            pe.wait_ge(s["q_evac"], 2 * PH * p + 2 + k + 1 + 2 * h)
                            pe.wait_ge(s["s_evac"], 2 * PH * p + k + 1 + 2 * h)
                            for t in range(NT):
                                last = mm(ps[:, 4 + k, t * P:(t + 1) * P], yT[:, k, t * P:(t + 1) * P], keys[:, k, :],
                                          start=True, stop=True)
                            last.then_inc(s["s_mm"], 1)
                    if p:
                        experts_block(p - 1, 1, BLOCKS // 2 + h, 2, RING)

            def experts_begin(g, t):
                pe.wait_ge(s["y_final"], g * NT + t + 1)
                for q in range(2):
                    mm(ps[:, q, :], last_row[0:1, :], cst[0:1, 0:512], start=True, stop=True)

            def experts_block(g, t, b, first=0, last=RING):
                base = (g * NT + t) * P
                for q in range(first, last):
                    j = q % RING
                    pe.wait_ge(s["diagd"], base + q + 1 + RING * b)
                    for half in range(2):
                        done = mm(ps[:, half, :], dgs[:, j, :], ring[:, j, D + half * 512:D + (half + 1) * 512],
                                  start=False, stop=False, skip_group_check=True)
                    done.then_inc(s["slot_free"], 1)

            for p in range(PASSES):
                norm(p, 0)
                if p:
                    experts_begin(p - 1, 0)
                project(p)
                branches(p)
                if p:
                    experts_begin(p - 1, 1)
                merge(p)
                output(p)
                norm(p, 1)
                find(p)
            p = PASSES
            norm(p, 0)
            experts_begin(p - 1, 0)
            project(p)
            pe.wait_ge(s["evac_a"], NT * NZ * p + 4 + NZ)
            with pe.Fori(PRB, BLOCKS) as b:
                experts_block(p - 1, 0, b)
            pe.wait_ge(s["y_final"], NT * (p - 1) + 2)
            sample_tensor(pe)
            experts_begin(p - 1, 1)
            merge(p)
            output(p)
            norm(p, 1)
            find(p)
            pe.wait_ge(s["y_final"], NT * p + 1)
            sample_experts_tensor(pe)

        @block.scalar
        def _(act):
            f = nc.scalar.activation

            def norm(p, which):
                rows_, tiles = tokens(p)
                if which == 0:
                    act.wait_ge(s["x_in"], 16 * (p + 1))
                else:
                    act.wait_ge(s["x2_done"], NT * NO * p + 32 + tiles * NO)
                for t in range(tiles):
                    last = f(arena[0:rows_, t * D:(t + 1) * D],
                             xin[0:rows_, t, :], ACT.Square, accum_out=ssq[0:rows_, t:t + 1])
                last.then_inc(s["ssq"], 1)
                act.wait_ge(s["inv_ready"], 2 * p + which + 1)
                f(rstd[0:rows_, 0:tiles], inv4[0:rows_, 0:tiles], ACT.Sqrt).then_inc(s["rstd_ready"], 1)
                for t in range(tiles):
                    act.wait_ge(s["xs_tr"], norms(p, which, t) + 1)
                    b = 2 + 2 * t
                    f(xT[:, :, t * P:t * P + rows_].rearrange("p (a c) n -> p a c n", a=2),
                      ps[:, b:b + 2, :].rearrange("p a (c n) -> p a c n", c=4)[:, :, :, 0:rows_], ACT.Copy).then_inc(s["xT_ready"], 1)

            def project(p):
                rows_, tiles = tokens(p)
                with act.Fori(0, NZ // PRG) as i:
                    for c in range(PRG):
                        for t in range(tiles):
                            act.wait_ge(s["z_mm"], NT * NZ * p + c * tiles + t + 1 + PRG * tiles * i)
                            f(z[0:rows_, t, bass.ds(PRG * ZC * i + c * ZC, ZC)], ps[0:rows_, 2 + 2 * (c % 2) + t, 0:ZC], ACT.Copy
                              ).then_inc(s["evac_a"], 1)
                        if p:
                            experts_block(p - 1, 0, project_block(i), *project_share(c))

            def branches(p):
                act.wait_ge(s["inv40"], p + 1)
                f(r40, inv40, ACT.Sqrt).then_inc(s["r40"], 1)
                act.wait_ge(s["evac_a"], NT * NZ * (p + 1) + 4)
                f(z[:, :, CO0:CO0 + 512], z[:, :, CO0:CO0 + 512], ACT.Sigmoid).then_inc(s["co_sig"], 1)
                act.wait_ge(s["absf"], p + 1)
                f(expf, absf, ACT.Exp, scale=-1.0).then_inc(s["expf"], 1)
                act.wait_ge(s["expf"], p + 1)
                f(lnf, expf, ACT.Ln, bias=1.0).then_inc(s["lnf"], 1)
                act.wait_ge(s["qkn"], p + 1)
                act.wait_ge(s["bias_in"], 16)
                with act.Fori(0, NT) as t:
                    here, before = p * NT + 2 + t, p * NT + 1 + t

                    def share(i):
                        if p:
                            experts_block(p - 1, 0, PRB + BRB * t, *BSHARE[i])

                    act.wait_ge(s["yaT_tr"], before)
                    f(qks, z[:, t, 0:640], ACT.Copy).then_inc(s["qks_ready"], 1)
                    act.wait_ge(s["cq_tr"], before)
                    act.wait_ge(s["pooly_mm"], before)
                    f(pcs, z[:, t, PIN0:PIN0 + 1024], ACT.Copy).then_inc(s["pcs_ready"], 1)
                    act.wait_ge(s["state_mm"], before)
                    f(kcs, z[:, t, CK0:CK0 + 512], ACT.Copy, scale=float(CD) ** -0.5).then_inc(s["kcs_ready"], 1)
                    share(0)
                    act.wait_ge(s["qk_tr"], here)
                    act.wait_ge(s["scores_mm"], before)
                    f(qTs, ps[:, 2, :].rearrange("p (j n) -> p j n", j=4), ACT.Copy).then_inc(s["qT_ready"], 1)
                    act.wait_ge(s["pin_tr"], here)
                    act.wait_ge(s["hist_done"], before)
                    f(pinT[:, :, 16:16 + P], ps[:, 6, :].rearrange("p (j n) -> p j n", j=4), ACT.Copy).then_inc(s["pinT_ready"], 1)
                    act.wait_ge(s["ck_tr"], here)
                    act.wait_ge(s["S_mm"], before)
                    f(kcT, ps[:, 5, :], ACT.Copy).then_inc(s["kcT_ready"], 1)
                    share(1)
                    act.wait_ge(s["am_ready"], here)
                    f(Am, Am, ACT.Exp).then_inc(s["E_ready"], 1)
                    act.wait_ge(s["args_ready"], here)
                    act.wait_ge(s["CT_ready"], before)
                    f(exps, args, ACT.Exp).then_inc(s["exps_ready"], 1)
                    act.wait_ge(s["L_ready"], here)
                    act.wait_ge(s["arden_ready"], before)
                    f(esink, sinkd, ACT.Exp).then_inc(s["esink_ready"], 1)
                    for h in range(AH):
                        last = f(L[:, h, :], L[:, h, :], ACT.Exp, bias=negmx[:, h:h + 1], accum_out=rsum[:, h:h + 1])
                    last.then_inc(s["P_exp"], 1)
                    share(2)
                    act.wait_ge(s["PTa_tr"], here)
                    act.wait_ge(s["PV_mm"], before)
                    f(PT[:, 0:8, :], ps[:, 2:4, :].rearrange("p b (i n) -> p (b i) n", i=4), ACT.Copy).then_inc(s["PTa_ready"], 1)
                    act.wait_ge(s["yaT_tr"], here)
                    f(yT[:, 0:4, bass.ds(P * t, P)], ps[:, 2, :].rearrange("p (j n) -> p j n", j=4), ACT.Copy).then_inc(s["yaT_done"], 1)
                act.wait_ge(s["hinv"], p + 1)
                f(hr, hinv, ACT.Sqrt).then_inc(s["hr16"], 1)
                act.wait_ge(s["intra_mm"], NT * (p + 1) + 1)
                for t in range(NT):
                    act.wait_ge(s["hyT_tr"], NT * p + t + 1)
                    f(yT[:, 8:12, t * P:(t + 1) * P], ps[:, 2 + t, :].rearrange("p (j n) -> p j n", j=4), ACT.Copy).then_inc(s["ycT_done"], 1)
                if p == PASSES - 1:
                    act.wait_ge(s["state_out_tr"], 1)
                    f(state_out, ps[:, 4, :], ACT.Copy).then_inc(s["state_out_sb"], 1)

            def merge(p):
                rows_, tiles = tokens(p)
                tok = rows_ * tiles
                with act.Fori(0, KC // 2) as i:
                    for k in range(6):
                        b = k % 3
                        if p:
                            experts_block(p - 1, 1, 2 * i + k // 3, *SHARE[b])
                        act.wait_ge(s["gate_mm"], 3 * KC * p + k + 1 + 6 * i)
                        act.wait_ge(s["merged"], KC * p + k // 3 + 1 + 2 * i)
                        f(sgs[:, b, 0:tok], ps[:, 2 + 2 * b, 0:tok], ACT.Tanh, scale=0.5).then_inc(s["sig_done"], 1)

            def find(p):
                rows_, tiles = tokens(p)
                tok = rows_ * tiles
                with act.Fori(0, PH) as h:
                    if p:
                        experts_block(p - 1, 1, BLOCKS // 2 + h, 0, 2)
                    for k in range(2):
                        act.wait_ge(s["kq_mm"], 2 * PH * p + k + 1 + 2 * h)
                        if p < PASSES:
                            act.wait_ge(s["s_mm"], 2 * PH * p + k + 1 + 2 * h)
                            f(yT[:, k, :], ps[:, 2 + k, 0:TOK], ACT.Copy).then_inc(s["q_evac"], 1)
                        else:
                            f(qTsmp[:, k, bass.ds(NS * h, NS)], ps[:, 2 + k, 0:tok], ACT.Copy).then_inc(s["q_evac"], 1)
                    if p:
                        experts_block(p - 1, 1, BLOCKS // 2 + h, 2, RING)
                    if p < PASSES:
                        act.wait_ge(s["idx1"], PH * p + 1 + h)
                        for k in range(2):
                            act.wait_ge(s["s_mm"], 2 * PH * p + k + 3 + 2 * h)
                            f(ssb[:, k, :, :], ps[:, 4 + k, 0:TOK].rearrange("p (t n) -> p t n", t=NT), ACT.Copy).then_inc(s["s_evac"], 1)
                if p < PASSES:
                    act.wait_ge(s["esub"], PH * (p + 1))
                    f(gates[:, :, :], gates[:, :, :], ACT.Exp).then_inc(s["eexp"], 1)

            def experts_block(g, t, b, first=0, last=RING):
                base = (g * NT + t) * P
                for q in range(first, last, 2):
                    j = q % RING
                    act.wait_ge(s["dotted"], base + q + 3 + RING * b)
                    f(gel[:, j:j + 2], dots[:, j:j + 2], ACT.Gelu).then_inc(s["gelud"], 1)

            for p in range(PASSES):
                norm(p, 0)
                project(p)
                branches(p)
                merge(p)
                norm(p, 1)
                find(p)
            p = PASSES
            norm(p, 0)
            project(p)
            with act.Fori(PRB, BLOCKS) as b:
                experts_block(p - 1, 0, b)
            sample_scalar(act)
            merge(p)
            norm(p, 1)
            find(p)
            sample_experts_scalar(act)

        @block.vector
        def _(dve):
            v = nc.vector
            dve.memset(T[0:33, 512:520], NEG).then_inc(s["init_v"], 1)
            dve.memset(ones[:, :], 1.0)
            dve.memset(CT[:, :, :], 0.0)
            dve.memset(pmask[:, 1:NT], 0.0)
            dve.memset(pmask[:, 0:1], NEG)
            dve.memset(mprev[:, :], 0.0).then_inc(s["init_v"], 1)
            dve.wait_ge(s["init_v"], 2)
            dve.wait_ge(s["setup"], 16 * 7)
            dve.wait_ge(s["buck_mm"], 1)
            v.tensor_copy(iota16[:, :], cst[:, C_IOTA:C_IOTA + 16])
            v.tensor_copy(T[0:AH, 1024:1408], ps[0:AH, 0, 0:384]).then_inc(s["buck_sb"], 1)

            def norm(p, which):
                rows_, tiles = tokens(p)
                n = 2 * p + which + 1
                dve.wait_ge(s["ssq"], n)
                v.tensor_scalar(ms4[0:rows_, 0:tiles], ssq[0:rows_, 0:tiles], 1.0 / D, EPS, ALU.mult, ALU.add).then_inc(s["ms_ready"], 1)
                dve.wait_ge(s["ms_ready"], n)
                v.reciprocal(inv4[0:rows_, 0:tiles], ms4[0:rows_, 0:tiles]).then_inc(s["inv_ready"], 1)
                dve.wait_ge(s["rstd_ready"], n)
                dve.wait_ge(s["g_in"], 16 * n)
                if p and which == 0:
                    dve.wait_ge(s["scr_out"], 32 * p)
                for t in range(tiles):
                    v.scalar_tensor_tensor(xs[0:rows_, t, :], xin[0:rows_, t, :], rstd[0:rows_, t:t + 1], grow[0:rows_, :],
                                           ALU.mult, ALU.mult).then_inc(s["xs_ready"], 1)

            def branches(p):
                n = p + 1
                dve.wait_ge(s["evac_a"], NT * NZ * n + 4)
                sq = R[:, 0:NT * 640].rearrange("p (t n) -> p t n", t=NT)
                v.tensor_tensor(sq, z[:, :, 0:640], z[:, :, 0:640], ALU.mult).then_inc(s["stats_v"], stats.step("sq_ready"))
                dve.wait_ge(s["stats_v"], stats.at("sq_ready", p))
                v.tensor_reduce(ss40, sq.rearrange("p t (h d) -> p (t h) d", d=AD), AX.X, ALU.add).then_inc(s["stats_v"], stats.step("ss_ready"))
                dve.wait_ge(s["stats_v"], stats.at("ss_ready", p))
                v.tensor_scalar(ms40, ss40, 1.0 / AD, EPS, ALU.mult, ALU.add).then_inc(s["stats_v"], stats.step("ms40"))
                dve.wait_ge(s["stats_v"], stats.at("ms40", p))
                v.reciprocal(inv40, ms40).then_inc(s["inv40"], 1)
                g4 = gts.rearrange("p (t n) -> p t n", t=NT)
                v.tensor_tensor(g4, z[:, :, G0:G0 + 8], row[:, R_GB:R_GB + 8].unsqueeze(1).broadcast_to([P, NT, 8]), ALU.add
                                ).then_inc(s["stats_v"], stats.step("gates_in"))
                dve.wait_ge(s["stats_v"], stats.at("gates_in", p))
                v.scalar_tensor_tensor(absf.rearrange("p (t n) -> p t n", t=NT), g4[:, :, CH:2 * CH], -1.0, g4[:, :, CH:2 * CH], ALU.mult, ALU.max).then_inc(s["absf"], 1)
                v.tensor_scalar(minf.rearrange("p (t n) -> p t n", t=NT), g4[:, :, CH:2 * CH], 0.0, None, ALU.min).then_inc(s["stats_v"], stats.step("minf"))
                v.memset(z[:, :, CV0:CV0 + CH * CD1].rearrange("p t (h d) -> p t h d", h=CH)[:, :, :, CD:CD1], 1.0).then_inc(s["ones_set"], 1)
                dve.wait_ge(s["r40"], n)
                zq = z[:, :, 0:640].rearrange("p t (h d) -> p t h d", d=AD)
                for t in range(NT):
                    last = v.tensor_tensor(zq[:, t], zq[:, t], r40[:, 10 * t:10 * t + 10].unsqueeze(2).broadcast_to([P, 10, AD]), ALU.mult)
                last.then_inc(s["stats_v"], stats.step("qk_scaled"))
                dve.wait_ge(s["stats_v"], stats.at("qk_scaled", p))
                v.tensor_tensor(z[:, :, 0:640], z[:, :, 0:640], row[:, R_QK:R_QK + 640].unsqueeze(1).broadcast_to([P, NT, 640]), ALU.mult
                                ).then_inc(s["qkn"], 1)
                dve.wait_ge(s["stats_v"], stats.at("minf", p))
                dve.wait_ge(s["lnf"], n)
                v.tensor_tensor(lf, minf, lnf, ALU.subtract).then_inc(s["lf_ready"], 1)
                dve.wait_ge(s["bias_in"], 16)
                ident4 = ident.unsqueeze(1).broadcast_to([P, CH, P])
                with dve.Fori(0, NT) as t:
                    here, before = p * NT + 2 + t, p * NT + 1 + t

                    def dots(i):
                        if p:
                            experts_dots(p - 1, 0, PRB + BRB * t, *BSHARE[i])

                    def diags(i):
                        if p:
                            experts_diags(p - 1, 0, PRB + BRB * t, *BSHARE[i])

                    dots(0)
                    dve.wait_ge(s["qk_tr"], here)
                    dve.wait_ge(s["kT_shift"], before)
                    v.tensor_copy(kTr[:, P:2 * P], ps[:, 3, 0:P]).then_inc(s["kT_ready"], 1)
                    dve.wait_ge(s["cq_tr"], here)
                    dve.wait_ge(s["inter_mm"], before)
                    v.tensor_copy(qcT, ps[:, 4, :]).then_inc(s["qcT_ready"], 1)
                    diags(0)
                    dve.wait_ge(s["cs_mm"], here)
                    dve.wait_ge(s["bcast_mm"], before)
                    v.tensor_copy(bM[:, 0:CH], ps[:, 7, 0:CH]).then_inc(s["tile_v"], tile.step("b_ready"))
                    dve.wait_ge(s["tile_v"], tile.at("b_ready", p * NT + 1) + tile.n * t)
                    v.tensor_tensor(asb, gts[:, bass.ds(8 * t, CH)], bM[:, 0:CH], ALU.subtract).then_inc(s["tile_v"], tile.step("a_ready"))
                    dve.wait_ge(s["tile_v"], tile.at("a_ready", p * NT + 1) + tile.n * t)
                    dve.wait_ge(s["tile_v"], tile.at("h_ready", p * NT) + tile.n * t)
                    v.tensor_tensor(tmpi[:, 0:512].rearrange("p (h n) -> p h n", h=CH), ident4, asb.unsqueeze(2).broadcast_to([P, CH, P]),
                                    ALU.mult).then_inc(s["diag_ready"], 1)
                    dots(1)
                    Am4 = Am.rearrange("p (h n) -> p h n", h=CH)
                    dve.wait_ge(s["arow_mm"], here)
                    dve.wait_ge(s["ST_tr"], before)
                    v.tensor_tensor(Am4, ps[:, 6, :].rearrange("p (h n) -> p h n", h=CH), cmask.unsqueeze(1).broadcast_to([P, CH, P]),
                                    ALU.add).then_inc(s["am0_ready"], 1)
                    dve.wait_ge(s["am0_ready"], here)
                    v.tensor_reduce(rmax, Am4, AX.X, ALU.max).then_inc(s["tile_v"], tile.step("rmax_ready"))
                    dve.wait_ge(s["tile_v"], tile.at("rmax_ready", p * NT + 1) + tile.n * t)
                    dve.wait_ge(s["tile_v"], tile.at("m_new", p * NT) + tile.n * t)
                    v.tensor_tensor(bM[:, CH:2 * CH], rmax, mprev[:, :], ALU.max).then_inc(s["M_ready"], 1)
                    dve.wait_ge(s["M_ready"], here)
                    v.tensor_tensor(Am4, Am4, bM[:, CH:2 * CH].unsqueeze(2).broadcast_to([P, CH, P]), ALU.subtract).then_inc(s["am_ready"], 1)
                    dve.wait_ge(s["exps_ready"], before)
                    v.tensor_tensor(args[:, 0:4], mprev[:, :], bM[:, CH:2 * CH], ALU.subtract)
                    v.scalar_tensor_tensor(args[:, 4:8], bM[:, 0:CH], -1.0, bM[:, CH:2 * CH], ALU.mult, ALU.subtract)
                    diags(1)
                    dve.wait_ge(s["bcast_mm"], here)
                    v.tensor_copy(bml, ps[:, 7, 0:8]).then_inc(s["bml_ready"], 1)
                    dve.wait_ge(s["bml_ready"], here)
                    v.tensor_tensor(args[:, 8:12], mprev[:, :], bml[:, 4:8], ALU.subtract)
                    v.tensor_tensor(args[:, 12:16], asb, bml[:, 4:8], ALU.subtract).then_inc(s["args_ready"], 1)
                    dve.wait_ge(s["args_ready"], here)
                    v.tensor_tensor(mprev[:, :], bml[:, 0:4], bml[:, 4:8], ALU.add).then_inc(s["tile_v"], tile.step("m_new"))
                    dve.wait_ge(s["scores_a"], here)
                    dve.wait_ge(s["PT_tr"], before)
                    v.scalar_tensor_tensor(R[:, 0:1024], psf[:, 1024:2048], float(AD) ** -0.5, bias[:, 0:1024], ALU.mult, ALU.add
                                           ).then_inc(s["tile_v"], tile.step("La_ready"))
                    dve.wait_ge(s["S_mm"], here)
                    dve.wait_ge(s["E_ready"], here)
                    v.tensor_tensor(Am, ps[:, 4, :], Am, ALU.mult).then_inc(s["Sm_ready"], 1)
                    dve.wait_ge(s["exps_ready"], here)
                    dve.wait_ge(s["ck_tr"], here)
                    kc4 = kcs.rearrange("p (h n) -> p h n", h=CH)
                    v.tensor_tensor(kc4, kc4, exps[:, 12:16].unsqueeze(2).broadcast_to([P, CH, P]), ALU.mult).then_inc(s["wk_ready"], 1)
                    dve.wait_ge(s["scores_mm"], here)
                    v.scalar_tensor_tensor(R[:, 1024:2048], psf[:, 1024:2048], float(AD) ** -0.5, bias[:, 1024:2048], ALU.mult, ALU.add
                                           ).then_inc(s["tile_v"], 1 if p == 0 else 2)
                    dve.wait_ge(s["tile_v"], tile.at("L0_ready", p * NT + 1) + tile.n * t)
                    if p == 0:
                        v.tensor_scalar(L[:, :, 0:P], L[:, :, 0:P], pmask[:, bass.ds(t, 1)], None, ALU.add).then_inc(s["tile_v"], tile.step("L1_ready"))
                        dve.wait_ge(s["tile_v"], tile.at("L1_ready", p * NT + 1) + tile.n * t)
                    v.tensor_reduce(mx8, L, AX.X, ALU.max).then_inc(s["tile_v"], tile.step("mx_ready"))
                    dve.wait_ge(s["tile_v"], tile.at("mx_ready", p * NT + 1) + tile.n * t)
                    v.tensor_tensor(mxs, mx8, row[:, R_SINK:R_SINK + 8], ALU.max).then_inc(s["tile_v"], tile.step("mx2_ready"))
                    dve.wait_ge(s["tile_v"], tile.at("mx2_ready", p * NT + 1) + tile.n * t)
                    dve.wait_ge(s["P_exp"], before)
                    v.tensor_scalar(negmx, mxs, -1.0, None, ALU.mult)
                    v.tensor_tensor(sinkd, row[:, R_SINK:R_SINK + 8], mxs, ALU.subtract).then_inc(s["L_ready"], 1)
                    dve.wait_ge(s["inter_mm"], here)
                    tmp4 = tmpi.rearrange("p (a h n) -> p a h n", a=2, h=2)
                    num56 = ps[:, 5:7, 0:2 * CD1].rearrange("p a (h n) -> p a h n", h=2)
                    v.tensor_tensor(tmp4, num56, exps[:, 0:4].rearrange("p (a h) -> p a h", a=2).unsqueeze(3).broadcast_to([P, 2, 2, CD1]),
                                    ALU.mult).then_inc(s["interw_ready"], 1)
                    dve.wait_ge(s["ST_tr"], here)
                    dve.wait_ge(s["intra_mm"], before)
                    v.tensor_copy(STs, ps[:, 4, :]).then_inc(s["ST_ready"], 1)
                    dots(2)
                    dve.wait_ge(s["intra_mm"], here)
                    dve.wait_ge(s["interw_ready"], here)
                    v.tensor_tensor(tmp4, num56, tmp4, ALU.add).then_inc(s["nd_ready"], 1)
                    dve.wait_ge(s["nd_ready"], here)
                    nd = tmpi.rearrange("p (h n) -> p h n", h=CH)
                    v.scalar_tensor_tensor(dn.unsqueeze(2), nd[:, :, CD:CD1], -1.0, nd[:, :, CD:CD1], ALU.mult, ALU.max
                                           ).then_inc(s["tile_v"], tile.step("den_abs"))
                    dve.wait_ge(s["tile_v"], tile.at("den_abs", p * NT + 1) + tile.n * t)
                    v.tensor_tensor(dn, dn, exps[:, 4:8], ALU.max).then_inc(s["tile_v"], tile.step("den_ready"))
                    dve.wait_ge(s["tile_v"], tile.at("den_ready", p * NT + 1) + tile.n * t)
                    v.reciprocal(rd, dn).then_inc(s["tile_v"], tile.step("h_done"))
                    dve.wait_ge(s["tile_v"], tile.at("h_done", p * NT + 1) + tile.n * t)
                    v.tensor_tensor(z[:, t, CQ0:CQ0 + 512].rearrange("p (h n) -> p h n", h=CH), nd[:, :, 0:CD],
                                    rd.unsqueeze(2).broadcast_to([P, CH, CD]), ALU.mult).then_inc(s["tile_v"], tile.step("h_ready"))
                    diags(2)
                    dve.wait_ge(s["state_mm"], here)
                    for h in range(CH):
                        last = v.scalar_tensor_tensor(CT[:, h, :], CT[:, h, :], exps[:, 8 + h:9 + h],
                                                      ps[:, 4 + 3 * (h // 2), (h % 2) * CD1:(h % 2 + 1) * CD1], ALU.mult, ALU.add)
                    last.then_inc(s["CT_ready"], 1)
                    dve.wait_ge(s["PT_tr"], here)
                    dve.wait_ge(s["PV_mm"], before)
                    v.tensor_copy(R[:, 3072:4096], psf[:, 1024:2048]).then_inc(s["PTd_ready"], 1)
                    dve.wait_ge(s["P_exp"], here)
                    v.tensor_tensor(aden, rsum, esink, ALU.add).then_inc(s["tile_v"], tile.step("aden_ready"))
                    dve.wait_ge(s["tile_v"], tile.at("aden_ready", p * NT + 1) + tile.n * t)
                    v.reciprocal(arden, aden).then_inc(s["arden_ready"], 1)
                    dve.wait_ge(s["arden_ready"], here)
                    dve.wait_ge(s["PV_mm"], here)
                    v.tensor_tensor(qks[:, 0:512].rearrange("p (j k n) -> p k j n", k=AKV, n=AD),
                                    ps[:, 2, :].rearrange("p (j k n) -> p k j n", k=AKV, n=AD),
                                    arden.rearrange("p (k j) -> p k j", k=AKV).unsqueeze(3).broadcast_to([P, AKV, AG, AD]), ALU.mult).then_inc(s["ya_ready"], 1)
                    dve.wait_ge(s["pooly_mm"], here)
                    v.tensor_tensor(yT[:, 4:8, bass.ds(P * t, P)], ps[:, 3, :].rearrange("p (h n) -> p h n", h=4),
                                    col[:, 0:4].unsqueeze(2).broadcast_to([P, 4, P]), ALU.mult).then_inc(s["poolT_done"], 1)
                if p:
                    experts_end(p - 1, 0)
                hz = z[:, :, CQ0:CQ0 + 512]
                dve.wait_ge(s["tile_v"], tile.at("h_ready", NT * n))
                dve.wait_ge(s["PV_mm"], NT * n + 1)
                hs = R[:, 0:NT * 512].rearrange("p (t n) -> p t n", t=NT)
                v.tensor_tensor(hs, hz, hz, ALU.mult).then_inc(s["stats_v"], stats.step("hsq"))
                dve.wait_ge(s["stats_v"], stats.at("hsq", p))
                v.tensor_reduce(hss, hs.rearrange("p t (h d) -> p (t h) d", d=CD), AX.X, ALU.add).then_inc(s["stats_v"], stats.step("hss"))
                dve.wait_ge(s["stats_v"], stats.at("hss", p))
                v.tensor_scalar(hms, hss, 1.0 / CD, EPS, ALU.mult, ALU.add).then_inc(s["stats_v"], stats.step("hms"))
                dve.wait_ge(s["stats_v"], stats.at("hms", p))
                v.reciprocal(hinv, hms).then_inc(s["hinv"], 1)
                dve.wait_ge(s["co_sig"], n)
                v.tensor_tensor(hz, hz, z[:, :, CO0:CO0 + 512], ALU.mult).then_inc(s["stats_v"], stats.step("hy1"))
                dve.wait_ge(s["stats_v"], stats.at("hy1", p))
                hz4 = hz.rearrange("p t (h d) -> p t h d", h=CH)
                for t in range(NT):
                    last = v.tensor_tensor(hz4[:, t], hz4[:, t], row[:, R_HN:R_HN + CD].unsqueeze(1).broadcast_to([P, CH, CD]), ALU.mult)
                last.then_inc(s["stats_v"], stats.step("hy2"))
                dve.wait_ge(s["stats_v"], stats.at("hy2", p))
                dve.wait_ge(s["hr16"], n)
                for t in range(NT):
                    last = v.tensor_tensor(hz4[:, t], hz4[:, t], hr[:, CH * t:CH * t + CH].unsqueeze(2).broadcast_to([P, CH, CD]), ALU.mult)
                last.then_inc(s["hy3"], 1)

            def merge(p):
                rows_, tiles = tokens(p)
                tok = rows_ * tiles
                if p < PASSES:
                    dve.wait_ge(s["ycT_done"], NT * (p + 1))
                if p == PASSES:
                    dve.wait_ge(s["state_c_stored"], 16 * 4)
                with dve.Fori(0, KC // 2) as i:
                    for k in range(6):
                        b = k % 3
                        n = 3 * KC * p + k
                        if p:
                            experts_block(p - 1, 1, 2 * i + k // 3, *SHARE[b])
                        dve.wait_ge(s["sig_done"], n + 1 + 6 * i)
                        dve.wait_ge(s["br_mm"], n + 1 + 6 * i)
                        v.scalar_tensor_tensor(sgs[:, b, 0:tok], sgs[:, b, 0:tok], 1.0, ps[:, 3 + 2 * b, 0:tok], ALU.add, ALU.mult).then_inc(s["gated"], 1)
                        if b:
                            dve.wait_ge(s["gated"], n + 4 + 6 * i)
                        if b == 1:
                            v.tensor_tensor(pr[:, 0:tok], sgs[:, 0, 0:tok], sgs[:, 1, 0:tok], ALU.add).then_inc(s["prod"], 1)
                        if b == 2:
                            dve.wait_ge(s["prod"], KC * p + k // 3 + 1 + 2 * i)
                            v.tensor_tensor(mT[:, bass.ds(2 * i + k // 3, 1), 0:tok].rearrange("p a n -> p (a n)"), pr[:, 0:tok], sgs[:, 2, 0:tok], ALU.add
                                            ).then_inc(s["merged"], 1)

            def output(p):
                rows_, tiles = tokens(p)
                with dve.Fori(0, NO // 2) as i:
                    for k in range(2):
                        for t in range(tiles):
                            dve.wait_ge(s["o_mm"], NT * NO * p + k * tiles + t + 1 + 2 * tiles * i)
                            o = xin[0:rows_, t, bass.ds(2 * OC * i + k * OC, OC)]
                            v.scalar_tensor_tensor(o, ps[0:rows_, 2 + 2 * k + t, 0:OC], 0.5, o, ALU.mult, ALU.add).then_inc(s["x2_done"], 1)

            def topk(n, side_in, side_rep, rows_, tiles, e, experts):
                pairs = [(k, t) for k in range(2) for t in range(tiles)]
                vv = v16[0:rows_, 0:2 * tiles * 16].rearrange("p (k t n) -> p k t n", k=2, t=tiles)
                ii = i16[0:rows_, 0:2 * tiles * 16].rearrange("p (k t n) -> p k t n", k=2, t=tiles)
                fi = f16[0:rows_, 0:2 * tiles * 16].rearrange("p (k t n) -> p k t n", k=2, t=tiles)
                for k, t in pairs:
                    last = v.max(vv[:, k, t, 0:8], side_in[0:rows_, k, t, :])
                last.then_inc(s["topk_v"], find_steps.step("top1"))
                hold(dve, s["topk_v"], find_steps.at("top1", n - 1))
                for k, t in pairs:
                    last = v.match_replace(side_rep[0:rows_, k, t, :], vv[:, k, t, 0:8], side_in[0:rows_, k, t, :], LOWEST)
                last.then_inc(s["topk_v"], find_steps.step("rep1"))
                for k, t in pairs:
                    last = v.max_index(ii[:, k, t, 0:8], vv[:, k, t, 0:8], side_in[0:rows_, k, t, :])
                last.then_inc(s["idx1"], 1)
                hold(dve, s["topk_v"], find_steps.at("rep1", n - 1))
                for k, t in pairs:
                    last = v.max(vv[:, k, t, 8:16], side_rep[0:rows_, k, t, :])
                last.then_inc(s["topk_v"], find_steps.step("top2"))
                hold(dve, s["topk_v"], find_steps.at("top2", n - 1))
                for k, t in pairs:
                    last = v.max_index(ii[:, k, t, 8:16], vv[:, k, t, 8:16], side_rep[0:rows_, k, t, :])
                last.then_inc(s["topk_v"], find_steps.step("idx2"))
                cd = cand[0:rows_, 0:tiles * 256].rearrange("p (t n) -> p t n", t=tiles)
                cr = crep[0:rows_, 0:tiles * 256].rearrange("p (t n) -> p t n", t=tiles)
                for t in range(tiles):
                    last = v.tensor_tensor(cd[:, t].rearrange("p (a b) -> p a b", a=16), vv[:, 0, t].unsqueeze(2).broadcast_to([rows_, 16, 16]),
                                           vv[:, 1, t].unsqueeze(1).broadcast_to([rows_, 16, 16]), ALU.add)
                last.then_inc(s["topk_v"], find_steps.step("cand"))
                dve.wait_ge(s["topk_v"], find_steps.at("idx2", n - 1))
                v.tensor_copy(fi, ii).then_inc(s["topk_v"], find_steps.step("idxf"))
                tv = v16[0:rows_, 128:128 + tiles * 16].rearrange("p (t n) -> p t n", t=tiles)
                tp = i16[0:rows_, 128:128 + tiles * 16].rearrange("p (t n) -> p t n", t=tiles)
                hold(dve, s["topk_v"], find_steps.at("cand", n - 1))
                for t in range(tiles):
                    last = v.max(tv[:, t, 0:8], cd[:, t])
                last.then_inc(s["topk_v"], find_steps.step("ctop1"))
                hold(dve, s["topk_v"], find_steps.at("ctop1", n - 1))
                for t in range(tiles):
                    last = v.match_replace(cr[:, t], tv[:, t, 0:8], cd[:, t], LOWEST)
                last.then_inc(s["topk_v"], find_steps.step("crep"))
                for t in range(tiles):
                    last = v.max_index(tp[:, t, 0:8], tv[:, t, 0:8], cd[:, t])
                last.then_inc(s["topk_v"], find_steps.step("cidx1"))
                hold(dve, s["topk_v"], find_steps.at("crep", n - 1))
                for t in range(tiles):
                    last = v.max(tv[:, t, 8:16], cr[:, t])
                last.then_inc(s["topk_v"], find_steps.step("ctop2"))
                hold(dve, s["topk_v"], find_steps.at("ctop2", n - 1))
                for t in range(tiles):
                    last = v.max_index(tp[:, t, 8:16], tv[:, t, 8:16], cr[:, t])
                last.then_inc(s["topk_v"], find_steps.step("cidx2"))
                v.tensor_tensor(e, tv, tv[:, :, 0:1].broadcast_to([rows_, tiles, 16]), ALU.subtract).then_inc(s["esub"], 1)
                m = tiles * 16
                tpf = i16[0:rows_, 128:128 + m]
                dve.wait_ge(s["topk_v"], find_steps.at("cidx2", n - 1))
                v.tensor_scalar(pab[0:rows_, 0, 0:m], tpf, 4, None, ALU.logical_shift_right)
                v.tensor_scalar(pab[0:rows_, 1, 0:m], tpf, 15, None, ALU.bitwise_and).then_inc(s["topk_v"], find_steps.step("pos_ab"))
                dve.wait_ge(s["topk_v"], find_steps.at("pos_ab", n - 1))
                v.tensor_copy(pabf[0:rows_, :, 0:m], pab[0:rows_, :, 0:m]).then_inc(s["topk_v"], find_steps.step("pos_f"))
                dve.wait_ge(s["topk_v"], find_steps.at("pos_f", n - 1))
                dve.wait_ge(s["topk_v"], find_steps.at("idxf", n - 1))
                eqs = [cand.bitcast(BF16), crep.bitcast(BF16)]
                for k in range(2):
                    eq = eqs[k][0:rows_, 0:m * 16].rearrange("p (m a) -> p m a", a=16)
                    last = v.tensor_tensor(eq, pabf[0:rows_, k, 0:m].unsqueeze(2).broadcast_to([rows_, m, 16]),
                                           iota16[0:rows_, :].unsqueeze(1).broadcast_to([rows_, m, 16]), ALU.is_equal)
                last.then_inc(s["topk_v"], find_steps.step("eq_a"))
                dve.wait_ge(s["topk_v"], find_steps.at("eq_a", n - 1))
                for k in range(2):
                    for t in range(tiles):
                        eq = eqs[k][0:rows_, t * 256:(t + 1) * 256].rearrange("p (m a) -> p m a", a=16)
                        last = v.tensor_tensor(eq, eq, fi[:, k, t].unsqueeze(1).broadcast_to([rows_, 16, 16]), ALU.mult)
                last.then_inc(s["topk_v"], find_steps.step("eq_ab"))
                dve.wait_ge(s["topk_v"], find_steps.at("eq_ab", n - 1))
                for k in range(2):
                    eq = eqs[k][0:rows_, 0:m * 16].rearrange("p (m a) -> p m a", a=16)
                    last = v.tensor_reduce(eab[0:rows_, k, 0:m], eq, AX.X, ALU.add)
                last.then_inc(s["topk_v"], find_steps.step("e_a"))
                dve.wait_ge(s["topk_v"], find_steps.at("e_a", n - 1))
                v.scalar_tensor_tensor(eab[0:rows_, 2, 0:m], eab[0:rows_, 0, 0:m], float(NKEY), eab[0:rows_, 1, 0:m],
                                       ALU.mult, ALU.add).then_inc(s["topk_v"], find_steps.step("e_ab"))
                dve.wait_ge(s["topk_v"], find_steps.at("e_ab", n - 1))
                v.tensor_copy(experts, eab[0:rows_, 2, 0:m].rearrange("p (t n) -> p t n", t=tiles)).then_inc(s["gate_ready"], 1)

            def softmax(p, g, m, rows_, sem, steps, rounds, names):
                dve.wait_ge(s["eexp"], p + 1)
                g = g.rearrange("p (m k) -> p m k", k=PK)
                v.tensor_reduce(esm[0:rows_, 0:m], g, AX.X, ALU.add).then_inc(sem, steps.step(names[0]))
                dve.wait_ge(sem, steps.at(names[0], rounds))
                v.reciprocal(esr[0:rows_, 0:m], esm[0:rows_, 0:m]).then_inc(sem, steps.step(names[1]))
                dve.wait_ge(sem, steps.at(names[1], rounds))
                v.tensor_tensor(g, g, esr[0:rows_, 0:m].unsqueeze(2).broadcast_to([rows_, m, PK]), ALU.mult).then_inc(s["gate_ready"], 1)

            def find(p):
                with dve.Fori(0, PH) as h:
                    if p:
                        experts_block(p - 1, 1, BLOCKS // 2 + h)
                    dve.wait_ge(s["gate_ready"], (PH + 1) * p + 1 + h)
                    hold(dve, s["s_evac"], 2 * PH * p + 4 + 2 * h)
                    head = bass.ds(PK * h, PK)
                    topk(PH * p + 1 + h, ssb, srep, P, NT, gates[:, :, head], eidx[:, :, head])
                softmax(p, gates[:, :, :].rearrange("p t n -> p (t n)"), NT * PH, P, s["stats_v"], stats, p, ("esum", "erec"))

            def experts_begin(g, t):
                n = g * NT + t
                dve.wait_ge(s["gate_ready"], (PH + 1) * (g + 1) + 1)
                if n:
                    dve.wait_ge(s["diagd"], n * P)
                v.tensor_copy(gcur[:, :], gates[:, t, :]).then_inc(s["gcur_ready"], 1)
                dve.wait_ge(s["gcur_ready"], n + 1)
                dve.wait_ge(s["cur_in"], 16 * (n + 1))

            def experts_block(g, t, b, first=0, last=RING):
                base = (g * NT + t) * P
                for q in range(first, last, 2):
                    experts_dots(g, t, b, q, q + 2)
                    experts_diags(g, t, b, q, q + 2)

            def experts_dots(g, t, b, first, last):
                base = (g * NT + t) * P
                for q in range(first, last):
                    j = q % RING
                    dve.wait_ge(got[j], 16 * (base // RING + q // RING + 1) + 16 * b)
                    v.tensor_tensor_reduce(ring[:, j, 0:D], ring[:, j, 0:D], xcur, 1.0, 0.0, ALU.mult, ALU.add,
                                           dots[:, j:j + 1]).then_inc(s["dotted"], 1)

            def experts_diags(g, t, b, first, last):
                base = (g * NT + t) * P
                for q in range(first, last):
                    j = q % RING
                    if q % 2 == 0:
                        dve.wait_ge(s["gelud"], base // 2 + q // 2 + 1 + RING // 2 * b)
                        dve.wait_ge(s["slot_free"], base + q + 2 + RING * b)
                    v.tensor_scalar(dgs[:, j, :], ident, gel[:, j:j + 1], gcur[:, bass.ds(RING * b + q, 1)],
                                    ALU.mult, ALU.mult).then_inc(s["diagd"], 1)

            def experts_end(g, t):
                n = g * NT + t
                dve.wait_ge(s["slot_free"], RING + P * (n + 1))
                dve.wait_ge(s["res_in"], 16 * (n + 1))
                v.tensor_tensor(xres, psf[:, 0:D], xres, ALU.add).then_inc(s["y_final"], 1)

            for p in range(PASSES):
                norm(p, 0)
                if p:
                    experts_begin(p - 1, 0)
                    with dve.Fori(0, PRB) as b:
                        experts_block(p - 1, 0, b)
                branches(p)
                if p:
                    experts_begin(p - 1, 1)
                merge(p)
                output(p)
                norm(p, 1)
                if p:
                    dve.wait_ge(s["ecur_ready"], NT * p)
                    dve.wait_ge(s["gcur_ready"], NT * p)
                find(p)
                if p:
                    experts_end(p - 1, 1)
            p = PASSES
            norm(p, 0)
            experts_begin(p - 1, 0)
            with dve.Fori(0, BLOCKS) as b:
                experts_block(p - 1, 0, b)
            experts_end(p - 1, 0)
            sample_vector(dve)
            experts_begin(p - 1, 1)
            merge(p)
            output(p)
            norm(p, 1)
            with dve.Fori(0, PH) as h:
                experts_block(p - 1, 1, BLOCKS // 2 + h)
            experts_end(p - 1, 1)
            dve.wait_ge(s["ecur_ready"], NT * p)
            sample_experts_vector(dve, topk, softmax)

        @block.gpsimd
        def _(pool):
            for n in STEPS:
                pool.sem_inc(s[n], 1)
            for n, k in PRIMED.items():
                pool.sem_inc(s[n], k)
            g = nc.gpsimd
            g.memset(kTr[:, 0:P], 0.0)
            g.memset(vprev[:, :], 0.0)
            g.memset(pinT[:, :, 0:16], 0.0)
            for c, w in enumerate(POOLW):
                last = g.memset(tab[:, c, :], 1.0 / w)
            last.then_inc(s["init_p"], 1)
            pool.wait_ge(s["init_p"], 1)
            pool.wait_ge(s["setup"], 16 * 7)
            g.tensor_copy(tab[:, :, 0:16], cst[:, C_CNT:C_CNT + 64].rearrange("p (c n) -> p c n", c=4)).then_inc(s["init_p"], 1)
            pool.wait_ge(s["init_p"], 2)

            def pool_tile(p, t):
                here, before = p * NT + 2 + t, p * NT + 1 + t
                pool.wait_ge(s["pinT_ready"], here)
                g.tensor_tensor(pA[:, :, 2:144], pinT[:, :, 2:144], pinT[:, :, 1:143], ALU.add).then_inc(s["pool_p"], pooling.step("sum2"))
                pool.wait_ge(s["pool_p"], pooling.at("sum2", p * NT) + pooling.n * t)
                g.tensor_tensor(pB[:, 1:4, 4:144], pA[:, 1:4, 4:144], pA[:, 1:4, 2:142], ALU.add).then_inc(s["pool_p"], pooling.step("sum4"))
                pool.wait_ge(s["pool_p"], pooling.at("sum4", p * NT) + pooling.n * t)
                g.tensor_tensor(pA[:, 2:4, 8:144], pB[:, 2:4, 8:144], pB[:, 2:4, 4:140], ALU.add).then_inc(s["pool_p"], pooling.step("sum8"))
                pool.wait_ge(s["pool_p"], pooling.at("sum8", p * NT) + pooling.n * t)
                g.tensor_tensor(pB[:, 3:4, 16:144], pA[:, 3:4, 16:144], pA[:, 3:4, 8:136], ALU.add).then_inc(s["pool_p"], pooling.step("sum16"))
                pool.wait_ge(s["pool_p"], pooling.at("sum16", p * NT) + pooling.n * t)
                g.tensor_tensor(pA[:, 0:4:2, 16:144], pA[:, 0:4:2, 16:144], tab[:, 0:4:2, :], ALU.mult)
                g.tensor_tensor(pB[:, 1:4:2, 16:144], pB[:, 1:4:2, 16:144], tab[:, 1:4:2, :], ALU.mult).then_inc(s["pool_p"], pooling.step("scaled"))
                pool.wait_ge(s["pool_p"], pooling.at("scaled", p * NT) + pooling.n * t)
                pool.wait_ge(s["pin_tr"], here)
                po = pcs[:, 0:512].rearrange("p (c n) -> p c n", c=4)
                g.tensor_tensor(po[:, 0:4:2, :], pA[:, 0:4:2, 16:144], pinT[:, 0:4:2, 16:144], ALU.subtract)
                g.tensor_tensor(po[:, 1:4:2, :], pB[:, 1:4:2, 16:144], pinT[:, 1:4:2, 16:144], ALU.subtract).then_inc(s["pooled_ready"], 1)
                hold(pool, s["pooled_ready"], here)
                g.tensor_copy(tab[:, :, 0:16], tab[:, :, 16:32])
                g.tensor_copy(pinT[:, :, 1:16], pinT[:, :, 129:144]).then_inc(s["hist_done"], 1)
                pool.wait_ge(s["hist_done"], here)
                hold(pool, s["scores_mm"], here)
                g.tensor_copy(kTr[:, 0:P], kTr[:, P:2 * P]).then_inc(s["kT_shift"], 1)
                hold(pool, s["PV_mm"], here)
                g.tensor_copy(vprev[:, :], z[:, t, V0:V0 + P]).then_inc(s["v_shift"], 1)

            def copies(n):
                return (PRB // 2 + PH) * (n // NT) + PRB // 2 * (n % NT)

            def experts_begin(n):
                pool.wait_ge(s["gate_ready"], (PH + 1) * (n // NT + 1) + 1)
                if n:
                    pool.wait_ge(s["idx_slot"], copies(n))
                if n % NT:
                    pool.wait_ge(s["dotted"], n * P + 1)
                g.tensor_copy(ecur[:, :], eidx[:, n % NT, :]).then_inc(s["ecur_ready"], 1)
                pool.wait_ge(s["ecur_ready"], n + 1)

            def experts_gather(n, i, first, last):
                for q in range(first, last):
                    b, j = q // PK, q % PK
                    if j == 0:
                        g.tensor_copy(islot[:, b * PK:(b + 1) * PK], ecur[:, bass.ds(2 * PK * i + b * PK, PK)]).then_inc(s["idx_slot"], 1)
                        pool.wait_ge(s["idx_slot"], copies(n) + b + 1 + 2 * i)
                    hold(pool, s["slot_free"], n * P + q + 1 + 2 * PK * i)
                    g.indirect_dma_start(ring[:, q % RING, :], None, uv,
                                         bass.IndirectOffsetOnAxis(ap=islot[:, q:q + 1], axis=0)).then_inc(got[q % RING], 16)

            def experts_tile(n, slots):
                experts_begin(n)
                with pool.Fori(0, slots // (2 * PK)) as i:
                    experts_gather(n, i, 0, 2 * PK)
                if slots % (2 * PK):
                    experts_gather(n, slots // (2 * PK), 0, slots % (2 * PK))

            def experts_blocks(n, t):
                for q in range((PRB + BRB * t) * RING, (PRB + BRB * (t + 1)) * RING):
                    hold(pool, s["slot_free"], n * P + q + 1)
                    g.indirect_dma_start(ring[:, q % RING, :], None, uv,
                                         bass.IndirectOffsetOnAxis(ap=ecur[:, q:q + 1], axis=0)).then_inc(got[q % RING], 16)

            for p in range(PASSES + 1):
                n = NT * (p - 1)
                if p:
                    experts_tile(n, PRB * RING)
                for t in range(NT):
                    if p:
                        experts_blocks(n, t)
                    if p < PASSES:
                        pool_tile(p, t)
                if p:
                    experts_tile(n + 1, P)
            sample_gpsimd(pool)


def kernel(x_prompt, x_sample, cache_k, cache_v, state_pool, state_mlstm_c, state_mlstm_n, state_mlstm_m, rel_bias,
           norm1_g, w_in, q_norm_g, k_norm_g, attn_sink, w_pool, pool_scale, b_igate, b_fgate, h_norm_g,
           w_br_a, w_br_b, w_br_c, w_out, norm2_g, peer_wq, peer_k1, peer_k2, peer_u, peer_v):
    import concourse.bacc as bacc
    from concourse.bass_utils import run_bass_kernel_spmd

    a = np.ascontiguousarray
    f = np.float32

    C = np.zeros((P, C_ALL), f)
    r = np.arange(P)
    C[:, C_ID:C_ID + P] = np.eye(P)
    C[:, C_TRI:C_TRI + P] = r[:, None] <= r[None, :]
    C[:, C_MASK:C_MASK + P] = np.where(r[None, :] <= r[:, None], 0.0, NEG)
    C[P - 1, C_LAST:C_LAST + P] = 1.0
    C[:, C_IOTA:C_IOTA + 16] = np.arange(16)
    for c, w in enumerate(POOLW):
        C[:, C_CNT + 16 * c:C_CNT + 16 * (c + 1)] = 1.0 / np.minimum(np.arange(16) + 1, w).astype(f)
    exact = 16
    d = np.arange(W)
    large = exact + (np.log(np.maximum(d, 1).astype(f) / f(exact)) / f(math.log(128 / exact)) * f(32 - exact)).astype(np.int32)
    bucket = np.where(d < exact, d, np.minimum(large, 31))
    for i in range(384):
        dist = 255 - i
        C[bucket[dist] if 0 <= dist < W else 32, C_BUCK + i] = 1.0
    for i in range(W):
        C[bucket[W - 1 - i], C_SBUCK + i] = 1.0
    selmat = np.zeros((64, NS + 64), f)
    for h in range(PH):
        for n in range(NS):
            selmat[h * NS + n, n] = 1.0
            selmat[n, NS + h * NS + n] = 1.0

    perm = np.array([kv * AG + j for j in range(AG) for kv in range(AKV)])
    w1 = np.asarray(w_in)[0]
    pts = np.cumsum([512, 128, 128, 512, 512, 512, 512, 4, 4, 512, 1024, 1024, 1024])
    aq, ak, av, pin, cq, ck, cv, ci, cf, co, ga, gb, gc = np.split(w1, pts[:-1], axis=1)
    aq = aq.reshape(D, AH, AD)[:, perm].reshape(D, 512)
    cv = np.concatenate([cv.reshape(D, CH, CD), np.zeros((D, CH, 1), f)], 2).reshape(D, CH * CD1)
    wz = np.concatenate([aq, ak, av, ci, cf, pin, cq, ck, co, cv], 1)
    wz = np.concatenate([wz, np.zeros((D, ZW - wz.shape[1]), f)], 1)
    wz = a(wz.reshape(KC, P, NZ, ZC).transpose(2, 1, 0, 3)).reshape(NZ, P, KC * ZC)
    bra = np.asarray(w_br_a)[0].reshape(AH, AD, D)[perm].reshape(512, D)
    parts = []
    for gw, bw in ((ga, bra), (gb, np.asarray(w_br_b)[0]), (gc, np.asarray(w_br_c)[0])):
        parts.append(np.concatenate([gw, bw], 0).reshape(12, P, KC, P).transpose(2, 1, 0, 3))
    wm = a(np.stack(parts, 1)).reshape(3 * KC, P, 12 * P)
    wo = a(np.asarray(w_out)[0].reshape(KC, P, NO, OC).transpose(2, 1, 0, 3)).reshape(NO, P, KC * OC)
    wq = a(np.asarray(peer_wq)[0].reshape(KC, P, 2 * PH, P).transpose(2, 1, 0, 3)).reshape(2 * PH, P, KC * P)
    uv = np.concatenate([np.asarray(peer_u)[0], np.asarray(peer_v)[0]], 1)

    rel_bias = np.asarray(rel_bias)
    sink = np.asarray(attn_sink)[0]
    rows = np.concatenate([np.tile(np.asarray(q_norm_g)[0], AH), np.tile(np.asarray(k_norm_g)[0], AKV), np.asarray(h_norm_g)[0],
                           np.asarray(b_igate)[0], np.asarray(b_fgate)[0], sink])[None]
    cols = np.zeros((P, 8), f)
    cols[:, 0:4] = np.asarray(pool_scale)[0].reshape(4, P).T
    cols[:, 4] = np.asarray(h_norm_g)[0]
    sinkcol = np.zeros((64, 4), f)
    sinkcol[:, 0] = np.tile(sink, NS)
    sinkcol[0:32, 1] = np.tile(np.asarray(b_igate)[0], NS)
    sinkcol[0:32, 2] = np.tile(np.asarray(b_fgate)[0], NS)

    arrays = {
        "x_prompt": a(np.asarray(x_prompt).reshape(PASSES, NT, P, D).transpose(0, 2, 1, 3)),
        "x_sample": a(np.asarray(x_sample).reshape(NS, D)),
        "cache_k": a(np.asarray(cache_k).reshape(NS, W, P)), "cache_v": a(np.asarray(cache_v).reshape(NS, W, P)),
        "state_pool": a(np.asarray(state_pool).reshape(NS, HIST, 512)),
        "st_c": a(np.asarray(state_mlstm_c).reshape(NS * CH, CD, CD).transpose(1, 0, 2)), "st_n": a(np.asarray(state_mlstm_n).reshape(NS * CH, CD)),
        "st_m": a(np.asarray(state_mlstm_m).reshape(NS * CH, 1)),
        "rel": rel_bias, "relr": a(np.tile(rel_bias, (1, NS))), "consts": C, "rows": a(rows), "cols": cols,
        "gains": a(np.concatenate([np.asarray(norm1_g), np.asarray(norm2_g)], 0)),
        "keysT": a(np.stack([np.asarray(peer_k1)[0].T, np.asarray(peer_k2)[0].T], 1)),
        "w_pool": a(np.asarray(w_pool)[0].transpose(1, 0, 2)), "sinkcol": sinkcol,
        "w_z": wz, "w_merge": wm, "w_o": wo, "w_q": wq, "uv": a(uv), "selmat": selmat,
    }
    outs = {
        "y_p": (PASSES, P, NT, D), "y_s": (NS, D), "k_p": (P, P), "v_p": (P, P), "pool_p": (HIST, 512), "c_p": (CH, CD, CD),
        "n_p": (CH, CD), "m_p": (1, CH), "k_s": (NS, W, P), "v_s": (NS, W, P), "pool_s": (NS, HIST, 512),
        "c_s": (CD, NS * CH, CD), "n_s": (NS * CH, CD), "m_s": (NS * CH, 1),
    }
    nc = bacc.Bacc("TRN2", target_bir_lowering=False, num_devices=1)
    args = [nc.dram_tensor(n, x.shape, F32, kind="ExternalInput").ap() for n, x in arrays.items()]
    args += [nc.dram_tensor(n, x, F32, kind="ExternalOutput").ap() for n, x in outs.items()]
    build(nc, *args)
    res = run_bass_kernel_spmd(nc, [arrays], core_ids=[0]).results[0]
    o = {n: res[n] for n in outs}
    kv = (1, 1, W, AKV, AD)
    skv = (1, NS, W, AKV, AD)
    return (a(o["y_p"].transpose(0, 2, 1, 3)).reshape(1, SEQ, D), o["y_s"].reshape(NS, 1, D), o["k_p"].reshape(kv), o["v_p"].reshape(kv),
            o["pool_p"].reshape(1, 1, HIST, 512), o["c_p"].reshape(1, 1, CH, CD, CD), o["n_p"].reshape(1, 1, CH, CD),
            o["m_p"].reshape(1, 1, CH), o["k_s"].reshape(skv), o["v_s"].reshape(skv), o["pool_s"].reshape(1, NS, HIST, 512),
            a(o["c_s"].transpose(1, 0, 2)).reshape(1, NS, CH, CD, CD), o["n_s"].reshape(1, NS, CH, CD), o["m_s"].reshape(1, NS, CH))
```
